# Optimizing a Trainium2 kernel written in Bass

```python
import math
import jax, jax.numpy as jnp
from jax import lax
import numpy as np

D_MODEL = 1024
BATCH = 1
SEQ = 256
DEPTH = 1

CHUNK = 64
GM_GROUPS = 8
GM_GROUP_DIM = D_MODEL // GM_GROUPS
GM_WIDTH = GM_GROUPS * GM_GROUP_DIM
GM_BLOCK = 128
DN_HEADS = 8
DN_DK = 128
DN_DV = 128
DN_KEY = DN_HEADS * DN_DK
DN_VAL = DN_HEADS * DN_DV
DN_CONV = 4
MOE_GROUPS = 4
MOE_EXPERTS_PER_GROUP = 8
N_EXPERTS = MOE_GROUPS * MOE_EXPERTS_PER_GROUP
MOE_TOPK = 2
D_EXPERT = D_MODEL // 2
MOE_BLOCK = 128
LN_EPS = 1e-5
RMS_EPS = 1e-6
L2_EPS = 1e-6
DEEPNORM_ALPHA = (2 * DEPTH) ** 0.25
DEEPNORM_BETA = (8 * DEPTH) ** -0.25
IN_SIZES = (2 * GM_WIDTH, 2 * DN_KEY + DN_VAL, DN_VAL, DN_HEADS, DN_HEADS, D_MODEL, D_MODEL)
IN_WIDTH = 2 * GM_WIDTH + 2 * DN_KEY + 2 * DN_VAL + 2 * DN_HEADS + 2 * D_MODEL


def _layer_norm(x, g, b):
    xf = x.astype(jnp.float32)
    mu = jnp.mean(xf, -1, keepdims=True)
    var = jnp.mean(jnp.square(xf - mu), -1, keepdims=True)
    return ((xf - mu) * lax.rsqrt(var + LN_EPS) * g + b).astype(x.dtype)

def _causal_dwconv(x, w):
    c = x.shape[-1]
    return lax.conv_general_dilated(
        x, w[:, None, :].astype(x.dtype), window_strides=(1,),
        padding=[(DN_CONV - 1, 0)], dimension_numbers=('NWC', 'WIO', 'NWC'),
        feature_group_count=c)

def _spatial_gating(u, v, ln_g, ln_b, w_s, b_s):
    bsz, t, _ = u.shape
    nb = t // GM_BLOCK
    v = _layer_norm(v, ln_g, ln_b).reshape(bsz, nb, GM_BLOCK, GM_GROUPS, GM_GROUP_DIM)
    chunk_id = jnp.arange(GM_BLOCK) // CHUNK
    mask = chunk_id[None, :] <= chunk_id[:, None]
    w = jnp.where(mask[None], w_s, 0).astype(v.dtype)
    s = jnp.einsum('gts,bnsgc->bntgc', w, v) + b_s.T[None, None, :, :, None].astype(v.dtype)
    return u * s.reshape(bsz, t, GM_WIDTH)

def _gated_delta_rule(q, k, v, g, beta):
    bsz, t, nh, dk = q.shape
    dv = v.shape[-1]
    n = t // CHUNK

    def to_chunks(a):
        a = a.reshape((bsz, n, CHUNK, nh) + a.shape[3:])
        return jnp.moveaxis(a, 3, 1)

    q, k, v, g, beta = (to_chunks(a) for a in (q, k, v, g, beta))
    q = q * (dk ** -0.5)
    G = jnp.cumsum(g, axis=-1)
    idx = jnp.arange(CHUNK)
    causal = idx[:, None] >= idx[None, :]
    strict = idx[:, None] > idx[None, :]
    decay = jnp.exp(jnp.where(causal, G[..., :, None] - G[..., None, :], -jnp.inf))
    kk = jnp.einsum('bhnik,bhnjk->bhnij', k, k)
    lmat = jnp.where(strict, beta[..., :, None] * kk * decay, 0.0)
    amat = jnp.eye(CHUNK, dtype=q.dtype) + lmat
    rhs = jnp.concatenate([v * beta[..., None], k * (beta * jnp.exp(G))[..., None]], -1)
    sol = lax.linalg.triangular_solve(amat, rhs, left_side=True, lower=True, unit_diagonal=True)
    u_c, w_c = sol[..., :dv], sol[..., dv:]
    attn = jnp.einsum('bhnik,bhnjk->bhnij', q, k) * decay
    q_dec = q * jnp.exp(G)[..., None]
    g_last = G[..., -1:]
    k_dec = k * jnp.exp(g_last - G)[..., None]
    chunk_decay = jnp.exp(g_last)[..., None]

    def step(state, xs):
        uu, ww, aa, qd, kd, cd = xs
        v_new = uu - jnp.einsum('bhck,bhkv->bhcv', ww, state)
        o = jnp.einsum('bhck,bhkv->bhcv', qd, state) + jnp.einsum('bhij,bhjv->bhiv', aa, v_new)
        state = state * cd + jnp.einsum('bhck,bhcv->bhkv', kd, v_new)
        return state, o

    xs = tuple(jnp.moveaxis(a, 2, 0) for a in (u_c, w_c, attn, q_dec, k_dec, chunk_decay))
    s0 = jnp.zeros((bsz, nh, dk, dv), q.dtype)
    _, o = lax.scan(step, s0, xs)
    return o.transpose(1, 0, 3, 2, 4).reshape(bsz, t, nh, dv)

def _token_mixer(h, w_in, b_in, gm_ln_g, gm_ln_b, gm_w_s, gm_b_s,
                 dn_conv_w, dn_a_log, dn_dt_bias, dn_norm_w, w_pa, w_pb, w_o):
    bsz, t, _ = h.shape
    proj = h @ w_in + b_in
    split_at = list(np.cumsum(IN_SIZES)[:-1])
    gm_uv, dn_qkv, dn_z, dn_a, dn_b, gate_a, gate_b = jnp.split(proj, split_at, axis=-1)

    u, v = jnp.split(jax.nn.gelu(gm_uv, approximate=False), 2, axis=-1)
    y_a = _spatial_gating(u, v, gm_ln_g, gm_ln_b, gm_w_s, gm_b_s)

    qkv = jax.nn.silu(_causal_dwconv(dn_qkv, dn_conv_w)).astype(jnp.float32)
    q, k, vv = jnp.split(qkv, [DN_KEY, 2 * DN_KEY], axis=-1)
    q = q.reshape(bsz, t, DN_HEADS, DN_DK)
    k = k.reshape(bsz, t, DN_HEADS, DN_DK)
    vv = vv.reshape(bsz, t, DN_HEADS, DN_DV)
    q = q * lax.rsqrt(jnp.sum(q * q, -1, keepdims=True) + L2_EPS)
    k = k * lax.rsqrt(jnp.sum(k * k, -1, keepdims=True) + L2_EPS)
    beta = jax.nn.sigmoid(dn_b.astype(jnp.float32))
    g = -jnp.exp(dn_a_log.astype(jnp.float32)) * jax.nn.softplus(
        dn_a.astype(jnp.float32) + dn_dt_bias.astype(jnp.float32))
    o = _gated_delta_rule(q, k, vv, g, beta)
    z = dn_z.astype(jnp.float32).reshape(bsz, t, DN_HEADS, DN_DV)
    o = o * lax.rsqrt(jnp.mean(o * o, -1, keepdims=True) + RMS_EPS) * dn_norm_w * jax.nn.silu(z)
    y_b = o.reshape(bsz, t, DN_VAL).astype(h.dtype)

    merged = jax.nn.sigmoid(gate_a) * (y_a @ w_pa) + jax.nn.sigmoid(gate_b) * (y_b @ w_pb)
    return merged @ w_o

def _hier_moe(x, w_rg, b_rg, w_re, b_re, w1, w3, w2):
    bsz, t, d = x.shape
    n_tok = bsz * t
    xt = x.reshape(n_tok, d)
    pg = jax.nn.softmax((xt @ w_rg + b_rg).astype(jnp.float32), -1)
    grp = jnp.argmax(pg, -1)
    p_grp = jnp.take_along_axis(pg, grp[:, None], -1)
    le = (xt @ w_re + b_re).astype(jnp.float32).reshape(n_tok, MOE_GROUPS, MOE_EXPERTS_PER_GROUP)
    le = jnp.take_along_axis(le, grp[:, None, None], 1)[:, 0]
    top_v, top_i = lax.top_k(le, MOE_TOPK)
    gate = (p_grp * jax.nn.softmax(top_v, -1)).reshape(-1)
    eid = (grp[:, None] * MOE_EXPERTS_PER_GROUP + top_i).reshape(-1).astype(jnp.int32)
    tok = jnp.repeat(jnp.arange(n_tok, dtype=jnp.int32), MOE_TOPK)
    m = n_tok * MOE_TOPK
    order = jnp.argsort(eid)
    e_s, tok_s, gate_s = eid[order], tok[order], gate[order]
    counts = jnp.zeros((N_EXPERTS,), jnp.int32).at[eid].add(1)
    start = jnp.cumsum(counts) - counts
    padded = (counts + MOE_BLOCK - 1) // MOE_BLOCK * MOE_BLOCK
    pad_end = jnp.cumsum(padded)
    pad_start = pad_end - padded
    dest = pad_start[e_s] + (jnp.arange(m, dtype=jnp.int32) - start[e_s])
    n_blocks = (m + N_EXPERTS * (MOE_BLOCK - 1) + MOE_BLOCK - 1) // MOE_BLOCK
    rows = n_blocks * MOE_BLOCK
    x_pad = jnp.zeros((rows, d), x.dtype).at[dest].set(xt[tok_s])
    blk_start = jnp.arange(n_blocks, dtype=jnp.int32) * MOE_BLOCK
    blk_e = jnp.minimum(jnp.sum(pad_end[None, :] <= blk_start[:, None], -1), N_EXPERTS - 1)

    def expert_block(args):
        xb, e = args
        hb = jax.nn.silu(xb @ w1[e]) * (xb @ w3[e])
        return hb @ w2[e]

    y_pad = lax.map(expert_block, (x_pad.reshape(n_blocks, MOE_BLOCK, d), blk_e)).reshape(rows, d)
    y = y_pad[dest] * gate_s[:, None].astype(x.dtype)
    out = jnp.zeros((n_tok, d), x.dtype).at[tok_s].add(y)
    return out.reshape(bsz, t, d)

def first_inputs(seed: int = 0) -> dict:
    key = jax.random.key(seed)
    ks = list(jax.random.split(key, 48))
    kit = iter(ks)

    def nrm(shape, scale):
        return scale * jax.random.normal(next(kit), shape, jnp.float32)

    def gain(shape):
        return 1.0 + nrm(shape, 0.05)

    L, D = DEPTH, D_MODEL
    s_in = D ** -0.5
    w_in = jnp.concatenate([
        nrm((L, D, 2 * GM_WIDTH), s_in * DEEPNORM_BETA),
        nrm((L, D, 2 * DN_KEY), s_in),
        nrm((L, D, DN_VAL), s_in * DEEPNORM_BETA),
        nrm((L, D, DN_VAL), s_in),
        nrm((L, D, 2 * DN_HEADS), s_in),
        nrm((L, D, 2 * D_MODEL), s_in),
    ], axis=-1)
    a_init = jax.random.uniform(next(kit), (L, DN_HEADS), jnp.float32, 1.0, 16.0)
    log_dt = jax.random.uniform(next(kit), (L, DN_HEADS), jnp.float32, math.log(1e-3), math.log(1e-1))
    dt = jnp.exp(log_dt)
    dt_bias = dt + jnp.log(-jnp.expm1(-dt))
    return {
        "x": jax.random.normal(next(kit), (BATCH, SEQ, D), jnp.float32),
        "ln_in_g": gain((D,)),
        "ln_in_b": nrm((D,), 0.02),
        "w_in": w_in,
        "b_in": nrm((L, IN_WIDTH), 0.01),
        "gm_ln_g": gain((L, GM_WIDTH)),
        "gm_ln_b": nrm((L, GM_WIDTH), 0.02),
        "gm_w_s": nrm((L, GM_GROUPS, GM_BLOCK, GM_BLOCK), 0.5 * GM_BLOCK ** -0.5),
        "gm_b_s": 1.0 + nrm((L, GM_GROUPS, GM_BLOCK), 0.1),
        "dn_conv_w": nrm((L, DN_CONV, 2 * DN_KEY + DN_VAL), DN_CONV ** -0.5),
        "dn_a_log": jnp.log(a_init),
        "dn_dt_bias": dt_bias,
        "dn_norm_w": gain((L, DN_DV)),
        "w_pa": nrm((L, GM_WIDTH, D), GM_WIDTH ** -0.5 * DEEPNORM_BETA),
        "w_pb": nrm((L, DN_VAL, D), DN_VAL ** -0.5 * DEEPNORM_BETA),
        "w_o": nrm((L, D, D), D ** -0.5 * DEEPNORM_BETA),
        "ln1_g": gain((L, D)),
        "ln1_b": nrm((L, D), 0.02),
        "w_rg": nrm((L, D, MOE_GROUPS), s_in),
        "b_rg": nrm((L, MOE_GROUPS), 0.01),
        "w_re": nrm((L, D, N_EXPERTS), s_in),
        "b_re": nrm((L, N_EXPERTS), 0.01),
        "w1": nrm((L, N_EXPERTS, D, D_EXPERT), s_in * DEEPNORM_BETA),
        "w3": nrm((L, N_EXPERTS, D, D_EXPERT), s_in * DEEPNORM_BETA),
        "w2": nrm((L, N_EXPERTS, D_EXPERT, D), D_EXPERT ** -0.5 * DEEPNORM_BETA),
        "ln2_g": gain((L, D)),
        "ln2_b": nrm((L, D), 0.02),
    }

def first_block(x, ln_in_g, ln_in_b, w_in, b_in, gm_ln_g, gm_ln_b, gm_w_s, gm_b_s,
              dn_conv_w, dn_a_log, dn_dt_bias, dn_norm_w, w_pa, w_pb, w_o,
              ln1_g, ln1_b, w_rg, b_rg, w_re, b_re, w1, w3, w2, ln2_g, ln2_b):
    h = _layer_norm(x, ln_in_g, ln_in_b)
    for l in range(DEPTH):
        mix = _token_mixer(h, w_in[l], b_in[l], gm_ln_g[l], gm_ln_b[l], gm_w_s[l], gm_b_s[l],
                           dn_conv_w[l], dn_a_log[l], dn_dt_bias[l], dn_norm_w[l],
                           w_pa[l], w_pb[l], w_o[l])
        h = _layer_norm(DEEPNORM_ALPHA * h + mix, ln1_g[l], ln1_b[l])
        ffn = _hier_moe(h, w_rg[l], b_rg[l], w_re[l], b_re[l], w1[l], w3[l], w2[l])
        h = _layer_norm(DEEPNORM_ALPHA * h + ffn, ln2_g[l], ln2_b[l])
    return h


DEPTH_2 = 2

EPS = 1e-6
BLOCK = 128

MLA_HEADS = 8
MLA_Q_LORA = 256
MLA_KV_LORA = 128
MLA_NOPE = 64
MLA_ROPE = 32
MLA_V = 64
ROPE_BASE = 10000.0

DIL_HEADS = 8
DIL_HEAD_DIM = 64
DIL_PATTERNS = ((128, 1), (512, 4), (2048, 16))

SWA_Q_HEADS = 16
SWA_KV_HEADS = 2
SWA_HEAD_DIM = 64
SWA_WINDOW = 128

D_FF = -(-8 * D_MODEL // (3 * 256)) * 256

N_EVEN = (DEPTH_2 + 1) // 2
N_ODD = DEPTH_2 // 2

MIX_IN_A = MLA_Q_LORA + MLA_KV_LORA + MLA_ROPE
MIX_IN_B = 3 * DIL_HEADS * DIL_HEAD_DIM
MIX_IN = MIX_IN_A + MIX_IN_B
MIX_OUT = MLA_HEADS * MLA_V + DIL_HEADS * DIL_HEAD_DIM
MLA_QK = MLA_NOPE + MLA_ROPE
SWA_QKV = (SWA_Q_HEADS + 2 * SWA_KV_HEADS) * SWA_HEAD_DIM
SWA_OUT = SWA_Q_HEADS * SWA_HEAD_DIM


def _rmsnorm(x, g):
    xf = x.astype(jnp.float32)
    y = xf * lax.rsqrt(jnp.mean(xf * xf, axis=-1, keepdims=True) + EPS)
    return (y * g.astype(jnp.float32)).astype(x.dtype)

def _alibi_slopes(n):
    return jnp.exp2(-8.0 * jnp.arange(1, n + 1, dtype=jnp.float32) / n)

def _rope_tables(seq, dim):
    pos = jnp.arange(seq, dtype=jnp.float32)
    inv_freq = ROPE_BASE ** (-jnp.arange(0, dim, 2, dtype=jnp.float32) / dim)
    ang = pos[:, None] * inv_freq[None, :]
    return jnp.cos(ang), jnp.sin(ang)

def _rope(x, cos, sin):
    half = x.shape[-1] // 2
    x1, x2 = x[..., :half], x[..., half:]
    c = cos.astype(x.dtype)
    s = sin.astype(x.dtype)
    return jnp.concatenate([x1 * c - x2 * s, x2 * c + x1 * s], axis=-1)

def _to_blocks(t):
    b, s, h, d = t.shape
    return t.reshape(b, s // BLOCK, BLOCK, h, d).transpose(1, 0, 2, 3, 4)

def _from_blocks(t):
    nb, b, blk, h, d = t.shape
    return t.transpose(1, 0, 2, 3, 4).reshape(b, nb * blk, h * d)

def _mla_causal_attention(q, k, v):
    S = q.shape[1]
    nb = S // BLOCK
    scale = 1.0 / math.sqrt(q.shape[-1])
    kpos = jnp.arange(S)

    def one(args):
        qi, bi = args
        s = jnp.einsum('bqhd,bshd->bhqs', qi, k).astype(jnp.float32) * scale
        qpos = bi * BLOCK + jnp.arange(BLOCK)
        s = jnp.where((kpos[None, :] <= qpos[:, None])[None, None], s, -jnp.inf)
        p = jax.nn.softmax(s, axis=-1)
        return jnp.einsum('bhqs,bshd->bqhd', p.astype(v.dtype), v)

    out = lax.map(one, (_to_blocks(q), jnp.arange(nb)))
    return _from_blocks(out)

def _dilated_attention(q, k, v, slopes):
    S = q.shape[1]
    nb = S // BLOCK
    scale = 1.0 / math.sqrt(q.shape[-1])

    def one(args):
        qi, bi = args
        qpos = bi * BLOCK + jnp.arange(BLOCK)
        outs, lses = [], []
        for window, dil in DIL_PATTERNS:
            offs = dil * jnp.arange(window // dil + 1)
            kpos = qpos[:, None] - offs[None, :]
            valid = kpos >= 0
            idx = jnp.maximum(kpos, 0)
            kg = jnp.take(k, idx, axis=1)
            vg = jnp.take(v, idx, axis=1)
            s = jnp.einsum('bqhd,bqjhd->bhqj', qi, kg).astype(jnp.float32) * scale
            s = s - slopes[:, None, None] * offs.astype(jnp.float32)[None, None, :]
            s = jnp.where(valid[None, None], s, -jnp.inf)
            lse = jax.nn.logsumexp(s, axis=-1)
            p = jnp.exp(s - lse[..., None])
            outs.append(jnp.einsum('bhqj,bqjhd->bqhd', p.astype(v.dtype), vg))
            lses.append(lse)
        w = jax.nn.softmax(jnp.stack(lses, axis=0), axis=0)
        w = w.transpose(0, 1, 3, 2)[..., None].astype(v.dtype)
        return jnp.sum(w * jnp.stack(outs, axis=0), axis=0)

    out = lax.map(one, (_to_blocks(q), jnp.arange(nb)))
    return _from_blocks(out)

def _swa_sink_attention(q, k, v, sinks, slopes):
    B_, S, Hq, dh = q.shape
    Hkv = k.shape[2]
    G = Hq // Hkv
    nb = S // BLOCK
    scale = 1.0 / math.sqrt(dh)
    qb = q.reshape(B_, nb, BLOCK, Hkv, G, dh)

    def band(t):
        cur = t.reshape(B_, nb, BLOCK, Hkv, dh)
        prev = jnp.pad(t, ((0, 0), (BLOCK, 0), (0, 0), (0, 0)))[:, :S].reshape(B_, nb, BLOCK, Hkv, dh)
        return jnp.concatenate([prev, cur], axis=2)

    kb, vb = band(k), band(v)
    qi = jnp.arange(BLOCK)
    kj = jnp.arange(2 * BLOCK)
    dist = qi[:, None] + BLOCK - kj[None, :]
    kpos = jnp.arange(nb)[:, None] * BLOCK - BLOCK + kj[None, :]
    valid = ((dist >= 0) & (dist < SWA_WINDOW))[None] & (kpos >= 0)[:, None, :]
    s = jnp.einsum('bnqkgd,bnjkd->bnkgqj', qb, kb).astype(jnp.float32) * scale
    s = s - slopes.reshape(Hkv, G)[:, :, None, None] * dist.astype(jnp.float32)
    s = jnp.where(valid[None, :, None, None], s, -jnp.inf)
    sink = jnp.broadcast_to(sinks.astype(jnp.float32).reshape(1, 1, Hkv, G, 1, 1), s.shape[:-1] + (1,))
    p = jax.nn.softmax(jnp.concatenate([s, sink], axis=-1), axis=-1)[..., :-1]
    o = jnp.einsum('bnkgqj,bnjkd->bnqkgd', p.astype(v.dtype), vb)
    return o.reshape(B_, S, Hq * dh)

def _even_mixer(h, w_in, g_q, g_kv, w_uq, w_ukv, w_out, cos, sin, dil_slopes):
    B_, S, _ = h.shape
    proj = h @ w_in
    o1 = MLA_Q_LORA
    o2 = o1 + MLA_KV_LORA
    o3 = o2 + MLA_ROPE
    nd = DIL_HEADS * DIL_HEAD_DIM
    c_q, c_kv, k_r = proj[..., :o1], proj[..., o1:o2], proj[..., o2:o3]
    qB = proj[..., o3:o3 + nd].reshape(B_, S, DIL_HEADS, DIL_HEAD_DIM)
    kB = proj[..., o3 + nd:o3 + 2 * nd].reshape(B_, S, DIL_HEADS, DIL_HEAD_DIM)
    vB = proj[..., o3 + 2 * nd:o3 + 3 * nd].reshape(B_, S, DIL_HEADS, DIL_HEAD_DIM)
    qA = (_rmsnorm(c_q, g_q) @ w_uq).reshape(B_, S, MLA_HEADS, MLA_QK)
    q_nope, q_rope = qA[..., :MLA_NOPE], qA[..., MLA_NOPE:]
    q_rope = _rope(q_rope, cos[None, :, None, :], sin[None, :, None, :])
    kv = (_rmsnorm(c_kv, g_kv) @ w_ukv).reshape(B_, S, MLA_HEADS, MLA_NOPE + MLA_V)
    k_nope, vA = kv[..., :MLA_NOPE], kv[..., MLA_NOPE:]
    k_rope = _rope(k_r, cos[None], sin[None])
    k_rope = jnp.broadcast_to(k_rope[:, :, None, :], (B_, S, MLA_HEADS, MLA_ROPE))
    oA = _mla_causal_attention(jnp.concatenate([q_nope, q_rope], axis=-1),
                               jnp.concatenate([k_nope, k_rope], axis=-1), vA)
    oB = _dilated_attention(qB, kB, vB, dil_slopes)
    return jnp.concatenate([oA, oB], axis=-1) @ w_out

def _odd_mixer(h, w_qkv, sinks, w_out, swa_slopes):
    B_, S, _ = h.shape
    qkv = h @ w_qkv
    nq = SWA_Q_HEADS * SWA_HEAD_DIM
    nk = SWA_KV_HEADS * SWA_HEAD_DIM
    q = qkv[..., :nq].reshape(B_, S, SWA_Q_HEADS, SWA_HEAD_DIM)
    k = qkv[..., nq:nq + nk].reshape(B_, S, SWA_KV_HEADS, SWA_HEAD_DIM)
    v = qkv[..., nq + nk:].reshape(B_, S, SWA_KV_HEADS, SWA_HEAD_DIM)
    return _swa_sink_attention(q, k, v, sinks, swa_slopes) @ w_out

def _swiglu(h, w_gate_up, w_down):
    gu = h @ w_gate_up
    gate, up = gu[..., :D_FF], gu[..., D_FF:]
    return (jax.nn.silu(gate) * up) @ w_down

def second_inputs(seed: int = 0) -> dict:
    key = jax.random.key(seed)
    ks = jax.random.split(key, 16)
    f32 = jnp.float32

    def w(k, shape, fan_in):
        return jax.random.normal(k, shape, f32) * (fan_in ** -0.5)

    def gain(k, shape):
        return 1.0 + 0.05 * jax.random.normal(k, shape, f32)

    return {
        "x": jax.random.normal(ks[0], (BATCH, SEQ, D_MODEL), f32),
        "attn_norm": gain(ks[1], (DEPTH_2, D_MODEL)),
        "ffn_norm": gain(ks[2], (DEPTH_2, D_MODEL)),
        "final_norm": gain(ks[3], (D_MODEL,)),
        "e_w_in": w(ks[4], (N_EVEN, D_MODEL, MIX_IN), D_MODEL),
        "e_q_norm": gain(ks[5], (N_EVEN, MLA_Q_LORA)),
        "e_kv_norm": gain(ks[6], (N_EVEN, MLA_KV_LORA)),
        "e_w_uq": w(ks[7], (N_EVEN, MLA_Q_LORA, MLA_HEADS * MLA_QK), MLA_Q_LORA),
        "e_w_ukv": w(ks[8], (N_EVEN, MLA_KV_LORA, MLA_HEADS * (MLA_NOPE + MLA_V)), MLA_KV_LORA),
        "e_w_out": w(ks[9], (N_EVEN, MIX_OUT, D_MODEL), MIX_OUT),
        "o_w_qkv": w(ks[10], (N_ODD, D_MODEL, SWA_QKV), D_MODEL),
        "o_sinks": jax.random.normal(ks[11], (N_ODD, SWA_Q_HEADS), f32),
        "o_w_out": w(ks[12], (N_ODD, SWA_OUT, D_MODEL), SWA_OUT),
        "f_w_gate_up": w(ks[13], (DEPTH_2, D_MODEL, 2 * D_FF), D_MODEL),
        "f_w_down": w(ks[14], (DEPTH_2, D_FF, D_MODEL), D_FF),
    }

def second_block(x, attn_norm, ffn_norm, final_norm, e_w_in, e_q_norm, e_kv_norm, e_w_uq,
              e_w_ukv, e_w_out, o_w_qkv, o_sinks, o_w_out, f_w_gate_up, f_w_down):
    S = x.shape[1]
    cos, sin = _rope_tables(S, MLA_ROPE)
    dil_slopes = _alibi_slopes(DIL_HEADS)
    swa_slopes = _alibi_slopes(SWA_Q_HEADS)
    h = x
    for layer in range(DEPTH_2):
        i = layer // 2
        hn = _rmsnorm(h, attn_norm[layer])
        if layer % 2 == 0:
            mix = _even_mixer(hn, e_w_in[i], e_q_norm[i], e_kv_norm[i], e_w_uq[i],
                              e_w_ukv[i], e_w_out[i], cos, sin, dil_slopes)
        else:
            mix = _odd_mixer(hn, o_w_qkv[i], o_sinks[i], o_w_out[i], swa_slopes)
        h = h + mix
        h = h + _swiglu(_rmsnorm(h, ffn_norm[layer]), f_w_gate_up[layer], f_w_down[layer])
    return _rmsnorm(h, final_norm)


def setup_inputs(seed=0):
    out = dict(first_inputs(seed))
    for name, value in second_inputs(seed + 1).items():
        if name != "x":
            out[name + "_2"] = value
    return out


def reference(
    x, ln_in_g, ln_in_b, w_in, b_in, gm_ln_g, gm_ln_b, gm_w_s, gm_b_s, dn_conv_w, dn_a_log,
    dn_dt_bias, dn_norm_w, w_pa, w_pb, w_o, ln1_g, ln1_b, w_rg, b_rg, w_re, b_re, w1, w3, w2,
    ln2_g, ln2_b, attn_norm_2, ffn_norm_2, final_norm_2, e_w_in_2, e_q_norm_2, e_kv_norm_2,
    e_w_uq_2, e_w_ukv_2, e_w_out_2, o_w_qkv_2, o_sinks_2, o_w_out_2, f_w_gate_up_2, f_w_down_2,
):
    x = first_block(
        x, ln_in_g, ln_in_b, w_in, b_in, gm_ln_g, gm_ln_b, gm_w_s, gm_b_s, dn_conv_w, dn_a_log,
        dn_dt_bias, dn_norm_w, w_pa, w_pb, w_o, ln1_g, ln1_b, w_rg, b_rg, w_re, b_re, w1, w3,
        w2, ln2_g, ln2_b,
    )
    return second_block(
        x, attn_norm_2, ffn_norm_2, final_norm_2, e_w_in_2, e_q_norm_2, e_kv_norm_2, e_w_uq_2,
        e_w_ukv_2, e_w_out_2, o_w_qkv_2, o_sinks_2, o_w_out_2, f_w_gate_up_2, f_w_down_2,
    )


_drawn_inputs = setup_inputs


def setup_inputs(seed=0):
    import zlib

    import numpy as np

    out = dict(_drawn_inputs(seed))
    spreads = {}
    factors = {'b_in': 8.0,
     'gm_ln_g': 8.0,
     'gm_ln_b': 8.0,
     'gm_b_s': 6.979,
     'dn_norm_w': 8.0,
     'b_rg': 8.0,
     'b_re': 8.0,
     'e_q_norm_2': 7.219,
     'e_kv_norm_2': 4.369,
     'ffn_norm_2': 2.984,
     'o_sinks_2': 3.844}
    for name, (base, spread) in spreads.items():
        noise = np.random.default_rng([zlib.crc32(name.encode()), seed]).standard_normal(out[name].shape)
        drawn = base * np.exp(spread * noise) if base else spread * noise
        out[name] = __import__('jax').numpy.asarray(drawn.astype(out[name].dtype))
    for name, factor in factors.items():
        out[name] = (out[name] * factor).astype(out[name].dtype)
    return out
```

```python
from contextlib import ExitStack

import numpy as np

import concourse.bass as bass
from concourse import mybir

F32 = mybir.dt.float32
F16 = mybir.dt.float16
I32 = mybir.dt.int32
U32 = mybir.dt.uint32
ALU = mybir.AluOpType
ACT = mybir.ActivationFunctionType
AX = mybir.AxisListType

P = 128
T = 256
NB = T // P
D = 1024
KD = D // P
HEADS = 8
CHUNK = 64
UNITS = HEADS * NB
EXPERTS = 32
GROUPS = 4
FE = 512
CAP = 64
MAX_PASSES = T // CAP
ASSIGN = 2 * T
SORTED = ASSIGN + MAX_PASSES * CAP
D_FF = 2816
FF_BLOCKS = D_FF // P
MLA_Q, MLA_KV, NOPE, ROPE, VDIM = 256, 128, 64, 32, 64
SWA_HEADS = 16
ALPHA = 2.0 ** 0.25
NEG = -1e30
NORMS = {"ln_in": KD, "gm": KD, "ln1": KD, "ln2": KD, "att0": KD, "cqn": 2, "ckvn": 1, "ffn0n": KD,
         "att1": KD, "ffn1n": KD, "final": KD}
LAYER_NORMS = ("ln_in", "gm", "ln1", "ln2")
SECTIONS = {"mla": HEADS, "dil": HEADS, "swa": SWA_HEADS}

SLOTS = 6
SLOT = 4096
PAGES = 13
PAGE = KD * T
BANK = 512

COLS = {}
_at = 0
for _name, _n in (("ln_in_g", 8), ("ln_in_b", 8), ("gm_g", 8), ("gm_b", 8), ("ln1_g", 8), ("ln1_b", 8),
                  ("ln2_g", 8), ("ln2_b", 8), ("att0", 8), ("att1", 8), ("ffn0", 8), ("ffn1", 8),
                  ("final", 8), ("b_in", 64), ("conv", 96), ("dn_norm", 1), ("q_norm", 2),
                  ("kv_norm", 1), ("eps5", 1), ("eps6", 1), ("qscale", 1)):
    COLS[_name] = _at
    _at += _n
NCOLS = _at
ROWS = {"a_log": 0, "dt_bias": 8, "b_a": 16, "b_b": 24, "b_router": 32, "sinks": 68}
NROWS = 84
TABLES = ("identity", "ones", "cumulate", "before")
MASKS = ("strict_low", "incl_up", "first", "first_t", "level2", "level4", "level8", "level16", "level32")
N_ROUTER = KD * 36 + ASSIGN + 64
SPAN = P + T


def shape_tables():
    i = np.arange(P)[:, None]
    j = np.arange(P)[None, :]
    same = i // CHUNK == j // CHUNK
    f32 = [np.eye(P), np.ones((P, P)), same & (i <= j), i < j]
    masks = [same & (i > j), same & (i <= j)]
    level = lambda s: (i // (2 * s) == j // (2 * s)) & (i // s % 2 == 1) & (j // s % 2 == 0)
    masks += [level(1), level(1).T] + [level(s) for s in (2, 4, 8, 16, 32)]
    experts = np.arange(EXPERTS)
    iota = np.concatenate([np.arange(ASSIGN), experts, experts // (EXPERTS // GROUPS)])
    dist = np.concatenate([i - j, i - j + P, i - j], axis=1)
    mult = sum(((dist >= 0) & (dist <= w) & (dist % r == 0)).astype(int) for w, r in ((128, 1), (512, 4), (2048, 16)))
    dil = np.where(mult > 0, -dist, NEG)
    swa = np.where((dist >= 0) & (dist < 128), -dist, NEG)
    causal = np.where(dist >= 0, 0, NEG)
    ang = np.arange(T)[None, :] * (10000.0 ** (-np.arange(0, ROPE, 2) / ROPE))[:, None]
    cos = np.zeros((P, T))
    sin = np.zeros((P, T))
    cos[NOPE:NOPE + ROPE] = np.concatenate([np.cos(ang), np.cos(ang)])
    sin[NOPE:NOPE + ROPE] = np.concatenate([-np.sin(ang), np.sin(ang)])
    return {
        "c_tables": np.concatenate(f32, axis=1).astype(np.float32),
        "c_masks": np.concatenate(masks, axis=1).astype(np.float16),
        "c_iota": np.tile(iota[None, :], (P, 1)).astype(np.float32),
        "c_attn": np.concatenate([dil, mult, swa, causal, cos, sin], axis=1).astype(np.float32),
    }


def stream_items():
    items = []
    for part in ("gm_v", "gm_u", "gate_a"):
        items += [(part, 0), (part, 1)]
    items += [("w_pa", 0), ("w_pa", 1)]
    for part in ("dn_q", "dn_k", "dn_v", "dn_z", "gate_b"):
        items += [(part, 0), (part, 1)]
    items += [("w_pb", 0), ("w_pb", 1), ("w_o", 0), ("w_o", 1)]
    before = len(items)
    for e in range(EXPERTS):
        items += [("w1", e), ("w3", e), ("w2", e)]
    items += [("e_in", n) for n in range(4)] + [("mla_up", 0), ("e_out", 0), ("e_out", 1)]
    items += [("ffn0", j) for j in range(FF_BLOCKS)]
    items += [("o_in", 0), ("o_in", 1), ("o_kv", 0), ("o_out", 0), ("o_out", 1)]
    items += [("ffn1", j) for j in range(FF_BLOCKS)]
    return items, before


def build(nc, io, out, phases=3):
    items, moe_first = stream_items()
    item_no = {it: n for n, it in enumerate(items)}
    with ExitStack() as ctx:
        sb = lambda name, shape, dt=F32: ctx.enter_context(nc.sbuf_tensor(name, shape, dt))
        sems = {}

        def shared(name):
            owner, _, kind = name.partition("_") if not name.startswith("ln_in") else ("ln_in", "", name[6:])
            if owner in NORMS:
                size = {"squared": lambda n: 2 if n == KD else 1, "centered": lambda n: 2, "rstd": lambda n: 1,
                        "scaled": lambda n: n, "out": lambda n: n}.get(kind)
                if size is None:
                    return name, 0
                named = [n for n in NORMS if kind not in ("centered", "out") or n in LAYER_NORMS]
                return f"norm_{kind}", sum(size(NORMS[n]) for n in named[:named.index(owner)])
            if owner in SECTIONS and kind in ("even_o", "probs", "pT", "max", "exp", "o_ready"):
                before = sum(list(SECTIONS.values())[:list(SECTIONS).index(owner)])
                return f"heads_{kind}", {"even_o": before // 2, "o_ready": before // 2, "max": 2 * before}.get(kind, before)
            return name, 0

        def S(name):
            name = shared(name)[0]
            if name not in sems:
                sems[name] = ctx.enter_context(nc.semaphore(name))
            return sems[name]

        def V(name, n):
            return S(name), shared(name)[1] + n

        ring = sb("ring", [P, SLOTS * SLOT])
        pages = sb("pages", [P, PAGES * PAGE])
        tables = sb("tables", [P, len(TABLES) * P])
        masks = sb("masks", [P, len(MASKS) * P], F16)
        cols = sb("cols", [P, NCOLS])
        rows = sb("rows", [P, NROWS])
        ab = sb("ab", [P, 16 * 12])
        starts = sb("starts", [1, EXPERTS + 2], I32)
        psum = ctx.enter_context(nc.psum_tensor("psum", [P, 8, BANK], F32))

        def table(name):
            n = TABLES.index(name)
            return tables[:, n * P:(n + 1) * P]

        def mask(name):
            n = MASKS.index(name)
            return masks[:, n * P:(n + 1) * P]

        def page(n, count=1):
            return pages[:, n * PAGE:(n + count) * PAGE]

        def fm(n):
            return page(n).rearrange("p (k t) -> p k t", t=T)

        def units(n):
            return page(n).rearrange("p (u t) -> p u t", t=P)

        def col(name, k=0):
            c = COLS[name] + k
            return cols[:, c:c + 1]

        def row(name, n):
            return rows[:, ROWS[name]:ROWS[name] + n]

        def slot(n, floats=SLOT):
            s = n % SLOTS
            return ring[:, s * SLOT:s * SLOT + floats]

        ident, ones = table("identity"), table("ones")
        full = [S(f"bank{b}_full") for b in range(8)]
        free = [S(f"bank{b}_free") for b in range(8)]
        landed = [S(f"slot{s}_landed") for s in range(SLOTS)]
        uses = [0] * 8
        place = {}
        released = {}

        def bank_of(name, use=0):
            return psum[:, place[name][0], :]

        def await_full(eng, name):
            b, n = place[name]
            eng.wait_ge(full[b], n)
            return psum[:, b, :]

        def empty(ins, name):
            ins.then_inc(free[place[name][0]], 1)

        class Steps:

            def __init__(self, eng, name):
                self.eng, self.sem, self.n, self.last = eng, S(name), 0, None
                self.counts = {}

            def do(self, ins, name=None):
                if name is None:
                    self.n += 1
                    ins.then_inc(self.sem, 1)
                    self.last = (self.sem, self.n)
                elif name in place:
                    empty(ins, name)
                    self.last = (free[place[name][0]], place[name][1])
                else:
                    own = shared(name)[0]
                    self.counts[own] = self.counts.get(own, 0) + 1
                    ins.then_inc(S(name), 1)
                    self.last = (S(name), self.counts[own])

            def settle(self):
                self.eng.wait_ge(*self.last)

        PROJ_BANKS = (0, 1, 2, 3)

        block = ctx.enter_context(nc.Block())

        @block.tensor
        def _(pe):
            turn = [0]

            def take(name, bank=None):
                if bank is None:
                    bank = PROJ_BANKS[turn[0] % len(PROJ_BANKS)]
                    turn[0] += 1
                if uses[bank]:
                    pe.wait_ge(free[bank], uses[bank])
                uses[bank] += 1
                place[name] = (bank, uses[bank])
                return psum[:, bank, :]

            def give(ins, name):
                ins.then_inc(full[place[name][0]], 1)

            def weights(item):
                n = item_no[item]
                pe.wait_ge(landed[n % SLOTS], 16 * (n // SLOTS + 1))
                return slot(n)

            def release(item, name):
                released[item_no[item]] = (full[place[name][0]], place[name][1])

            def mm(o, lhsT, rhs, start, stop):
                return pe.matmul(o, lhsT, rhs, start=start, stop=stop, skip_group_check=True)

            def project(part, rhs, item_names, first_block=0):
                for n, item in enumerate(item_names):
                    w = weights(item).rearrange("p (k c) -> p k c", k=KD)
                    for pair in range(2):
                        name = f"{part}{2 * n + pair}"
                        o = take(name)
                        for half in range(2):
                            c = (2 * pair + half) * P
                            for k in range(KD):
                                last = mm(o[:, half * T:(half + 1) * T], w[:, k, c:c + P], rhs[:, k, :],
                                          k == 0, k == KD - 1)
                        give(last, name)
                    release(item, name)

            def column_sums(name, src, nblocks, scope=None):
                o = take(name, scope)
                for k in range(nblocks):
                    last = mm(o[:, 0:T], ones, src[:, k, :], k == 0, k == nblocks - 1)
                give(last, name)

            def norm(nm, src, squares, nblocks, mean):
                if mean:
                    column_sums(f"{nm}_mu", src, nblocks)
                pe.wait_ge(*V(f"{nm}_squared", 2 if nblocks == KD else 1))
                column_sums(f"{nm}_var", squares, nblocks)

            def transposes(name, srcs, bank=None):
                o = take(name, bank)
                for j, s in enumerate(srcs):
                    last = pe.transpose(o[:, j * P:(j + 1) * P], s, ident)
                give(last, name)

            pe.wait_ge(*V("constants", 16 * 6))
            pe.wait_ge(*V("x_landed", 16))
            norm("ln_in", fm(1), fm(2), KD, True)
            h = fm(0)
            pe.wait_ge(*V("ln_in_out", KD))
            project("gm_v", h, [("gm_v", 0), ("gm_v", 1)])
            project("gm_u", h, [("gm_u", 0), ("gm_u", 1)])
            pe.wait_ge(*V("gm_v_ready", 4))
            column_sums("gm_mu", fm(2), KD)
            project("gate_a", h, [("gate_a", 0)])
            pe.wait_ge(*V("gm_squared", 2))
            column_sums("gm_var", fm(4), KD)
            w = ("gate_a", 1)
            project("gate_a_", h, [w])
            for b in range(NB):
                for half in range(2):
                    pe.wait_ge(*V("gm_out", 4 * half + 4))
                    transposes(f"gm_t{b}{half}", [fm(2)[:, 4 * half + j, b * P:(b + 1) * P] for j in range(4)])
            pe.wait_ge(*V("gate_masked", 1))
            pe.wait_ge(*V("bs_landed", 16))
            vtm = page(4).rearrange("p (b c) -> p b c", b=NB)
            wgt = page(3)[:, 0:KD * P].rearrange("p (g t) -> p g t", t=P)
            pe.wait_ge(*V("gm_vtm", 4))
            for g2 in range(KD // 2):
                o = take(f"spatial{g2}")
                for half in range(2):
                    g = 2 * g2 + half
                    for b in range(NB):
                        dst = o[:, half * T + b * P:half * T + (b + 1) * P]
                        mm(dst, vtm[:, b, g * P:(g + 1) * P], wgt[:, g, :], True, False)
                        last = mm(dst, ones[0:1, :], page(3)[0:1, KD * P + g * P:KD * P + (g + 1) * P], False, True)
                give(last, f"spatial{g2}")
            pe.wait_ge(*V("ya_ready", 4))
            project("w_pa", fm(5), [("w_pa", 0), ("w_pa", 1)])
            project("dn_q", h, [("dn_q", 0), ("dn_q", 1)])
            project("dn_k", h, [("dn_k", 0), ("dn_k", 1)])
            o = take("ab")
            wab = ab[:, 0:P].rearrange("p (k c) -> p k c", k=KD)
            for b in range(NB):
                for k in range(KD):
                    last = mm(o[:, b * 16:(b + 1) * 16], h[:, k, b * P:(b + 1) * P], wab[:, k, :], k == 0, k == KD - 1)
            give(last, "ab")
            project("dn_v", h, [("dn_v", 0), ("dn_v", 1)])
            pe.wait_ge(*V("g_ready", 1))
            g_tm = ab[:, 0:16]
            o = take("G")
            give(mm(o[:, 0:16], table("cumulate"), g_tm, True, True), "G")
            for q4 in range(4):
                o = take(f"Gb{q4}", 4 + q4)
                for j in range(4):
                    u = 4 * q4 + j
                    hd, b = u // NB, u % NB
                    c = b * HEADS + hd
                    last = mm(o[:, j * P:(j + 1) * P], g_tm[:, c:c + 1].broadcast_to([P, P]), table("cumulate"), True, True)
                give(last, f"Gb{q4}")
            for part, pg in (("q", 7), ("k", 8)):
                for q4 in range(4):
                    pe.wait_ge(*V(f"{part}_squared", q4 + 1))
                    name = f"{part}_ss{q4}"
                    o = take(name)
                    for half in range(2):
                        last = mm(o[:, half * T:(half + 1) * T], ones, fm(pg)[:, 2 * q4 + half, :], True, True)
                    give(last, name)
            project("dn_z", h, [("dn_z", 0)])
            for q4 in range(4):
                pe.wait_ge(*V("k_normed", q4 + 1))
                transposes(f"k_t{q4}", [units(3)[:, 4 * q4 + j, :] for j in range(4)])
                pe.wait_ge(*V("v_ready", 2 * q4 + 2))
                transposes(f"v_t{q4}", [units(4)[:, 4 * q4 + j, :] for j in range(4)])
            for q4 in range(4):
                name = f"kk{q4}"
                o = take(name, 4 + q4)
                for j in range(4):
                    k = units(3)[:, 4 * q4 + j, :]
                    last = mm(o[:, j * P:(j + 1) * P], k, k, True, True)
                give(last, name)
            for q4 in range(4):
                name = f"qk{q4}"
                pe.wait_ge(*V("q_normed", q4 + 1))
                o = take(name)
                for j in range(4):
                    u = 4 * q4 + j
                    last = mm(o[:, j * P:(j + 1) * P], units(3)[:, u, :], units(2)[:, u, :], True, True)
                give(last, name)
            for q4 in range(4):
                pe.wait_ge(*V("L_ready", q4 + 1))
                transposes(f"L_t{q4}", [units(11)[:, 4 * q4 + j, :] for j in range(4)], 4 + q4)
            X, XT, Y, LT = units(5), units(4), units(9), units(12)
            for lv in range(5):
                for q4 in range(4):
                    pe.wait_ge(*V("X_ready", 4 * lv + q4 + 1))
                    name = f"Y{lv}_{q4}"
                    o = take(name, 4 + q4)
                    for j in range(4):
                        u = 4 * q4 + j
                        last = mm(o[:, j * P:(j + 1) * P], LT[:, u, :], X[:, u, :], True, True)
                    give(last, name)
                for q4 in range(4):
                    pe.wait_ge(*V("Y_ready", 4 * lv + q4 + 1))
                    name = f"ZT{lv}_{q4}"
                    o = take(name, q4)
                    for j in range(4):
                        u = 4 * q4 + j
                        last = mm(o[:, j * P:(j + 1) * P], Y[:, u, :], XT[:, u, :], True, True)
                    give(last, name)
                    if lv < 4:
                        name = f"Z{lv}_{q4}"
                        o = take(name, 4 + q4)
                        for j in range(4):
                            u = 4 * q4 + j
                            last = mm(o[:, j * P:(j + 1) * P], XT[:, u, :], Y[:, u, :], True, True)
                        give(last, name)
                if lv == 1:
                    project("dn_z_", h, [("dn_z", 1)])
            pe.wait_ge(*V("XT_final", 4))
            pe.wait_ge(*V("vb_ready", 1))
            for q4 in range(4):
                name = f"uc{q4}"
                o = take(name, 4 + q4)
                for j in range(4):
                    u = 4 * q4 + j
                    last = mm(o[:, j * P:(j + 1) * P], XT[:, u, :], units(8)[:, u, :], True, True)
                give(last, name)
            pe.wait_ge(*V("kbg_ready", 1))
            for q4 in range(4):
                name = f"wc{q4}"
                o = take(name, q4)
                for j in range(4):
                    u = 4 * q4 + j
                    last = mm(o[:, j * P:(j + 1) * P], units(3)[:, u, :], XT[:, u, :], True, True)
                give(last, name)
            state = page(5)[:, 0:HEADS * P].rearrange("p (h d) -> p h d", d=P)
            vnew, wT, qd, aT, kdec = units(11), units(12), units(2), units(10), units(7)
            pe.wait_ge(*V("wc_ready", 4))
            pe.wait_ge(*V("qd_ready", 1))
            pe.wait_ge(*V("kdec_ready", 1))
            for c in range(T // CHUNK):
                b, r = c // 2, CHUNK * (c % 2)
                if c > 0:
                    pe.wait_ge(*V("state_ready", c))
                    for hh in range(2):
                        name = f"ws{c}_{hh}"
                        o = take(name, 4 + hh)
                        for j in range(4):
                            hd = 4 * hh + j
                            last = mm(o[r:r + CHUNK, j * P:(j + 1) * P], wT[:, hd * NB + b, r:r + CHUNK],
                                      state[:, hd, :], True, True)
                        give(last, name)
                pe.wait_ge(*V("vnew_ready", 2 * c + 2))
                if c < T // CHUNK - 1:
                    for hh in range(2):
                        name = f"ds{c}_{hh}"
                        o = take(name, 6 + hh)
                        for j in range(4):
                            u = (4 * hh + j) * NB + b
                            last = mm(o[:, j * P:(j + 1) * P], kdec[r:r + CHUNK, u, :], vnew[r:r + CHUNK, u, :], True, True)
                        give(last, name)
                name = f"o{c}"
                o = take(name)
                for hd in range(HEADS):
                    u = hd * NB + b
                    dst = o[:, hd * CHUNK:(hd + 1) * CHUNK]
                    if c > 0:
                        mm(dst, state[:, hd, :], qd[:, u, r:r + CHUNK], True, False)
                    last = mm(dst, vnew[r:r + CHUNK, u, :], aT[r:r + CHUNK, u, r:r + CHUNK], c == 0, True)
                give(last, name)
                if c in (0, 1):
                    project(f"gate_b{'_' * c}", h, [("gate_b", c)])
            for q4 in range(4):
                pe.wait_ge(*V("o_squared", q4 + 1))
                name = f"o_ss{q4}"
                o = take(name)
                for half in range(2):
                    last = mm(o[:, half * T:(half + 1) * T], ones, fm(3)[:, 2 * q4 + half, :], True, True)
                give(last, name)
            pe.wait_ge(*V("yb_ready", KD))
            project("w_pb", fm(4), [("w_pb", 0), ("w_pb", 1)])
            pe.wait_ge(*V("merged", 4))
            project("w_o", fm(1), [("w_o", 0), ("w_o", 1)])
            pe.wait_ge(*V("res1", 4))
            norm("ln1", fm(0), fm(2), KD, True)
            if phases < 2:
                return

            pe.wait_ge(*V("ln1_out", KD))
            pe.wait_ge(*V("router_landed", 32))
            h = fm(0)
            wr = page(10)[:, 0:KD * 36].rearrange("p (k c) -> p k c", k=KD)
            o = take("router")
            for b in range(NB):
                for k in range(KD):
                    last = mm(o[:, b * 36:(b + 1) * 36], h[:, k, b * P:(b + 1) * P], wr[:, k, :], k == 0, k == KD - 1)
            give(last, "router")
            for b in range(NB):
                for half in range(2):
                    transposes(f"h_t{b}{half}", [h[:, 4 * half + j, b * P:(b + 1) * P] for j in range(4)])
            pick = page(11)[:, 512:576].rearrange("p (b e) -> p b e", b=NB)
            pe.wait_ge(*V("picked", 1))
            o = take("rank")
            mm(o[:, 0:32], table("before"), pick[:, 0, :], True, True)
            mm(o[:, 32:64], ones, pick[:, 0, :], True, False)
            mm(o[:, 32:64], table("before"), pick[:, 1, :], False, True)
            mm(o[:, 64:96], ones, pick[:, 0, :], True, False)
            mm(o[:, 64:96], ones, pick[:, 1, :], False, True)
            mm(o[0:EXPERTS, 96:97], pick[:, 0, :], ones[:, 0:1], True, False)
            give(mm(o[0:EXPERTS, 96:97], pick[:, 1, :], ones[:, 0:1], False, True), "rank")
            pe.wait_ge(*V("counts_spread", 1))
            o = take("start")
            give(mm(o[:, 0:EXPERTS], page(11)[0:EXPERTS, 640:640 + P], table("before")[0:EXPERTS, 0:EXPERTS], True, True), "start")
            onehot = page(8)[:, 0:NB * ASSIGN].rearrange("p (b s) -> p b s", b=NB)
            gated = page(8)[:, NB * ASSIGN:2 * NB * ASSIGN].rearrange("p (b s) -> p b s", b=NB)
            htm = page(1).rearrange("p (b c) -> p b c", b=NB)
            pe.wait_ge(*V("htm_ready", 4))
            pe.wait_ge(*V("onehot_ready", NB))
            for k in range(KD):
                name = f"xs{k}"
                o = take(name)
                for b in range(NB):
                    last = mm(o, htm[:, b, k * P:(k + 1) * P], onehot[:, b, :], b == 0, b == NB - 1)
                give(last, name)
            pe.wait_ge(*V("gated_ready", NB))
            for b in range(NB):
                transposes(f"gt{b}", [gated[:, b, s * P:(s + 1) * P] for s in range(4)])

            xs = page(2, 3).rearrange("p (k s) -> p k s", k=KD)
            act = page(10)[:, 1536:2048].rearrange("p (r s) -> p r s", r=2)

            def expert_h(r, start, slots, hbank, half):
                w = slots[half].rearrange("p (k c) -> p k c", k=KD)
                for f in range(FE // P):
                    for k in range(KD):
                        last = mm(psum[:, hbank, half * T + f * CAP:half * T + (f + 1) * CAP],
                                  w[:, k, f * P:(f + 1) * P], xs[:, k, bass.ds(start, CAP)], k == 0, k == KD - 1)
                return last

            def expert_y(r, w2, ybank):
                w = w2.rearrange("p (f c) -> p f c", c=D)
                for m in range(KD):
                    for f in range(FE // P):
                        last = mm(psum[:, ybank, m * CAP:(m + 1) * CAP], w[:, f, m * P:(m + 1) * P],
                                  act[:, r, f * CAP:(f + 1) * CAP], f == 0, f == FE // P - 1)
                return last

            pe.wait_ge(*V("xs_ready", KD))
            pe.wait_ge(*V("xs_tail", 1))
            pe.wait_ge(*V("starts_ready", 1))
            base = list(uses)
            place["moe_base"] = tuple(base)
            with pe.Fori(0, EXPERTS // 2) as it:
                for r in range(2):
                    n = moe_first + 3 * r
                    start = pe.value_load(starts[0:1, bass.ds(it * 2 + r, 1)], min_val=0, max_val=ASSIGN)
                    pe.wait_ge(free[r], it + base[r])
                    pe.wait_ge(landed[n % SLOTS], it * 16 + 16 * (n // SLOTS + 1))
                    expert_h(r, start, [slot(n), slot(n + 1)], r, 0).then_inc(S("w1_read"), 1)
                    pe.wait_ge(landed[(n + 1) % SLOTS], it * 16 + 16 * ((n + 1) // SLOTS + 1))
                    expert_h(r, start, [slot(n), slot(n + 1)], r, 1).then_inc(full[r], 1)
                    pe.wait_ge(free[2 + r], it + base[2 + r])
                    pe.wait_ge(free[r], it + base[r] + 1)
                    pe.wait_ge(landed[(n + 2) % SLOTS], it * 16 + 16 * ((n + 2) // SLOTS + 1))
                    expert_y(r, slot(n + 2), 2 + r).then_inc(full[2 + r], 1)
            for b in range(4):
                uses[b] += EXPERTS // 2
            for r in range(2):
                n = moe_first + 3 * (EXPERTS - 2 + r)
                released[n] = (S("w1_read"), EXPERTS - 1 + r)
                released[n + 1] = (full[r], uses[r])
                released[n + 2] = (full[2 + r], uses[2 + r])
            most = pe.value_load(starts[0:1, EXPERTS:EXPERTS + 1], min_val=0, max_val=T)
            for b in range(4):
                pe.wait_ge(free[b], uses[b])
            with pe.If(most > CAP):
                with pe.Fori(0, EXPERTS) as e:
                    pe.wait_ge(*V("more_landed", e * 48 + 48))
                    for c in range(MAX_PASSES):
                        start = pe.value_load(starts[0:1, bass.ds(e, 1)], min_val=0, max_val=ASSIGN)
                        begin = start + c * CAP
                        if c:
                            pe.wait_ge(*V("more_out", e * MAX_PASSES + c))
                        else:
                            pe.wait_ge(*V("more_out", e * MAX_PASSES))
                        expert_h(0, begin, [slot(0), slot(1)], 0, 0)
                        expert_h(0, begin, [slot(0), slot(1)], 0, 1).then_inc(S("more_h"), 1)
                        pe.wait_ge(*V("more_act", e * MAX_PASSES + c + 1))
                        expert_y(0, slot(2), 2).then_inc(S("more_y"), 1)
            ys = page(5, 3).rearrange("p (k s) -> p k s", k=KD)
            pe.wait_ge(*V("experts_done", 1))
            for s in range(4):
                for half in range(2):
                    transposes(f"y_t{s}{half}", [ys[:, 4 * half + j, s * P:(s + 1) * P] for j in range(4)])
            ytm = page(11, 2).rearrange("p (s c) -> p s c", s=4)
            gt = page(9)[:, 0:4 * T].rearrange("p (s t) -> p s t", t=T)
            pe.wait_ge(*V("ytm_ready", 8))
            pe.wait_ge(*V("gt_ready", 2))
            for m in range(4):
                name = f"moe{m}"
                o = take(name)
                for half in range(2):
                    k = 2 * m + half
                    for s in range(4):
                        last = mm(o[:, half * T:(half + 1) * T], ytm[:, s, k * P:(k + 1) * P], gt[:, s, :], s == 0, s == 3)
                give(last, name)
            pe.wait_ge(*V("res2", 4))
            norm("ln2", fm(0), fm(2), KD, True)
            if phases < 3:
                return

            def rms(nm, src, squares, nblocks=KD):
                norm(nm, src, squares, nblocks, False)

            def score(name, pairs):
                o = take(name)
                q, k = pairs
                mm(o[:, 0:P], q[:, 0:P], k[:, 0:P], True, True)
                give(mm(o[:, P:SPAN], q[:, P:T], k, True, True), name)

            def attend(sec, nheads, operands, values):
                e = lambda g: page(6)[:, (g % 3) * SPAN:(g % 3 + 1) * SPAN]
                pT = lambda g: page(7)[:, (g % 2) * SPAN:(g % 2 + 1) * SPAN]
                for i in range(nheads + 2):
                    if i < nheads:
                        score(f"{sec}s{i}", operands(i))
                    if 1 <= i <= nheads:
                        g = i - 1
                        pe.wait_ge(*V(f"{sec}_probs", g + 1))
                        transposes(f"{sec}t{g}", [e(g)[:, j * P:(j + 1) * P] for j in range(3)], 4 + g % 2)
                    if i >= 2:
                        g = i - 2
                        r = VDIM * (g % 2)
                        pe.wait_ge(*V(f"{sec}_pT", g + 1))
                        name = f"{sec}o{g // 2}"
                        o = take(name, 6 + g // 2 % 2) if g % 2 == 0 else bank_of(name)
                        dst = o[r:r + VDIM, :]
                        mm(dst[:, 0:P], values(g, 0), pT(g)[:, 0:P], True, True)
                        mm(dst[:, P:T], values(g, 0), pT(g)[:, P:2 * P], True, False)
                        last = mm(dst[:, P:T], values(g, 1), pT(g)[:, 2 * P:3 * P], False, True)
                        if g % 2:
                            give(last, name)
                        else:
                            last.then_inc(S(f"{sec}_even_o"), 1)

            def ffn(nm, layer):
                rhs = fm(1)
                first = item_no[(nm, 0)]
                base = list(uses)
                for b in range(3):
                    if base[b]:
                        pe.wait_ge(free[b], base[b])
                for b in range(4, 8):
                    pe.wait_ge(free[b], base[b])
                place[nm] = tuple(base)

                def gate_up(n, wait_landed, wait_free):
                    w = slot(n)[:, 0:2 * KD * P].rearrange("p (k c) -> p k c", k=KD)
                    bank = (n - first) % 3
                    wait_landed(n)
                    wait_free(bank)
                    for half in range(2):
                        for k in range(KD):
                            last = mm(psum[:, bank, half * T:(half + 1) * T], w[:, k, half * P:(half + 1) * P],
                                      rhs[:, k, :], k == 0, k == KD - 1)
                    last.then_inc(full[bank], 1)

                def down(n, wait_act, begin, end):
                    w = slot(n)[:, 2 * KD * P:3 * KD * P]
                    j3 = (n - first) % 3
                    a = page(2)[:, j3 * T:(j3 + 1) * T]
                    wait_act(j3)
                    for m in range(KD):
                        last = mm(psum[:, 4 + m // 2, (m % 2) * T:(m % 2 + 1) * T], w[:, m * P:(m + 1) * P], a,
                                  begin and m % 2 == 0, end)
                        if end and m % 2:
                            last.then_inc(full[4 + m // 2], 1)
                    if not end:
                        last.then_inc(S(f"{nm}_down"), 1)

                land = lambda n: pe.wait_ge(landed[n % SLOTS], 16 * (n // SLOTS + 1))
                gate_up(first, land, lambda b: None)
                with pe.Fori(0, 3) as it:
                    for r in range(6):
                        j = 1 + r
                        gate_up(first + j, lambda n: pe.wait_ge(landed[n % SLOTS], it * 16 + 16 * (n // SLOTS + 1)),
                                lambda b: pe.wait_ge(free[b], it * 2 + base[b] + j // 3))
                        down(first + j - 1, lambda b: pe.wait_ge(free[b], it * 2 + base[b] + (j - 1) // 3 + 1),
                             False, False)
                for j in range(19, FF_BLOCKS):
                    gate_up(first + j, land, lambda b: pe.wait_ge(free[b], base[b] + j // 3))
                    down(first + j - 1, lambda b: pe.wait_ge(free[b], base[b] + (j - 1) // 3 + 1), False, False)
                down(first + FF_BLOCKS - 1, lambda b: pe.wait_ge(free[b], base[b] + (FF_BLOCKS - 1) // 3 + 1), False, True)
                for b in range(3):
                    uses[b] += (FF_BLOCKS - b + 2) // 3
                for b in range(4, 8):
                    uses[b] += 1
                for j in range(FF_BLOCKS - 1):
                    released[first + j] = (S(f"{nm}_down"), j + 1)
                released[first + FF_BLOCKS - 1] = (full[7], uses[7])

            def clear_sums(nth):
                for b in range(4, 8):
                    if uses[b]:
                        pe.wait_ge(free[b], uses[b])
                pe.wait_ge(*V("zeros_ready", nth))
                for b in range(4, 8):
                    mm(psum[:, b, :], page(2)[:, 768:768 + P], page(2)[:, 768:768 + BANK], True, False)

            rms("att0", fm(0), fm(11))
            pe.wait_ge(*V("att0_scaled", KD))
            hn = fm(1)
            w = weights(("e_in", 0))[:, 0:KD * 448].rearrange("p (k c) -> p k c", k=KD)
            for nm_, c0, c1, r in (("cq", 0, 256, 0), ("ckv", 256, 384, 0), ("kr", 384, 448, NOPE)):
                o = take(nm_)
                if nm_ == "kr":
                    for half in range(2):
                        for k in range(KD):
                            c = c0 + half * ROPE
                            last = mm(o[r:r + ROPE, half * T:(half + 1) * T], w[:, k, c:c + ROPE], hn[:, k, :],
                                      k == 0, k == KD - 1)
                else:
                    for half in range((c1 - c0) // P):
                        for k in range(KD):
                            last = mm(o[:, half * T:(half + 1) * T], w[:, k, c0 + half * P:c0 + (half + 1) * P],
                                      hn[:, k, :], k == 0, k == KD - 1)
                give(last, nm_)
            release(("e_in", 0), "kr")
            project("qB", hn, [("e_in", 1)])
            project("kB", hn, [("e_in", 2)])
            rms("cqn", page(9)[:, 0:512].rearrange("p (k t) -> p k t", t=T),
                page(11)[:, 0:512].rearrange("p (k t) -> p k t", t=T), 2)
            rms("ckvn", page(9)[:, 512:768].rearrange("p (k t) -> p k t", t=T),
                page(11)[:, 512:768].rearrange("p (k t) -> p k t", t=T), 1)
            w = weights(("e_in", 3)).rearrange("p (k c) -> p k c", k=KD)
            for b in range(NB):
                o = take(f"vB{b}")
                for k in range(KD):
                    last = mm(o, hn[:, k, b * P:(b + 1) * P], w[:, k, :], k == 0, k == KD - 1)
                give(last, f"vB{b}")
            release(("e_in", 3), "vB1")
            w = weights(("mla_up", 0))
            wq = w[:, 0:2 * D].rearrange("p (k c) -> p k c", k=2)
            wkv = w[:, 2 * D:3 * D]
            cq = page(9)[:, 768:1280].rearrange("p (k t) -> p k t", t=T)
            ckv = page(9)[:, 1280:1536]
            pe.wait_ge(*V("cqn_scaled", 2))
            for hd in range(HEADS):
                name = f"qA{hd}"
                o = take(name)
                for k in range(2):
                    mm(o[0:NOPE + ROPE, 0:T], wq[:, k, hd * 96:(hd + 1) * 96], cq[:, k, :], k == 0, k == 1)
                for k in range(2):
                    c = 768 + hd * ROPE
                    last = mm(o[NOPE:NOPE + ROPE, T:2 * T], wq[:, k, c:c + ROPE], cq[:, k, :], k == 0, k == 1)
                give(last, name)
            pe.wait_ge(*V("ckvn_scaled", 1))
            for h2 in range(HEADS // 2):
                name = f"kA{h2}"
                o = take(name)
                for half in range(2):
                    c = (2 * h2 + half) * NOPE
                    last = mm(o[0:NOPE, half * T:(half + 1) * T], wkv[:, c:c + NOPE], ckv, True, True)
                give(last, name)
            for b in range(NB):
                o = take(f"vA{b}")
                last = mm(o, ckv[:, b * P:(b + 1) * P], wkv[:, 512:D], True, True)
                give(last, f"vA{b}")
            release(("mla_up", 0), "vA1")
            qA, kA = fm(2), fm(3)
            vA = page(4)[:, 0:D].rearrange("p (b c) -> p b c", b=NB)
            vB = page(4)[:, D:2 * D].rearrange("p (b c) -> p b c", b=NB)
            qB = page(5)[:, 0:D].rearrange("p (k t) -> p k t", t=T)
            kB = page(5)[:, D:2 * D].rearrange("p (k t) -> p k t", t=T)
            pe.wait_ge(*V("qA_ready", HEADS))
            pe.wait_ge(*V("kA_ready", 5))
            pe.wait_ge(*V("vA_ready", NB))
            attend("mla", HEADS, lambda i: (qA[0:96, i, :], kA[0:96, i, :]),
                   lambda g, b: vA[:, b, g * VDIM:(g + 1) * VDIM])
            pe.wait_ge(*V("qkB_ready", 4))
            pe.wait_ge(*V("vB_ready", NB))
            half_of = lambda i: slice(VDIM * (i % 2), VDIM * (i % 2) + VDIM)
            attend("dil", HEADS, lambda i: (qB[half_of(i), i // 2, :], kB[half_of(i), i // 2, :]),
                   lambda g, b: vB[:, b, g * VDIM:(g + 1) * VDIM])
            pe.wait_ge(*V("mla_o_ready", 4))
            pe.wait_ge(*V("dil_o_ready", 4))
            project("e_out", fm(8), [("e_out", 0), ("e_out", 1)])
            pe.wait_ge(*V("res3", 4))
            rms("ffn0n", fm(0), fm(11))
            pe.wait_ge(*V("ffn0n_scaled", KD))
            clear_sums(1)
            ffn("ffn0", 0)
            pe.wait_ge(*V("res4", 4))
            rms("att1", fm(0), fm(11))
            pe.wait_ge(*V("att1_scaled", KD))
            project("qS", hn, [("o_in", 0), ("o_in", 1)])
            w = weights(("o_kv", 0))[:, 0:KD * T].rearrange("p (k c) -> p k c", k=KD)
            o = take("kS")
            for k in range(KD):
                last = mm(o[:, 0:T], w[:, k, 0:P], hn[:, k, :], k == 0, k == KD - 1)
            give(last, "kS")
            o = take("vS")
            for b in range(NB):
                for k in range(KD):
                    last = mm(o[:, b * P:(b + 1) * P], hn[:, k, b * P:(b + 1) * P], w[:, k, P:2 * P], k == 0, k == KD - 1)
            give(last, "vS")
            release(("o_kv", 0), "vS")
            qS, kS = fm(2), page(3)[:, 0:T]
            vS = page(4)[:, 0:T].rearrange("p (b c) -> p b c", b=NB)
            pe.wait_ge(*V("qS_ready", 4))
            pe.wait_ge(*V("kvS_ready", 2))
            attend("swa", SWA_HEADS, lambda i: (qS[half_of(i), i // 2, :], kS[half_of(i), :]),
                   lambda g, b: vS[:, b, half_of(g)])
            pe.wait_ge(*V("swa_o_ready", 8))
            project("o_out", fm(8), [("o_out", 0), ("o_out", 1)])
            pe.wait_ge(*V("res5", 4))
            rms("ffn1n", fm(0), fm(11))
            pe.wait_ge(*V("ffn1n_scaled", KD))
            clear_sums(2)
            ffn("ffn1", 1)
            pe.wait_ge(*V("res6", 4))
            rms("final", fm(0), fm(11))

        @block.scalar
        def _(act_e):
            st = Steps(act_e, "act_step")

            def act(o, i, func, name=None, **kw):
                st.do(act_e.activation(o, i, func, **kw), name)

            def halves(name, fn, part_done, count):
                pass

            def norm(nm, src, squares, small, nblocks, width, eps, dst=None, bias=None):
                nh = 2 if nblocks == KD else 1
                for i in range(nh):
                    if bias is not None:
                        act_e.wait_ge(*V(f"{nm}_centered", i + 1))
                    sl = slice(i * nblocks // nh, (i + 1) * nblocks // nh)
                    act(squares[:, sl, :], src[:, sl, :], ACT.Square, f"{nm}_squared")
                v = await_full(act_e, f"{nm}_var")
                act(small, v[:, 0:T], ACT.Ln, f"{nm}_var", scale=1.0 / width, bias=col(eps))
                st.settle()
                act(small, small, ACT.Exp, f"{nm}_rstd", scale=-0.5)
                if bias is not None:
                    add_bias(nm, dst, bias)

            def add_bias(nm, dst, bias):
                for k in range(KD):
                    act_e.wait_ge(*V(f"{nm}_scaled", k + 1))
                    act(dst[:, k, :], dst[:, k, :], ACT.Identity, f"{nm}_out", bias=col(bias, k))

            def evacuate(part, npairs, dst, func, bias, done, first=0):
                for n in range(npairs):
                    v = await_full(act_e, f"{part}{n}")
                    k = first + 2 * n
                    act(dst[:, k, :], v[:, 0:T], func, bias=col("b_in", bias + k))
                    act(dst[:, k + 1, :], v[:, T:2 * T], func, f"{part}{n}", bias=col("b_in", bias + k + 1))

            for dst, src in ((tables[:], io["c_tables"]), (masks[:], io["c_masks"]), (cols[:], io["cols"]),
                             (rows[:], io["rows"][0:1, :].partition_broadcast(P)),
                             (ab[:, 0:P].rearrange("p (k c) -> p k c", k=KD), io["w_ab"].rearrange("(k p) c -> p k c", p=P)),
                             (page(3)[:, 0:KD * P].rearrange("p (g t) -> p g t", t=P), io["w_s"].rearrange("g s t -> s g t"))):
                act_e.dma_start(dst, src).then_inc(S("constants"), 16)
            act_e.dma_start(page(3)[0:1, KD * P:2 * KD * P], io["b_s"]).then_inc(S("bs_landed"), 16)
            act_e.wait_ge(*V("constants", 16 * 6))
            norm("ln_in", fm(0), fm(2), page(4)[:, 512:768], KD, D, "eps5", fm(0), "ln_in_b")
            evacuate("gm_v", 4, fm(2), ACT.Gelu, 8, None)
            act_e.wait_ge(*V("ln_in_out", KD))
            for n in range(4):
                v = await_full(act_e, f"gm_u{n}")
                for half in range(2):
                    act(fm(5)[:, 2 * n + half, :], v[:, half * T:(half + 1) * T], ACT.Gelu,
                        f"gm_u{n}" if half else None, bias=col("b_in", 2 * n + half))
            for i in range(2):
                act_e.wait_ge(*V("gm_centered", i + 1))
                act(fm(4)[:, 4 * i:4 * i + 4, :], fm(2)[:, 4 * i:4 * i + 4, :], ACT.Square, "gm_squared")
            evacuate("gate_a", 2, fm(6), ACT.Sigmoid, 48, None)
            v = await_full(act_e, "gm_var")
            act(page(7)[:, 256:512], v[:, 0:T], ACT.Ln, "gm_var", scale=1.0 / D, bias=col("eps5"))
            st.settle()
            act(page(7)[:, 256:512], page(7)[:, 256:512], ACT.Exp, "gm_rstd", scale=-0.5)
            add_bias("gm", fm(2), "gm_b")
            evacuate("gate_a_", 2, fm(6), ACT.Sigmoid, 48, None, first=4)
            stage = lambda n: page(5)[:, n % 6 * 260:n % 6 * 260 + 260]
            for part, pg, base in (("dn_q", 2, 0), ("dn_k", 3, 8), ("dn_v", 4, 16)):
                if part == "dn_q":
                    act_e.wait_ge(*V("stage_zero", 6))
                for n in range(4):
                    v = await_full(act_e, f"{part}{n}")
                    for half in range(2):
                        blk = base + 2 * n + half
                        if blk >= 6:
                            act_e.wait_ge(*V("conv_done", blk - 5))
                        act(stage(blk)[:, 4:260], v[:, half * T:(half + 1) * T], ACT.Identity, "staged",
                            bias=col("b_in", 16 + blk))
                    act_e.wait_ge(*V("staged", blk + 1))
                    act_e.sem_inc(free[place[f"{part}{n}"][0]], 1)
                    for b2 in (blk - 3, blk - 2):
                        if b2 >= 0:
                            silu_block(act_e, st, S, fm, b2)
                if part == "dn_k":
                    v = await_full(act_e, "ab")
            for b2 in (22, 23):
                silu_block(act_e, st, S, fm, b2)
            for part, pg, src in (("q", 7, 2), ("k", 8, 3)):
                for q4 in range(4):
                    act(fm(pg)[:, 2 * q4:2 * q4 + 2, :], fm(src)[:, 2 * q4:2 * q4 + 2, :], ACT.Square, f"{part}_squared")
            act_e.wait_ge(*V("ab_ready", 1))
            act(ab[:, 32:48], ab[:, 32:48], ACT.Exp, scale=-1.0)
            act(ab[:, 48:64], ab[:, 48:64], ACT.Exp, scale=-1.0)
            act(ab[:, 64:72], row("a_log", 8), ACT.Exp)
            st.settle()
            act(ab[:, 48:64], ab[:, 48:64], ACT.Ln, "ab_exps", bias=1.0)
            for q4 in range(4):
                v = await_full(act_e, f"Gb{q4}")
                act(page(9)[:, q4 * BANK:(q4 + 1) * BANK], v, ACT.Exp, "expG_row")
            act_e.wait_ge(*V("G_small", 1))
            act(ab[:, 96:128], ab[:, 96:128], ACT.Exp, "expG_col")
            act_e.wait_ge(*V("decay_clipped", 1))
            act(page(10, 2), page(10, 2), ACT.Exp, "decay_ready")
            for part, pg in (("q", 7), ("k", 8)):
                for q4 in range(4):
                    v = await_full(act_e, f"{part}_ss{q4}")
                    dst = page(pg)[:, q4 * BANK:(q4 + 1) * BANK]
                    act(dst, v, ACT.Ln, f"{part}_ss{q4}", bias=col("eps6"))
                    st.settle()
                    if part == "q":
                        act(dst, dst, ACT.Exp, "q_inv", scale=-0.5, bias=col("qscale"))
                    else:
                        act(dst, dst, ACT.Exp, "k_inv", scale=-0.5)
            for n in range(2):
                v = await_full(act_e, f"dn_z{n}")
                for half in range(2):
                    k = 2 * n + half
                    act(fm(6)[:, k, :], v[:, half * T:(half + 1) * T], ACT.Silu, f"dn_z{n}" if half else None,
                        bias=col("b_in", 40 + k))
            for q4 in range(4):
                act_e.wait_ge(*V("k_normed", 4))
                v = await_full(act_e, f"k_t{q4}")
                act(page(7)[:, q4 * BANK:(q4 + 1) * BANK], v, ACT.Copy, f"k_t{q4}")
                v = await_full(act_e, f"v_t{q4}")
                act(page(8)[:, q4 * BANK:(q4 + 1) * BANK], v, ACT.Copy, f"v_t{q4}")
            act_e.wait_ge(*st.last)
            act_e.sem_inc(S("tm_ready"), 1)
            for q4 in range(4):
                v = await_full(act_e, f"L_t{q4}")
                act(page(12)[:, q4 * BANK:(q4 + 1) * BANK], v, ACT.Copy, "LT_ready")
            for n in range(2):
                v = await_full(act_e, f"dn_z_{n}")
                for half in range(2):
                    k = 4 + 2 * n + half
                    act(fm(6)[:, k, :], v[:, half * T:(half + 1) * T], ACT.Silu, f"dn_z_{n}" if half else None,
                        bias=col("b_in", 40 + k))
            act_e.wait_ge(*st.last)
            act_e.sem_inc(S("z_ready"), 1)
            for q4 in range(4):
                v = await_full(act_e, f"wc{q4}")
                act(page(12)[:, q4 * BANK:(q4 + 1) * BANK], v, ACT.Copy, "wc_evac")
            act_e.wait_ge(*V("wc_evac", 4))
            for q4 in range(4):
                act_e.sem_inc(free[place[f"wc{q4}"][0]], 1)
                act_e.sem_inc(S("wc_ready"), 1)
            oT = fm(4)
            for c in range(T // CHUNK):
                v = await_full(act_e, f"o{c}")
                act(oT[:, :, c * CHUNK:(c + 1) * CHUNK], v.rearrange("p (h t) -> p h t", h=HEADS), ACT.Copy, f"o{c}")
                if c in (0, 1):
                    part = "gate_b" + "_" * c
                    for n in range(2):
                        v = await_full(act_e, f"{part}{n}")
                        for half in range(2):
                            k = 4 * c + 2 * n + half
                            act(fm(9)[:, k, :], v[:, half * T:(half + 1) * T], ACT.Sigmoid,
                                f"{part}{n}" if half else None, bias=col("b_in", 56 + k))
            st.settle()
            for q4 in range(4):
                act(fm(3)[:, 2 * q4:2 * q4 + 2, :], oT[:, 2 * q4:2 * q4 + 2, :], ACT.Square, "o_squared")
            for q4 in range(4):
                v = await_full(act_e, f"o_ss{q4}")
                dst = page(7)[:, q4 * BANK:(q4 + 1) * BANK]
                act(dst, v, ACT.Ln, f"o_ss{q4}", scale=1.0 / P, bias=col("eps6"))
                st.settle()
                act(dst, dst, ACT.Exp, "o_inv", scale=-0.5)
            if phases >= 2:
                act_e.dma_start(page(10)[:, 0:KD * 36].rearrange("p (k c) -> p k c", k=KD),
                                io["w_router"].rearrange("(k p) c -> p k c", p=P)).then_inc(S("router_landed"), 16)
                act_e.dma_start(page(10)[:, KD * 36:N_ROUTER], io["c_iota"]).then_inc(S("router_landed"), 16)
            norm("ln1", fm(0), fm(2), page(12)[:, 256:512], KD, D, "eps5", fm(0), "ln1_b")
            if phases < 2:
                return

            for b in range(NB):
                for half in range(2):
                    v = await_full(act_e, f"h_t{b}{half}")
                    act(page(1)[:, b * D + half * 512:b * D + (half + 1) * 512], v, ACT.Copy, "htm_evac")
                    act_e.wait_ge(*V("htm_evac", 2 * b + half + 1))
                    act_e.sem_inc(free[place[f"h_t{b}{half}"][0]], 1)
                    act_e.sem_inc(S("htm_ready"), 1)
            act_e.wait_ge(*V("group_centered", 1))
            act(page(11)[:, 80:96].rearrange("p (b g) -> p b g", b=NB)[:, :, 0:GROUPS],
                page(11)[:, 80:96].rearrange("p (b g) -> p b g", b=NB)[:, :, 0:GROUPS], ACT.Exp, "group_exp")
            act_e.wait_ge(*V("top_diff", 1))
            act(page(11)[:, 240:242], page(11)[:, 240:242], ACT.Exp, "top_exp")
            for k in range(KD):
                if k % 2 == 0:
                    v = await_full(act_e, f"xs{k}")
                    act(page(2, 3).rearrange("p (k s) -> p k s", k=KD)[:, k, 0:ASSIGN], v, ACT.Copy, f"xs{k}")
            act_e.wait_ge(*st.last)
            act_e.wait_ge(*V("xs_odd", 4))
            act_e.sem_inc(S("xs_ready"), KD)
            for b in range(NB):
                v = await_full(act_e, f"gt{b}")
                act(page(9)[:, 0:4 * T].rearrange("p (s t) -> p s t", t=T)[:, :, b * P:(b + 1) * P],
                    v.rearrange("p (s t) -> p s t", s=4), ACT.Copy, f"gt{b}")
            act_e.wait_ge(*st.last)
            act_e.sem_inc(S("gt_ready"), 2)
            silu = page(10)[:, 1024:1536].rearrange("p (r s) -> p r s", r=2)
            base = place["moe_base"]
            with act_e.Fori(0, EXPERTS // 2) as it:
                for r in range(2):
                    act_e.wait_ge(full[r], it + base[r] + 1)
                    act_e.wait_ge(free[r], it + base[r])
                    act_e.activation(silu[:, r, :], psum[:, r, 0:T], ACT.Silu).then_inc(S("silu_ready"), 1)
            most = act_e.value_load(starts[0:1, EXPERTS:EXPERTS + 1], min_val=0, max_val=T)
            with act_e.If(most > CAP):
                with act_e.Fori(0, EXPERTS) as e:
                    for c in range(MAX_PASSES):
                        act_e.wait_ge(*V("more_h", e * MAX_PASSES + c + 1))
                        act_e.wait_ge(*V("more_act", e * MAX_PASSES + c))
                        act_e.activation(silu[:, 0, :], psum[:, 0, 0:T], ACT.Silu).then_inc(S("more_silu"), 1)
            if phases >= 3:
                act_e.wait_ge(*V("experts_done", 1))
                act_e.dma_start(page(10), io["c_attn"]).then_inc(S("attn_tables"), 16)
            for s in range(4):
                for half in range(2):
                    v = await_full(act_e, f"y_t{s}{half}")
                    if half == 0:
                        act(page(11, 2)[:, s * D:s * D + 512], v, ACT.Copy, f"y_t{s}{half}")
            act_e.wait_ge(*st.last)
            act_e.wait_ge(*V("ytm_odd", 4))
            act_e.sem_inc(S("ytm_ready"), 8)
            norm("ln2", fm(0), fm(2), page(12)[:, 256:512], KD, D, "eps5", fm(0), "ln2_b")
            if phases < 3:
                return

            def rms(nm, src, squares, small, nblocks, width, before=None):
                if before:
                    act_e.wait_ge(*before)
                norm(nm, src, squares, small, nblocks, width, "eps6")

            def attend(sec, nheads, sink=False):
                stats = page(7)[:, 1024:1024 + 64]
                e = lambda g: page(6)[:, (g % 3) * SPAN:(g % 3 + 1) * SPAN]
                pT = lambda g: page(7)[:, (g % 2) * SPAN:(g % 2 + 1) * SPAN]
                for i in range(nheads + 1):
                    if i < nheads:
                        g = i
                        negm = stats[:, (g % 3) * 8:(g % 3) * 8 + 2]
                        z = stats[:, (g % 3) * 8 + 2:(g % 3) * 8 + 4]
                        act_e.wait_ge(*V(f"{sec}_max", 2 * g + 2))
                        if sec == "dil":
                            act(e(g)[:, 0:P], e(g)[:, 0:P], ACT.Exp, bias=negm[:, 0:1])
                            act(e(g)[:, P:SPAN], e(g)[:, P:SPAN], ACT.Exp, f"{sec}_exp", bias=negm[:, 1:2])
                        else:
                            act(e(g)[:, 0:P], e(g)[:, 0:P], ACT.Exp, bias=negm[:, 0:1], accum_out=z[:, 0:1])
                            if sink:
                                hd = g // 2 + HEADS * (g % 2)
                                act(stats[:, (g % 3) * 8 + 4:(g % 3) * 8 + 6], negm, ACT.Exp,
                                    bias=rows[:, ROWS["sinks"] + hd:ROWS["sinks"] + hd + 1])
                            act(e(g)[:, P:SPAN], e(g)[:, P:SPAN], ACT.Exp, f"{sec}_exp", bias=negm[:, 1:2],
                                accum_out=z[:, 1:2])
                    if i >= 1:
                        g = i - 1
                        v = await_full(act_e, f"{sec}t{g}")
                        if g >= 2:
                            if g % 2:
                                b_, n_ = place[f"{sec}o{(g - 2) // 2}"]
                                act_e.wait_ge(full[b_], n_)
                            else:
                                act_e.wait_ge(*V(f"{sec}_even_o", (g - 2) // 2 + 1))
                        act(pT(g), v[:, 0:SPAN], ACT.Copy, f"{sec}_pT")
                        act_e.wait_ge(*V(f"{sec}_pT", g + 1))
                        act_e.sem_inc(free[place[f"{sec}t{g}"][0]], 1)

            def ffn(nm):
                base = place[nm]
                silu_buf = page(2)[:, 1280:2048].rearrange("p (r t) -> p r t", t=T)

                def one(j3, wait_full, wait_free):
                    wait_full(j3)
                    wait_free(j3)
                    act_e.activation(silu_buf[:, j3, :], psum[:, j3, 0:T], ACT.Silu).then_inc(S(f"{nm}_silu"), 1)

                with act_e.Fori(0, 7) as it:
                    for r in range(3):
                        one(r, lambda b: act_e.wait_ge(full[b], it + base[b] + 1),
                            lambda b: act_e.wait_ge(free[b], it + base[b]))
                one(0, lambda b: act_e.wait_ge(full[b], 7 + base[b] + 1), lambda b: act_e.wait_ge(free[b], 7 + base[b]))
                st.last = (S(f"{nm}_silu"), FF_BLOCKS)

            rms("att0", fm(0), fm(11), page(12)[:, 256:512], KD, D, V("ln2_out", KD))
            q9 = page(9)[:, 0:512].rearrange("p (k t) -> p k t", t=T)
            v = await_full(act_e, "cq")
            act(page(9)[:, 0:512], v, ACT.Copy, "cq")
            v = await_full(act_e, "ckv")
            act(page(9)[:, 512:768], v[:, 0:T], ACT.Copy, "ckv")
            for part, off, scale in (("qB", 0, DIL_SCALE), ("kB", D, 1.0)):
                for n in range(2):
                    v = await_full(act_e, f"{part}{n}")
                    act(page(5)[:, off + n * 512:off + (n + 1) * 512], v, ACT.Copy, f"{part}{n}", scale=scale)
            st.settle()
            act_e.sem_inc(S("qkB_ready"), 4)
            rms("cqn", q9, page(11)[:, 0:512].rearrange("p (k t) -> p k t", t=T), page(12)[:, 512:768], 2, MLA_Q)
            rms("ckvn", page(9)[:, 512:768].rearrange("p (k t) -> p k t", t=T),
                page(11)[:, 512:768].rearrange("p (k t) -> p k t", t=T), page(12)[:, 768:1024], 1, MLA_KV)
            for b in range(NB):
                v = await_full(act_e, f"vB{b}")
                act(page(4)[:, D + b * 512:D + (b + 1) * 512], v, ACT.Copy, f"vB{b}")
            st.settle()
            act_e.sem_inc(S("vB_ready"), NB)
            for hd in range(HEADS):
                v = await_full(act_e, f"qA{hd}")
                act(fm(2)[0:NOPE, hd, :], v[0:NOPE, 0:T], ACT.Copy, "qA_nope", scale=MLA_SCALE)
            for h2 in range(HEADS // 2):
                v = await_full(act_e, f"kA{h2}")
                act(fm(3)[0:NOPE, 2 * h2:2 * h2 + 2, :], v[0:NOPE, :].rearrange("p (a t) -> p a t", a=2), ACT.Copy,
                    "kA_nope")
                act_e.wait_ge(*V("kA_nope", h2 + 1))
                act_e.sem_inc(free[place[f"kA{h2}"][0]], 1)
                act_e.sem_inc(S("kA_ready"), 1)
            for b in range(NB):
                v = await_full(act_e, f"vA{b}")
                act(page(4)[:, b * 512:(b + 1) * 512], v, ACT.Copy, f"vA{b}")
            st.settle()
            act_e.sem_inc(S("vA_ready"), NB)
            attend("mla", HEADS)
            attend("dil", HEADS)
            rms("ffn0n", fm(0), fm(11), page(12)[:, 256:512], KD, D, (S("res3"), 4))
            ffn("ffn0")
            rms("att1", fm(0), fm(11), page(12)[:, 256:512], KD, D, (S("res4"), 4))
            for n in range(4):
                v = await_full(act_e, f"qS{n}")
                act(page(2)[:, n * 512:(n + 1) * 512], v, ACT.Copy, "qS_evac", scale=DIL_SCALE)
                act_e.wait_ge(*V("qS_evac", n + 1))
                act_e.sem_inc(free[place[f"qS{n}"][0]], 1)
                act_e.sem_inc(S("qS_ready"), 1)
            v = await_full(act_e, "kS")
            act(page(3)[:, 0:T], v[:, 0:T], ACT.Copy, "kS")
            v = await_full(act_e, "vS")
            act(page(4)[:, 0:T], v[:, 0:T], ACT.Copy, "vS")
            st.settle()
            act_e.sem_inc(S("kvS_ready"), 2)
            attend("swa", SWA_HEADS, sink=True)
            rms("ffn1n", fm(0), fm(11), page(12)[:, 256:512], KD, D, (S("res5"), 4))
            ffn("ffn1")
            rms("final", fm(0), fm(11), page(12)[:, 256:512], KD, D, (S("res6"), 4))

        @block.vector
        def _(ve):
            st = Steps(ve, "dve_step")
            do, settle = st.do, st.settle

            def bc(ap, axis, shape):
                return ap.unsqueeze(axis).broadcast_to(shape)

            def center(nm, src, dst, small):
                v = await_full(ve, f"{nm}_mu")
                do(ve.tensor_scalar(small, v[:, 0:T], 1.0 / D, None, ALU.mult), f"{nm}_mu")
                settle()
                for i in range(2):
                    sl = slice(4 * i, 4 * i + 4)
                    do(ve.tensor_tensor(dst[:, sl, :], src[:, sl, :], bc(small, 1, [P, 4, T]), ALU.subtract),
                       f"{nm}_centered")

            def scale_rows(nm, src, dst, small, gain, nblocks, done):
                ve.wait_ge(*V(f"{nm}_rstd", 1))
                for k in range(nblocks):
                    do(ve.scalar_tensor_tensor(dst[:, k, :], src[:, k, :], col(gain, k), small, ALU.mult, ALU.mult), done)

            def layer_norm(nm, src, dst, mean, rstd, gain):
                center(nm, src, dst, mean)
                scale_rows(nm, dst, dst, rstd, gain, KD, f"{nm}_scaled")

            for n in range(6):
                pass
            ve.wait_ge(*V("constants", 16 * 6))
            ve.wait_ge(*V("x_landed", 16))
            layer_norm("ln_in", fm(1), fm(0), page(4)[:, 256:512], page(4)[:, 512:768], "ln_in_g")
            do(ve.memset(page(3)[CHUNK:P, 0:KD * P].rearrange("p (g t) -> p g t", t=P)[:, :, 0:CHUNK], 0.0), "gate_masked")
            for n in range(4):
                b_, n_ = place[f"gm_v{n}"]
                ve.wait_ge(free[b_], n_)
            ve.sem_inc(S("gm_v_ready"), 4)
            layer_norm("gm", fm(2), fm(2), page(7)[:, 0:256], page(7)[:, 256:512], "gm_g")
            for b in range(NB):
                for half in range(2):
                    v = await_full(ve, f"gm_t{b}{half}")
                    do(ve.tensor_copy(page(4)[:, b * D + half * 512:b * D + (half + 1) * 512], v), f"gm_t{b}{half}")
            settle()
            ve.sem_inc(S("gm_vtm"), 4)
            for n in range(4):
                v = await_full(ve, f"spatial{n}")
                b_, n_ = place[f"gm_u{n}"]
                ve.wait_ge(free[b_], n_)
                do(ve.tensor_tensor(page(5)[:, n * 512:(n + 1) * 512], v, page(5)[:, n * 512:(n + 1) * 512], ALU.mult),
                   f"spatial{n}")
            settle()
            ve.sem_inc(S("ya_ready"), 4)
            for part, off in (("gate_a", 0), ("gate_a_", 2)):
                for n in range(2):
                    b_, n_ = place[f"{part}{n}"]
                    ve.wait_ge(free[b_], n_)
            for n in range(4):
                v = await_full(ve, f"w_pa{n}")
                do(ve.tensor_tensor(page(1)[:, n * 512:(n + 1) * 512], v, page(6)[:, n * 512:(n + 1) * 512], ALU.mult),
                   f"w_pa{n}")
            settle()
            stage = lambda n: page(5)[:, n % 6 * 260:n % 6 * 260 + 260]
            for n in range(6):
                do(ve.memset(stage(n)[:, 0:4], 0.0), "stage_zero")
            for blk in range(24):
                if blk == 16:
                    ab_stage(ve, st, S, ab, row, await_full, bc)
                dst = fm(2 + blk // 8)[:, blk % 8, :]
                s = stage(blk)
                ve.wait_ge(*V("staged", blk + 1))
                tap = lambda j: col("conv", j * 24 + blk)
                do(ve.tensor_scalar(dst, s[:, 4:260], tap(3), None, ALU.mult))
                for j in range(3):
                    settle()
                    do(ve.scalar_tensor_tensor(dst, s[:, 1 + j:257 + j], tap(j), dst, ALU.mult, ALU.add),
                       "conv_done" if j == 2 else None)
            ve.wait_ge(*V("ab_exps", 1))
            ab_finish(ve, st, S, ab)
            v = await_full(ve, "G")
            G = ab[:, 80:96]
            do(ve.tensor_copy(G, v[:, 0:16]), "G")
            settle()
            D_, DT = page(11), page(10)
            for q4 in range(4):
                v = await_full(ve, f"Gb{q4}")
                ve.wait_ge(*V("expG_row", q4 + 1))
                v4 = v.rearrange("p (h b t) -> p h b t", h=2, b=NB)
                last = ab[:, 160 + 4 * q4:164 + 4 * q4].rearrange("p (h b) -> p h b", h=2)
                do(ve.tensor_copy(last[0:CHUNK], v4[0:CHUNK, :, :, CHUNK - 1]))
                do(ve.tensor_copy(last[CHUNK:P], v4[CHUNK:P, :, :, P - 1]))
                gcol = G.rearrange("p (b h) -> p h b", b=NB)[:, 2 * q4:2 * q4 + 2, :]
                gcol = gcol.unsqueeze(3).broadcast_to([P, 2, NB, P])
                view = lambda pg: pg[:, q4 * BANK:(q4 + 1) * BANK].rearrange("p (h b t) -> p h b t", h=2, b=NB)
                for hh in range(2):
                    do(ve.tensor_tensor(view(DT)[:, hh], v4[:, hh], gcol[:, hh], ALU.subtract))
                    do(ve.tensor_tensor(view(D_)[:, hh], gcol[:, hh], v4[:, hh], ALU.subtract),
                       f"Gb{q4}" if hh else None)
            settle()
            do(ve.tensor_scalar(page(10, 2), page(10, 2), 0.0, None, ALU.min), "decay_clipped")
            do(ve.tensor_copy(ab[:, 96:112], G))
            do(ve.tensor_tensor(ab[:, 112:128].rearrange("p (b h) -> p h b", b=NB), ab[:, 160:176].rearrange("p (h b) -> p h b", b=NB),
                                G.rearrange("p (b h) -> p h b", b=NB), ALU.subtract), "G_small")
            for part, pg, src in (("q", 7, 2), ("k", 8, 3)):
                for q4 in range(4):
                    ve.wait_ge(*V(f"{part}_inv", q4 + 1))
                    sl = slice(q4 * BANK, (q4 + 1) * BANK)
                    do(ve.tensor_tensor(page(src)[:, sl], page(src)[:, sl], page(pg)[:, sl], ALU.mult), f"{part}_normed")
            ve.wait_ge(*V("decay_masked", 2))
            for q4 in range(4):
                v = await_full(ve, f"kk{q4}")
                sl = slice(q4 * BANK, (q4 + 1) * BANK)
                do(ve.tensor_tensor(page(11)[:, sl], v, page(11)[:, sl], ALU.mult), f"kk{q4}")
                settle()
                ve.sem_inc(S("L_ready"), 1)
            ve.wait_ge(*V("tm_ready", 1))
            idb = bc(ident, 1, [P, 4, P])
            for q4 in range(4):
                sl = slice(q4 * BANK, (q4 + 1) * BANK)
                v3 = lambda pg: page(pg)[:, sl].rearrange("p (u t) -> p u t", t=P)
                do(ve.tensor_tensor(v3(5), v3(11), bc(mask("first"), 1, [P, 4, P]), ALU.mult))
                ve.wait_ge(*V("LT_ready", q4 + 1))
                do(ve.tensor_tensor(v3(4), v3(12), bc(mask("first_t"), 1, [P, 4, P]), ALU.mult))
                settle()
                do(ve.tensor_tensor(v3(5), idb, v3(5), ALU.subtract))
                do(ve.tensor_tensor(v3(4), idb, v3(4), ALU.subtract), "X_ready")
                b_, n_ = place[f"L_t{q4}"]
                ve.sem_inc(free[b_], 1)
            for q4 in range(4):
                v = await_full(ve, f"qk{q4}")
                sl = slice(q4 * BANK, (q4 + 1) * BANK)
                do(ve.tensor_tensor(page(10)[:, sl], v, page(10)[:, sl], ALU.mult), f"qk{q4}")
            settle()
            do(ve.tensor_tensor(page(2), page(2), page(9), ALU.mult), "qd_ready")
            cd = ab[:, 128:160]
            do(ve.tensor_copy(cd, page(9).rearrange("p (x t) -> p x t", t=CHUNK)[:, :, CHUNK - 1]))
            settle()
            for lv in range(5):
                for q4 in range(4):
                    sl = slice(q4 * BANK, (q4 + 1) * BANK)
                    v3 = lambda pg: page(pg)[:, sl].rearrange("p (u t) -> p u t", t=P)
                    name = f"Y{lv}_{q4}"
                    v = await_full(ve, name)
                    do(ve.tensor_tensor(v3(9), v.rearrange("p (u t) -> p u t", t=P),
                                        bc(mask(f"level{2 << lv}"), 1, [P, 4, P]), ALU.mult), "Y_evac")
                    ve.wait_ge(*V("Y_evac", 4 * lv + q4 + 1))
                    ve.sem_inc(free[place[name][0]], 1)
                    ve.sem_inc(S("Y_ready"), 1)
                for q4 in range(4):
                    sl = slice(q4 * BANK, (q4 + 1) * BANK)
                    if lv < 4:
                        v = await_full(ve, f"Z{lv}_{q4}")
                    w = await_full(ve, f"ZT{lv}_{q4}")
                    do(ve.tensor_tensor(page(4)[:, sl], page(4)[:, sl], w, ALU.subtract), f"ZT{lv}_{q4}")
                    if lv < 4:
                        do(ve.tensor_tensor(page(5)[:, sl], page(5)[:, sl], v, ALU.subtract), f"Z{lv}_{q4}")
                        settle()
                        ve.sem_inc(S("X_ready"), 1)
            settle()
            ve.sem_inc(S("XT_final"), 4)
            for q4 in range(4):
                v = await_full(ve, f"uc{q4}")
                do(ve.tensor_copy(page(11)[:, q4 * BANK:(q4 + 1) * BANK], v), f"uc{q4}")
            settle()
            ve.sem_inc(S("vnew_ready"), 2)
            state = page(5)[:, 0:HEADS * P]
            vn = page(11).rearrange("p (h b d) -> p h b d", b=NB, d=P)
            for c in range(T // CHUNK):
                b, r = c // 2, CHUNK * (c % 2)
                if c > 0:
                    for hh in range(2):
                        v = await_full(ve, f"ws{c}_{hh}")
                        dst = vn[r:r + CHUNK, 4 * hh:4 * hh + 4, b, :]
                        do(ve.tensor_tensor(dst, dst, v[r:r + CHUNK, :].rearrange("p (h d) -> p h d", h=4), ALU.subtract),
                           "vnew_evac")
                        ve.wait_ge(*V("vnew_evac", 2 * (c - 1) + hh + 1))
                        ve.sem_inc(free[place[f"ws{c}_{hh}"][0]], 1)
                        ve.sem_inc(S("vnew_ready"), 1)
                if c < T // CHUNK - 1:
                    if c > 0:
                        b_, n_ = place[f"o{c}"]
                        ve.wait_ge(full[b_], n_)
                    for hh in range(2):
                        v = await_full(ve, f"ds{c}_{hh}")
                        if c == 0:
                            do(ve.tensor_copy(state[:, hh * 512:(hh + 1) * 512], v), f"ds{c}_{hh}")
                        else:
                            for j in range(4):
                                hd = 4 * hh + j
                                sl = slice(hd * P, (hd + 1) * P)
                                x = hd * 4 + c
                                do(ve.scalar_tensor_tensor(state[:, sl], state[:, sl], cd[:, x:x + 1],
                                                           v[:, j * P:(j + 1) * P], ALU.mult, ALU.add),
                                   f"ds{c}_{hh}" if j == 3 else None)
                    settle()
                    ve.sem_inc(S("state_ready"), 1)
            b_, n_ = place["o3"]
            ve.wait_ge(free[b_], n_)
            ve.wait_ge(*V("z_ready", 1))
            for q4 in range(4):
                ve.wait_ge(*V("o_inv", q4 + 1))
                sl = slice(q4 * BANK, (q4 + 1) * BANK)
                do(ve.scalar_tensor_tensor(page(4)[:, sl], page(4)[:, sl], col("dn_norm"), page(7)[:, sl], ALU.mult,
                                           ALU.mult))
                settle()
                do(ve.tensor_tensor(page(4)[:, sl], page(4)[:, sl], page(6)[:, sl], ALU.mult))
                settle()
                ve.sem_inc(S("yb_ready"), 2)
            for n in range(4):
                v = await_full(ve, f"w_pb{n}")
                sl = slice(n * BANK, (n + 1) * BANK)
                do(ve.tensor_tensor(page(9)[:, sl], v, page(9)[:, sl], ALU.mult), f"w_pb{n}")
                settle()
                do(ve.tensor_tensor(page(1)[:, sl], page(1)[:, sl], page(9)[:, sl], ALU.add), "merged")

            def residual(part, alpha, done, names):
                for n, name in enumerate(names):
                    v = await_full(ve, name)
                    sl = slice(n * BANK, (n + 1) * BANK)
                    if alpha is None:
                        do(ve.tensor_tensor(page(0)[:, sl], page(0)[:, sl], v, ALU.add), name)
                    else:
                        do(ve.scalar_tensor_tensor(page(0)[:, sl], page(0)[:, sl], alpha, v, ALU.mult, ALU.add), name)
                    settle()
                    ve.sem_inc(S(done), 1)

            residual("w_o", ALPHA, "res1", [f"w_o{n}" for n in range(4)])
            layer_norm("ln1", fm(0), fm(0), page(12)[:, 0:256], page(12)[:, 256:512], "ln1_g")
            if phases < 2:
                return

            r11 = page(11)
            logits = r11[:, 0:72].rearrange("p (b c) -> p b c", b=NB)
            v = await_full(ve, "router")
            ve.wait_ge(*V("ln1_out", KD))
            ve.wait_ge(*V("router_landed", 32))
            do(ve.tensor_tensor(logits, v[:, 0:72].rearrange("p (b c) -> p b c", b=NB), bc(row("b_router", 36), 1, [P, NB, 36]),
                                ALU.add), "router")
            ge = r11[:, 80:96].rearrange("p (b g) -> p b g", b=NB)
            do(ve.memset(r11[:, 80:96], -1.0))
            settle()
            two = lambda n: r11[:, 96 + 2 * n:98 + 2 * n]
            col2 = lambda ap, b: ap[:, b:b + 1]
            do(ve.tensor_reduce(two(0), logits[:, :, 0:GROUPS], AX.X, ALU.max))
            settle()
            do(ve.tensor_tensor(ge[:, :, 0:GROUPS], logits[:, :, 0:GROUPS], bc(two(0), 2, [P, NB, GROUPS]), ALU.subtract),
               "group_centered")
            ve.wait_ge(*V("group_exp", 1))
            do(ve.tensor_reduce(two(1), ge[:, :, 0:GROUPS], AX.X, ALU.add))
            settle()
            do(ve.reciprocal(two(2), two(1)))
            iota = page(10)[:, KD * 36:KD * 36 + ASSIGN]
            expert_row = page(10)[:, KD * 36 + ASSIGN:KD * 36 + ASSIGN + 32]
            group_row = page(10)[:, KD * 36 + ASSIGN + 32:KD * 36 + ASSIGN + 64]
            idx = r11[:, 128:192].bitcast(U32)
            masked = r11[:, 256:320].rearrange("p (b e) -> p b e", b=NB)
            for b in range(NB):
                do(ve.max(r11[:, 192:200], ge[:, b, :]))
                settle()
                do(ve.max_index(idx[:, 0:8], r11[:, 192:200], ge[:, b, :]))
                settle()
                do(ve.tensor_copy(r11[:, 112 + b:113 + b], idx[:, 0:1]))
                settle()
                do(ve.tensor_scalar(masked[:, b, :], group_row, r11[:, 112 + b:113 + b], None, ALU.is_equal))
                settle()
                do(ve.tensor_scalar(masked[:, b, :], masked[:, b, :], 1.0, 1e30, ALU.subtract, ALU.mult))
                settle()
                do(ve.tensor_tensor(masked[:, b, :], masked[:, b, :], logits[:, b, GROUPS:36], ALU.add))
                settle()
                do(ve.max(r11[:, 200 + 8 * b:208 + 8 * b], masked[:, b, :]))
                settle()
                do(ve.max_index(idx[:, 8 + 8 * b:16 + 8 * b], r11[:, 200 + 8 * b:208 + 8 * b], masked[:, b, :]))
                settle()
                do(ve.tensor_copy(r11[:, 120 + 2 * b:122 + 2 * b], idx[:, 8 + 8 * b:10 + 8 * b]))
            best = r11[:, 200:216].rearrange("p (b x) -> p b x", b=NB)
            settle()
            do(ve.tensor_tensor(r11[:, 240:242], best[:, :, 1], best[:, :, 0], ALU.subtract), "top_diff")
            eh = lambda s: r11[:, 320 + 64 * s:384 + 64 * s].rearrange("p (b e) -> p b e", b=NB)
            pick = r11[:, 512:576]
            for b in range(NB):
                for s in range(2):
                    do(ve.tensor_scalar(eh(s)[:, b, :], expert_row, r11[:, 120 + 2 * b + s:121 + 2 * b + s], None, ALU.is_equal))
            settle()
            do(ve.tensor_tensor(pick, r11[:, 320:384], r11[:, 384:448], ALU.add), "picked")
            ve.wait_ge(*V("top_exp", 1))
            do(ve.tensor_scalar(r11[:, 242:244], r11[:, 240:242], 1.0, None, ALU.add))
            settle()
            do(ve.reciprocal(r11[:, 244:246], r11[:, 242:244]))
            settle()
            do(ve.tensor_tensor(r11[:, 246:248], r11[:, 244:246], two(2), ALU.mult))
            settle()
            do(ve.tensor_tensor(r11[:, 248:250], r11[:, 246:248], r11[:, 240:242], ALU.mult))
            v = await_full(ve, "rank")
            do(ve.tensor_copy(r11[0:EXPERTS, 640:640 + P], v[0:EXPERTS, 96:97].broadcast_to([EXPERTS, P])), "counts_spread")
            do(ve.tensor_reduce(r11[0:1, 252:253], v[0:1, 64:96], AX.X, ALU.max))
            settle()
            do(ve.tensor_copy(starts[0:1, EXPERTS:EXPERTS + 1], r11[0:1, 252:253]))
            do(ve.tensor_copy(r11[:, 576:640], v[:, 0:64]), "rank")
            v = await_full(ve, "start")
            do(ve.tensor_copy(starts[0:1, 0:EXPERTS], v[0:1, 0:EXPERTS]))
            settle()
            ve.sem_inc(S("starts_ready"), 1)
            where = r11[:, 576:640].rearrange("p (b e) -> p b e", b=NB)
            do(ve.tensor_tensor(where, where, bc(v[:, 0:EXPERTS], 1, [P, NB, EXPERTS]), ALU.add), "start")
            settle()
            for s in range(2):
                do(ve.tensor_tensor(eh(s), eh(s), where, ALU.mult))
            settle()
            for s in range(2):
                do(ve.tensor_reduce(r11[:, 224 + 2 * s:226 + 2 * s], eh(s), AX.X, ALU.add))
            settle()
            onehot = page(8)[:, 0:NB * ASSIGN].rearrange("p (b s) -> p b s", b=NB)
            gated = page(8)[:, NB * ASSIGN:2 * NB * ASSIGN].rearrange("p (b s) -> p b s", b=NB)
            pos = lambda s, b: r11[:, 224 + 2 * s + b:225 + 2 * s + b]
            gate = lambda s, b: r11[:, 246 + 2 * s + b:247 + 2 * s + b]
            for b in range(NB):
                do(ve.tensor_scalar(onehot[:, b, :], iota, pos(0, b), None, ALU.is_equal))
                settle()
                do(ve.scalar_tensor_tensor(onehot[:, b, :], iota, pos(1, b), onehot[:, b, :], ALU.is_equal, ALU.add),
                   "onehot_ready")
            spare = r11[:, 1024:1536]
            for b in range(NB):
                do(ve.tensor_scalar(gated[:, b, :], iota, pos(0, b), gate(0, b), ALU.is_equal, ALU.mult))
                do(ve.tensor_scalar(spare, iota, pos(1, b), gate(1, b), ALU.is_equal, ALU.mult))
                settle()
                do(ve.tensor_tensor(gated[:, b, :], gated[:, b, :], spare, ALU.add), "gated_ready")
                settle()
            for k in range(1, KD, 2):
                v = await_full(ve, f"xs{k}")
                do(ve.tensor_copy(page(2, 3).rearrange("p (k s) -> p k s", k=KD)[:, k, 0:ASSIGN], v), f"xs{k}")
            settle()
            ve.sem_inc(S("xs_odd"), 4)
            silu = page(10)[:, 1024:1536].rearrange("p (r s) -> p r s", r=2)
            acts = page(10)[:, 1536:2048].rearrange("p (r s) -> p r s", r=2)
            ys = page(5, 3).rearrange("p (k s) -> p k s", k=KD)
            base = place["moe_base"]
            with ve.Fori(0, EXPERTS // 2) as it:
                for r in range(2):
                    start = ve.value_load(starts[0:1, bass.ds(it * 2 + r, 1)], min_val=0, max_val=ASSIGN)
                    ve.wait_ge(*V("silu_ready", it * 2 + r + 1))
                    ve.wait_ge(full[2 + r], it + base[2 + r])
                    ve.tensor_tensor(acts[:, r, :], silu[:, r, :], psum[:, r, T:2 * T], ALU.mult).then_inc(free[r], 1)
                    ve.wait_ge(full[2 + r], it + base[2 + r] + 1)
                    ve.tensor_copy(ys[:, :, bass.ds(start, CAP)],
                                   psum[:, 2 + r, :].rearrange("p (k s) -> p k s", k=KD)).then_inc(free[2 + r], 1)
            st.last = (free[3], base[3] + EXPERTS // 2)
            settle()
            most = ve.value_load(starts[0:1, EXPERTS:EXPERTS + 1], min_val=0, max_val=T)
            with ve.If(most > CAP):
                with ve.Fori(0, EXPERTS) as e:
                    start = ve.value_load(starts[0:1, bass.ds(e, 1)], min_val=0, max_val=ASSIGN)
                    for c in range(MAX_PASSES):
                        ve.wait_ge(*V("more_silu", e * MAX_PASSES + c + 1))
                        ve.tensor_tensor(acts[:, 0, :], silu[:, 0, :], psum[:, 0, T:2 * T], ALU.mult).then_inc(S("more_act"), 1)
                        ve.wait_ge(*V("more_y", e * MAX_PASSES + c + 1))
                        ve.wait_ge(*V("more_out", e * MAX_PASSES + c))
                        ve.tensor_copy(ys[:, :, bass.ds(start + c * CAP, CAP)],
                                       psum[:, 2, :].rearrange("p (k s) -> p k s", k=KD)).then_inc(S("more_out"), 1)
                ve.wait_ge(*V("more_out", EXPERTS * MAX_PASSES))
            do(ve.memset(ab[:, 0:1], 0.0), "experts_done")
            for s in range(4):
                v = await_full(ve, f"y_t{s}1")
                do(ve.tensor_copy(page(11, 2)[:, s * D + 512:(s + 1) * D], v), f"y_t{s}1")
            settle()
            ve.sem_inc(S("ytm_odd"), 4)
            residual("moe", ALPHA, "res2", [f"moe{m}" for m in range(4)])
            layer_norm("ln2", fm(0), fm(0), page(12)[:, 0:256], page(12)[:, 256:512], "ln2_g")
            if phases < 3:
                return

            attn = lambda n: page(10)[:, n * SPAN:(n + 1) * SPAN]
            dil_t, mult_t, swa_t, causal_t = (attn(n) for n in range(4))
            cos = page(10)[:, 4 * SPAN:4 * SPAN + T]
            sin = page(10)[:, 4 * SPAN + T:4 * SPAN + 2 * T]
            rope = slice(NOPE, NOPE + ROPE)

            def attend(sec, nheads, bias, slope, sink=False):
                stats = page(7)[:, 1024:1024 + 64]
                e = lambda g: page(6)[:, (g % 3) * SPAN:(g % 3 + 1) * SPAN]
                for i in range(nheads + 1):
                    if i < nheads:
                        g = i
                        v = await_full(ve, f"{sec}s{g}")
                        if g >= 3:
                            b_, n_ = place[f"{sec}t{g - 3}"]
                            ve.wait_ge(full[b_], n_)
                        negm = stats[:, (g % 3) * 8:(g % 3) * 8 + 2]
                        do(ve.scalar_tensor_tensor(e(g), bias, slope(g), v[:, 0:SPAN], ALU.mult, ALU.add), f"{sec}s{g}")
                        settle()
                        if sink:
                            hd = g // 2 + HEADS * (g % 2)
                            do(ve.tensor_reduce(negm[:, 0:1], e(g)[:, 0:P], AX.X, ALU.max))
                            do(ve.tensor_reduce(negm[:, 1:2], e(g)[:, P:SPAN], AX.X, ALU.max))
                            settle()
                            do(ve.tensor_scalar(negm, negm, rows[:, ROWS["sinks"] + hd:ROWS["sinks"] + hd + 1], -1.0,
                                                ALU.max, ALU.mult))
                            settle()
                            ve.sem_inc(S(f"{sec}_max"), 2)
                        else:
                            do(ve.tensor_reduce(negm[:, 0:1], e(g)[:, 0:P], AX.X, ALU.max, negate=True))
                            do(ve.tensor_reduce(negm[:, 1:2], e(g)[:, P:SPAN], AX.X, ALU.max, negate=True))
                            settle()
                            ve.sem_inc(S(f"{sec}_max"), 2)
                    if i >= 1:
                        g = i - 1
                        z = stats[:, (g % 3) * 8 + 2:(g % 3) * 8 + 4]
                        ve.wait_ge(*V(f"{sec}_exp", g + 1))
                        if sec == "dil":
                            for a, b, n in ((0, P, 0), (P, SPAN, 1)):
                                do(ve.tensor_tensor_reduce(e(g)[:, a:b], e(g)[:, a:b], mult_t[:, a:b], 1.0, 0.0,
                                                           ALU.mult, ALU.add, z[:, n:n + 1]))
                            settle()
                        if sink:
                            do(ve.tensor_tensor(z, z, stats[:, (g % 3) * 8 + 4:(g % 3) * 8 + 6], ALU.add))
                            settle()
                        do(ve.reciprocal(z, z))
                        settle()
                        do(ve.tensor_scalar(e(g)[:, 0:P], e(g)[:, 0:P], z[:, 0:1], None, ALU.mult))
                        do(ve.tensor_scalar(e(g)[:, P:SPAN], e(g)[:, P:SPAN], z[:, 1:2], None, ALU.mult), f"{sec}_probs")
                    if i >= 3 and i % 2 == 1:
                        output(sec, (i - 3) // 2)
                output(sec, nheads // 2 - 1)

            def output(sec, n):
                name = f"{sec}o{n}"
                v = await_full(ve, name)
                first = {"mla": 0, "dil": 4, "swa": 0}[sec]
                do(ve.tensor_copy(fm(8)[:, first + n, :], v[:, 0:T]), name)
                settle()
                ve.sem_inc(S(f"{sec}_o_ready"), 1)

            def ffn(nm, done):
                base = place[nm]
                silu_buf = page(2)[:, 1280:2048].rearrange("p (r t) -> p r t", t=T)
                acts = page(2)[:, 0:768].rearrange("p (r t) -> p r t", t=T)

                def one(j, it, first):
                    j3 = j % 3
                    ve.wait_ge(*V(f"{nm}_silu", it * 3 + j + 1 if it is not None else j + 1))
                    if not first:
                        ve.wait_ge(*V(f"{nm}_down", it * 3 + j - 2 if it is not None else j - 2))
                    ve.tensor_tensor(acts[:, j3, :], silu_buf[:, j3, :], psum[:, j3, T:2 * T], ALU.mult).then_inc(free[j3], 1)

                for j in range(3):
                    one(j, None, True)
                with ve.Fori(0, 6) as it:
                    for r in range(3):
                        one(3 + r, it, False)
                one(21, None, False)
                for n in range(4):
                    b = 4 + n
                    ve.wait_ge(full[b], base[b] + 1)
                    sl = slice(n * BANK, (n + 1) * BANK)
                    do(ve.tensor_tensor(page(0)[:, sl], page(0)[:, sl], psum[:, b, :], ALU.add), "ffn_sum")
                    settle()
                    ve.sem_inc(free[b], 1)
                    ve.sem_inc(S(done), 1)

            ve.wait_ge(*V("ln2_out", KD))
            scale_rows("att0", fm(0), fm(1), page(12)[:, 256:512], "att0", KD, "att0_scaled")
            ve.wait_ge(*V("attn_tables", 16))
            v = await_full(ve, "kr")
            t1, t2 = page(7)[rope, 1536:1792], page(7)[rope, 1792:2048]
            do(ve.tensor_tensor(t1, v[rope, 0:T], cos[rope, :], ALU.mult))
            do(ve.tensor_tensor(t2, v[rope, T:2 * T], sin[rope, :], ALU.mult), "kr")
            settle()
            do(ve.tensor_tensor(t1, t1, t2, ALU.add))
            settle()
            do(ve.tensor_copy(fm(3)[rope, :, :], bc(t1, 1, [ROPE, HEADS, T])))
            settle()
            ve.sem_inc(S("kA_ready"), 1)
            scale_rows("cqn", page(9)[:, 0:512].rearrange("p (k t) -> p k t", t=T),
                       page(9)[:, 768:1280].rearrange("p (k t) -> p k t", t=T), page(12)[:, 512:768], "q_norm", 2, "cqn_scaled")
            scale_rows("ckvn", page(9)[:, 512:768].rearrange("p (k t) -> p k t", t=T),
                       page(9)[:, 1280:1536].rearrange("p (k t) -> p k t", t=T), page(12)[:, 768:1024], "kv_norm", 1, "ckvn_scaled")
            for hd in range(HEADS):
                v = await_full(ve, f"qA{hd}")
                ve.wait_ge(*V("qA_nope", hd + 1))
                do(ve.scalar_tensor_tensor(t1, v[rope, 0:T], MLA_SCALE, cos[rope, :], ALU.mult, ALU.mult))
                do(ve.scalar_tensor_tensor(t2, v[rope, T:2 * T], MLA_SCALE, sin[rope, :], ALU.mult, ALU.mult), f"qA{hd}")
                settle()
                do(ve.tensor_tensor(fm(2)[rope, hd, :], t1, t2, ALU.add), "qA_ready")
                settle()
            attend("mla", HEADS, causal_t, lambda g: 1.0)
            attend("dil", HEADS, dil_t, lambda g: 2.0 ** -(g + 1))
            residual("e_out", None, "res3", [f"e_out{n}" for n in range(4)])
            scale_rows("ffn0n", fm(0), fm(1), page(12)[:, 256:512], "ffn0", KD, "ffn0n_scaled")
            do(ve.memset(page(2)[:, 768:1280], 0.0), "zeros_ready")
            ffn("ffn0", "res4")
            scale_rows("att1", fm(0), fm(1), page(12)[:, 256:512], "att1", KD, "att1_scaled")
            attend("swa", SWA_HEADS, swa_t, lambda g: 2.0 ** (-0.5 * (g // 2 + HEADS * (g % 2) + 1)), sink=True)
            residual("o_out", None, "res5", [f"o_out{n}" for n in range(4)])
            scale_rows("ffn1n", fm(0), fm(1), page(12)[:, 256:512], "ffn1", KD, "ffn1n_scaled")
            do(ve.memset(page(2)[:, 768:1280], 0.0), "zeros_ready")
            ffn("ffn1", "res6")
            scale_rows("final", fm(0), fm(1), page(12)[:, 256:512], "final", KD, "final_scaled")

        @block.gpsimd
        def _(pool):
            st = Steps(pool, "pool_step")
            pool.wait_ge(*V("decay_ready", 1))
            beta = ab[:, 16:32].rearrange("p (b h) -> p h b", b=NB)
            v3 = lambda pg: units(pg)
            bcu = lambda ap: ap.unsqueeze(1).broadcast_to([P, UNITS, P])
            st.do(pool.tensor_tensor(v3(11), v3(11), bcu(mask("strict_low")), ALU.mult))
            st.do(pool.tensor_tensor(v3(10), v3(10), bcu(mask("incl_up")), ALU.mult), "decay_masked")
            st.settle()

            def per_token(dst, src, what, name):
                for b in range(NB):
                    d = dst.rearrange("p (h b) t -> p h b t", b=NB)[:, :, b, :]
                    s = src.rearrange("p (h b) t -> p h b t", b=NB)[:, :, b, :]
                    w = what[:, b * HEADS:(b + 1) * HEADS].unsqueeze(2).broadcast_to([P, HEADS, P])
                    st.do(pool.tensor_tensor(d, s, w, ALU.mult), name if b else None)

            per_token(v3(11), v3(11), ab[:, 16:32], "decay_masked")
            pool.wait_ge(*V("tm_ready", 1))
            per_token(v3(8), v3(8), ab[:, 16:32], "vb_ready")
            pool.wait_ge(*V("expG_col", 1))
            st.do(pool.tensor_tensor(ab[:, 96:112], ab[:, 96:112], ab[:, 16:32], ALU.mult))
            st.settle()
            for q4 in range(4):
                b_, n_ = place[f"qk{q4}"]
                pool.wait_ge(full[b_], n_)
            per_token(v3(3), v3(7), ab[:, 96:112], "kbg_ready")
            st.settle()
            per_token(v3(7), v3(7), ab[:, 112:128], "kdec_ready")
            if phases >= 2:
                pool.wait_ge(*V("ln1_out", KD))
                st.do(pool.memset(page(2, 3).rearrange("p (k s) -> p k s", k=KD)[:, :, ASSIGN:SORTED], 0.0), "xs_tail")

        @block.sync
        def _(sp):
            sp.dma_start(fm(1), io["xT"].rearrange("(k p) t -> p k t", p=P)).then_inc(S("x_landed"), 16)

            def columns(name, c0, width):
                return io[name].rearrange("(k p) c -> p k c", p=P)[:, :, c0:c0 + width]

            first_column = {"gm_u": 0, "gm_v": 1024, "dn_q": 2048, "dn_k": 3072, "dn_v": 4096, "dn_z": 5120,
                            "gate_a": 6160, "gate_b": 7184}

            def source(name, i):
                if name in first_column:
                    return columns("w_in", first_column[name] + 512 * i, 512)
                if name in ("w_pa", "w_pb", "w_o", "e_out", "o_out"):
                    return columns(name, 512 * i, 512)
                if name == "e_in":
                    return columns("e_in", 0, 448) if i == 0 else columns("e_in", 448 + 512 * (i - 1), 512)
                if name == "mla_up":
                    return io["mla_up"]
                if name == "o_in":
                    return columns("o_in", 512 * i, 512)
                if name == "o_kv":
                    return columns("o_in", 1024, 256)
                return io[name][i]

            def load(n, name, i, wait=True):
                if wait and n >= SLOTS:
                    sp.wait_ge(*released[n - SLOTS])
                src = source(name, i)
                floats = int(np.prod(src.shape[1:]))
                dst = slot(n, floats)
                if len(src.shape) == 3:
                    dst = dst.rearrange("p (k c) -> p k c", k=src.shape[1])
                sp.dma_start(dst, src).then_inc(landed[n % SLOTS], 16)

            expert_src = lambda name, e: io[name][bass.ds(e, 1)].rearrange("e (k p) c -> p (e k) c", p=P)

            def load_expert(n, name, e):
                src = expert_src(name, e)
                sp.dma_start(slot(n).rearrange("p (k c) -> p k c", k=src.shape[1]), src)\
                    .then_inc(landed[n % SLOTS], 16)

            for n, (name, i) in enumerate(items[:moe_first]):
                load(n, name, i)
            if phases >= 2:
                for r in range(2):
                    for x, name in enumerate(("w1", "w3", "w2")):
                        n = moe_first + 3 * r + x
                        sp.wait_ge(*released[n - SLOTS])
                        src = io[name][r].rearrange("(k p) c -> p k c", p=P)
                        sp.dma_start(slot(n).rearrange("p (k c) -> p k c", k=src.shape[1]), src)\
                            .then_inc(landed[n % SLOTS], 16)
                base = place["moe_base"]
                with sp.Fori(1, EXPERTS // 2) as it:
                    for r in range(2):
                        n = moe_first + 3 * r
                        sp.wait_ge(*V("w1_read", it * 2 + r - 1))
                        src = expert_src("w1", it * 2 + r)
                        sp.dma_start(slot(n).rearrange("p (k c) -> p k c", k=KD), src).then_inc(landed[n % SLOTS], 16)
                        sp.wait_ge(full[r], it + base[r])
                        src = expert_src("w3", it * 2 + r)
                        sp.dma_start(slot(n + 1).rearrange("p (k c) -> p k c", k=KD), src).then_inc(landed[(n + 1) % SLOTS], 16)
                        sp.wait_ge(full[2 + r], it + base[2 + r])
                        src = expert_src("w2", it * 2 + r)
                        sp.dma_start(slot(n + 2).rearrange("p (k c) -> p k c", k=FE // P), src).then_inc(landed[(n + 2) % SLOTS], 16)
                sp.wait_ge(*V("starts_ready", 1))
                most = sp.value_load(starts[0:1, EXPERTS:EXPERTS + 1], min_val=0, max_val=T)
                with sp.If(most > CAP):
                    for n in range(moe_first + 3 * EXPERTS - SLOTS, moe_first + 3 * EXPERTS):
                        sp.wait_ge(*released[n])
                    with sp.Fori(0, EXPERTS) as e:
                        sp.wait_ge(*V("more_y", e * MAX_PASSES))
                        for s, name in enumerate(("w1", "w3", "w2")):
                            src = expert_src(name, e)
                            sp.dma_start(slot(s).rearrange("p (k c) -> p k c", k=src.shape[1]), src)\
                                .then_inc(S("more_landed"), 16)
                    sp.wait_ge(*V("more_y", EXPERTS * MAX_PASSES))
            if phases >= 3:
                for n in range(moe_first + 3 * EXPERTS, len(items)):
                    load(n, *items[n])
            if phases == 3:
                sp.wait_ge(*V("final_scaled", KD))
                result = fm(1)
            else:
                sp.wait_ge(*V("ln1_out" if phases == 1 else "ln2_out", KD))
                result = fm(0)
            sp.dma_start(out.rearrange("(k p) t -> p k t", p=P), result).then_inc(S("stored"), 16)
            sp.wait_ge(*V("stored", 16))


MLA_SCALE = 1.0 / float(np.sqrt(NOPE + ROPE))
DIL_SCALE = 0.125


def silu_block(act_e, st, S, fm, blk):
    act_e.wait_ge(S("conv_done"), blk + 1)
    dst = fm(2 + blk // 8)[:, blk % 8, :]
    st.do(act_e.activation(dst, dst, ACT.Silu), "v_ready" if blk >= 16 else "qk_silu")


def ab_stage(ve, st, S, ab, row, await_full, bc):
    v = await_full(ve, "ab")
    v3 = v[:, 0:32].rearrange("p (b c) -> p b c", b=NB)
    view = lambda c: ab[:, c:c + 16].rearrange("p (b h) -> p b h", b=NB)
    st.do(ve.tensor_tensor(view(144), v3[:, :, 0:8], bc(row("b_a", 8), 1, [P, NB, 8]), ALU.add))
    st.do(ve.tensor_tensor(view(32), v3[:, :, 8:16], bc(row("b_b", 8), 1, [P, NB, 8]), ALU.add), "ab")
    st.settle()
    st.do(ve.tensor_tensor(view(144), view(144), bc(row("dt_bias", 8), 1, [P, NB, 8]), ALU.add))
    st.settle()
    st.do(ve.tensor_scalar(ab[:, 128:144], ab[:, 144:160], -1.0, None, ALU.mult))
    st.settle()
    st.do(ve.tensor_tensor(ab[:, 48:64], ab[:, 128:144], ab[:, 144:160], ALU.max), "ab_ready")


def ab_finish(ve, st, S, ab):
    st.do(ve.tensor_scalar(ab[:, 32:48], ab[:, 32:48], 1.0, None, ALU.add))
    st.do(ve.scalar_tensor_tensor(ab[:, 144:160], ab[:, 144:160], 0.0, ab[:, 48:64], ALU.max, ALU.add))
    st.settle()
    st.do(ve.reciprocal(ab[:, 16:32], ab[:, 32:48]))
    view = lambda c: ab[:, c:c + 16].rearrange("p (b h) -> p b h", b=NB)
    st.do(ve.scalar_tensor_tensor(view(0), view(144), -1.0, ab[:, 64:72].unsqueeze(1).broadcast_to([P, NB, HEADS]),
                                  ALU.mult, ALU.mult), "g_ready")


def lay_out(inputs):
    f = {k: np.asarray(v) for k, v in inputs.items()}
    blocks = lambda v: np.ascontiguousarray(v).reshape(-1, P).T
    b_in = f["b_in"][0]
    ab0 = 6 * D
    main = np.concatenate([b_in[:ab0], b_in[ab0 + 16:]])
    cols = np.concatenate([
        blocks(f["ln_in_g"]), blocks(f["ln_in_b"]), blocks(f["gm_ln_g"]), blocks(f["gm_ln_b"]),
        blocks(f["ln1_g"]), blocks(f["ln1_b"]), blocks(f["ln2_g"]), blocks(f["ln2_b"]),
        blocks(f["attn_norm_2"][0]), blocks(f["attn_norm_2"][1]), blocks(f["ffn_norm_2"][0]),
        blocks(f["ffn_norm_2"][1]), blocks(f["final_norm_2"]), blocks(main), blocks(f["dn_conv_w"][0]),
        blocks(f["dn_norm_w"]), blocks(f["e_q_norm_2"]), blocks(f["e_kv_norm_2"]),
        np.full((P, 1), 1e-5, np.float32), np.full((P, 1), 1e-6, np.float32),
        np.full((P, 1), -0.5 * np.log(float(P)), np.float32)], axis=1)
    rows = np.concatenate([f["dn_a_log"][0], f["dn_dt_bias"][0], b_in[ab0:ab0 + 16], f["b_rg"][0], f["b_re"][0],
                           f["o_sinks_2"][0]])[None, :]
    e_in = f["e_w_in_2"][0]
    swap = lambda w: np.concatenate([w[..., ROPE // 2:], w[..., :ROPE // 2]], axis=-1)
    kr = e_in[:, 384:416]
    e_in = np.concatenate([e_in[:, 0:416], swap(kr), e_in[:, 416:]], axis=1)
    uq = f["e_w_uq_2"][0]
    uq_rope = swap(uq.reshape(MLA_Q, HEADS, 96)[:, :, NOPE:]).reshape(MLA_Q, HEADS * ROPE)
    uq = np.concatenate([uq, uq_rope], axis=1).reshape(2, P, D).transpose(1, 0, 2).reshape(P, 2 * D)
    ukv = f["e_w_ukv_2"][0].reshape(MLA_KV, HEADS, 2, NOPE).transpose(0, 2, 1, 3).reshape(MLA_KV, D)
    pairs = lambda w: w.reshape(2, HEADS, 64, -1).transpose(1, 0, 2, 3).reshape(w.shape)
    o_in = f["o_w_qkv_2"][0]
    o_in = np.concatenate([pairs(np.ascontiguousarray(o_in[:, :D].T)).T, o_in[:, D:]], axis=1)

    def ffn(layer):
        gu = f["f_w_gate_up_2"][layer].reshape(KD, P, 2, FF_BLOCKS, P).transpose(3, 1, 0, 2, 4)
        down = f["f_w_down_2"][layer].reshape(FF_BLOCKS, P, D)
        return np.concatenate([gu.reshape(FF_BLOCKS, P, 2 * KD * P), down], axis=2)

    return {
        "xT": f["x"][0].T, "cols": cols, "rows": rows,
        "w_in": f["w_in"][0], "w_ab": f["w_in"][0][:, ab0:ab0 + 16],
        "w_s": f["gm_w_s"][0].transpose(0, 2, 1), "b_s": f["gm_b_s"][0].reshape(1, -1),
        "w_pa": f["w_pa"][0], "w_pb": f["w_pb"][0], "w_o": f["w_o"][0],
        "w_router": np.concatenate([f["w_rg"][0], f["w_re"][0]], axis=1),
        "w1": f["w1"][0], "w3": f["w3"][0], "w2": f["w2"][0],
        "e_in": e_in, "mla_up": np.concatenate([uq, ukv], axis=1), "e_out": f["e_w_out_2"][0],
        "o_in": o_in, "o_out": pairs(f["o_w_out_2"][0]), "ffn0": ffn(0), "ffn1": ffn(1),
    }


def kernel(phases=3, **inputs):
    import concourse.bacc as bacc
    from concourse.bass_utils import run_bass_kernel_spmd

    nc = bacc.Bacc("TRN2", target_bir_lowering=False, num_devices=1)
    arrays, io = {}, {}
    for name, a in {**lay_out(inputs), **shape_tables()}.items():
        arrays[f"in_{name}"] = np.ascontiguousarray(a)
        io[name] = nc.dram_tensor(f"in_{name}", a.shape, mybir.dt.from_np(a.dtype), kind="ExternalInput").ap()
    out = nc.dram_tensor("out", (D, T), F32, kind="ExternalOutput").ap()
    build(nc, io, out, phases)
    got = run_bass_kernel_spmd(nc, [arrays], core_ids=[0]).results[0]["out"]
    return np.ascontiguousarray(got.T)[None]
```

```python
from contextlib import ExitStack

import numpy as np

import concourse.bass as bass
from concourse import mybir

F32 = mybir.dt.float32
F16 = mybir.dt.float16
I32 = mybir.dt.int32
U32 = mybir.dt.uint32
F32R = mybir.dt.float32r
ALU = mybir.AluOpType
ACT = mybir.ActivationFunctionType
AX = mybir.AxisListType

P = 128
T = 256
NB = T // P
D = 1024
KD = D // P
HEADS = 8
CHUNK = 64
UNITS = HEADS * NB
EXPERTS = 32
GROUPS = 4
FE = 512
CAP = 64
MAX_PASSES = T // CAP
ASSIGN = 2 * T
SORTED = ASSIGN + MAX_PASSES * CAP
D_FF = 2816
FF_BLOCKS = D_FF // P
MLA_Q, MLA_KV, NOPE, ROPE, VDIM = 256, 128, 64, 32, 64
SWA_HEADS = 16
ALPHA = 2.0 ** 0.25
NEG = -1e30
NORMS = {"ln_in": KD, "gm": KD, "ln1": KD, "ln2": KD, "att0": KD, "cqn": 2, "ckvn": 1, "ffn0n": KD,
         "att1": KD, "ffn1n": KD, "final": KD}
LAYER_NORMS = ("ln_in", "gm", "ln1", "ln2")
SECTIONS = {"mla": HEADS, "dil": HEADS, "swa": SWA_HEADS}

SLOTS = 6
SLOT = 4096
PAGES = 13
PAGE = KD * T
BANK = 512

COLS = {}
_at = 0
for _name, _n in (("ln_in_g", 8), ("ln_in_b", 8), ("gm_g", 8), ("gm_b", 8), ("ln1_g", 8), ("ln1_b", 8),
                  ("ln2_g", 8), ("ln2_b", 8), ("att0", 8), ("att1", 8), ("ffn0", 8), ("ffn1", 8),
                  ("final", 8), ("b_in", 64), ("conv", 96), ("dn_norm", 1), ("q_norm", 2),
                  ("kv_norm", 1), ("eps5", 1), ("eps6", 1), ("qscale", 1)):
    COLS[_name] = _at
    _at += _n
NCOLS = _at
ROWS = {"a_log": 0, "dt_bias": 8, "b_a": 16, "b_b": 24, "b_router": 32, "sinks": 68}
NROWS = 84
TABLES = ("identity", "ones", "cumulate", "before")
MASKS = ("strict_low", "incl_up", "first", "first_t", "level2", "level4", "level8", "level16", "level32")
N_ROUTER = KD * 36 + ASSIGN + 64
SPAN = P + T


def shape_tables():
    i = np.arange(P)[:, None]
    j = np.arange(P)[None, :]
    same = i // CHUNK == j // CHUNK
    f32 = [np.eye(P), np.ones((P, P)), same & (i <= j), i < j]
    masks = [same & (i > j), same & (i <= j)]
    level = lambda s: (i // (2 * s) == j // (2 * s)) & (i // s % 2 == 1) & (j // s % 2 == 0)
    masks += [level(1), level(1).T] + [level(s) for s in (2, 4, 8, 16, 32)]
    experts = np.arange(EXPERTS)
    iota = np.concatenate([np.arange(ASSIGN), experts, experts // (EXPERTS // GROUPS)])
    dist = np.concatenate([i - j, i - j + P, i - j], axis=1)
    mult = sum(((dist >= 0) & (dist <= w) & (dist % r == 0)).astype(int) for w, r in ((128, 1), (512, 4), (2048, 16)))
    dil = np.where(mult > 0, -dist, NEG)
    swa = np.where((dist >= 0) & (dist < 128), -dist, NEG)
    causal = np.where(dist >= 0, 0, NEG)
    ang = np.arange(T)[None, :] * (10000.0 ** (-np.arange(0, ROPE, 2) / ROPE))[:, None]
    cos = np.zeros((P, T))
    sin = np.zeros((P, T))
    cos[NOPE:NOPE + ROPE] = np.concatenate([np.cos(ang), np.cos(ang)])
    sin[NOPE:NOPE + ROPE] = np.concatenate([-np.sin(ang), np.sin(ang)])
    return {
        "c_tables": np.concatenate(f32, axis=1).astype(np.float32),
        "c_masks": np.concatenate(masks, axis=1).astype(np.float16),
        "c_iota": np.tile(iota[None, :], (P, 1)).astype(np.float32),
        "c_attn": np.concatenate([dil, mult, swa, causal, cos, sin], axis=1).astype(np.float32),
    }


def stream_items():
    items = []
    for part in ("gm_v", "gm_u", "gate_a"):
        items += [(part, 0), (part, 1)]
    items += [("w_pa", 0), ("w_pa", 1)]
    for part in ("dn_q", "dn_k", "dn_v", "dn_z", "gate_b"):
        items += [(part, 0), (part, 1)]
    items += [("w_pb", 0), ("w_pb", 1), ("w_o", 0), ("w_o", 1)]
    before = len(items)
    for e in range(EXPERTS):
        items += [("w1", e), ("w3", e), ("w2", e)]
    items += [("e_in", n) for n in range(4)] + [("mla_up", 0), ("e_out", 0), ("e_out", 1)]
    items += [("ffn0", j) for j in range(FF_BLOCKS)]
    items += [("o_in", 0), ("o_in", 1), ("o_kv", 0), ("o_out", 0), ("o_out", 1)]
    items += [("ffn1", j) for j in range(FF_BLOCKS)]
    return items, before


def build(nc, io, out, phases=3):
    items, moe_first = stream_items()
    item_no = {it: n for n, it in enumerate(items)}
    with ExitStack() as ctx:
        sb = lambda name, shape, dt=F32: ctx.enter_context(nc.sbuf_tensor(name, shape, dt))
        sems = {}

        def shared(name):
            owner, _, kind = name.partition("_") if not name.startswith("ln_in") else ("ln_in", "", name[6:])
            if owner in NORMS:
                size = {"squared": lambda n: 2 if n == KD else 1, "centered": lambda n: 2, "rstd": lambda n: 1,
                        "scaled": lambda n: n, "out": lambda n: n}.get(kind)
                if size is None:
                    return name, 0
                named = [n for n in NORMS if kind not in ("centered", "out") or n in LAYER_NORMS]
                return f"norm_{kind}", sum(size(NORMS[n]) for n in named[:named.index(owner)])
            if owner in SECTIONS and kind in ("even_o", "probs", "pT", "max", "exp", "o_ready"):
                before = sum(list(SECTIONS.values())[:list(SECTIONS).index(owner)])
                return f"heads_{kind}", {"even_o": before // 2, "o_ready": before // 2, "max": 2 * before}.get(kind, before)
            return name, 0

        def S(name):
            name = shared(name)[0]
            if name not in sems:
                sems[name] = ctx.enter_context(nc.semaphore(name))
            return sems[name]

        def V(name, n):
            return S(name), shared(name)[1] + n

        ring = sb("ring", [P, SLOTS * SLOT])
        pages_at = -(-nc.sbuf_base // 32) * 32
        pages = sb("pages", [P, PAGES * PAGE])
        tables = sb("tables", [P, len(TABLES) * P])
        masks = sb("masks", [P, len(MASKS) * P], F16)
        cols = sb("cols", [P, NCOLS])
        rows = sb("rows", [P, NROWS])
        ab = sb("ab", [P, 16 * 12])
        starts = sb("starts", [1, EXPERTS + 2], I32)
        psum = ctx.enter_context(nc.psum_tensor("psum", [P, 8, BANK], F32))

        def table(name):
            n = TABLES.index(name)
            return tables[:, n * P:(n + 1) * P]

        def mask(name):
            n = MASKS.index(name)
            return masks[:, n * P:(n + 1) * P]

        def page(n, count=1):
            return pages[:, n * PAGE:(n + count) * PAGE]

        def fm(n):
            return page(n).rearrange("p (k t) -> p k t", t=T)

        def units(n):
            return page(n).rearrange("p (u t) -> p u t", t=P)

        def col(name, k=0):
            c = COLS[name] + k
            return cols[:, c:c + 1]

        def row(name, n):
            return rows[:, ROWS[name]:ROWS[name] + n]

        def slot(n, floats=SLOT):
            s = n % SLOTS
            return ring[:, s * SLOT:s * SLOT + floats]

        ident, ones = table("identity"), table("ones")
        full = [S(f"bank{b}_full") for b in range(8)]
        free = [S(f"bank{b}_free") for b in range(8)]
        landed = [S(f"slot{s}_landed") for s in range(SLOTS)]
        uses = [0] * 8
        place = {}
        released = {}

        def bank_of(name, use=0):
            return psum[:, place[name][0], :]

        def await_full(eng, name):
            b, n = place[name]
            eng.wait_ge(full[b], n)
            return psum[:, b, :]

        def empty(ins, name):
            ins.then_inc(free[place[name][0]], 1)

        def part(name, start, size):
            return nc.alloc_sbuf_tensor_at(name, [P, size], F32R, offset=pages_at + 4 * start)[:]

        x_part = {"hi": part("x_hi", 9 * PAGE, PAGE).rearrange("p (k t) -> p k t", t=T),
                  "lo": part("x_lo", PAGE, PAGE).rearrange("p (k t) -> p k t", t=T)}
        gu_size, down_size = 2 * KD * P, KD * P
        gu_part = {"hi": [part(f"gu_hi{b}", 3 * PAGE + 2 * b * gu_size, gu_size) for b in range(2)],
                   "lo": [part(f"gu_lo{b}", 3 * PAGE + (2 * b + 1) * gu_size, gu_size) for b in range(2)]}
        down_part = {"hi": [part(f"down_hi{b}", 7 * PAGE + 2 * b * down_size, down_size) for b in range(2)],
                     "lo": [part(f"down_lo{b}", 7 * PAGE + (2 * b + 1) * down_size, down_size) for b in range(2)]}
        hidden = page(11)[:, 0:3 * T].rearrange("p (r t) -> p r t", t=T)
        hidden_part = {"hi": part("hidden_hi", 2 * PAGE, 3 * T).rearrange("p (r t) -> p r t", t=T),
                       "lo": part("hidden_lo", 11 * PAGE + 3 * T, 3 * T).rearrange("p (r t) -> p r t", t=T)}
        PARTS = (("hi", "hi"), ("hi", "lo"), ("lo", "hi"))

        class LayerSteps:

            def __init__(self, layer, it=None):
                self.layer, self.it = layer, it

            def at(self, n, each):
                return n if self.it is None else self.it * each + n

            def landed(self, eng, n):
                eng.wait_ge(landed[n % SLOTS], self.at(16 * (n // SLOTS + 1), 16))

            def bank(self, eng, sem, base, j, extra):
                eng.wait_ge(sem[j % 3], self.at(base[j % 3] + j // 3 + extra, 2))

            def step(self, eng, name, j):
                eng.wait_ge(S(name), self.at(self.layer * FF_BLOCKS + j + 1, 6))

        class Steps:

            def __init__(self, eng, name):
                self.eng, self.sem, self.n, self.last = eng, S(name), 0, None
                self.counts = {}

            def do(self, ins, name=None):
                if name is None:
                    self.n += 1
                    ins.then_inc(self.sem, 1)
                    self.last = (self.sem, self.n)
                elif name in place:
                    empty(ins, name)
                    self.last = (free[place[name][0]], place[name][1])
                else:
                    own = shared(name)[0]
                    self.counts[own] = self.counts.get(own, 0) + 1
                    ins.then_inc(S(name), 1)
                    self.last = (S(name), self.counts[own])

            def settle(self):
                self.eng.wait_ge(*self.last)

        PROJ_BANKS = (0, 1, 2, 3)

        block = ctx.enter_context(nc.Block())

        @block.tensor
        def _(pe):
            turn = [0]

            def take(name, bank=None):
                if bank is None:
                    bank = PROJ_BANKS[turn[0] % len(PROJ_BANKS)]
                    turn[0] += 1
                if uses[bank]:
                    pe.wait_ge(free[bank], uses[bank])
                uses[bank] += 1
                place[name] = (bank, uses[bank])
                return psum[:, bank, :]

            def give(ins, name):
                ins.then_inc(full[place[name][0]], 1)

            def weights(item):
                n = item_no[item]
                pe.wait_ge(landed[n % SLOTS], 16 * (n // SLOTS + 1))
                return slot(n)

            def release(item, name):
                released[item_no[item]] = (full[place[name][0]], place[name][1])

            def mm(o, lhsT, rhs, start, stop):
                return pe.matmul(o, lhsT, rhs, start=start, stop=stop, skip_group_check=True)

            def project(part, rhs, item_names, first_block=0):
                for n, item in enumerate(item_names):
                    w = weights(item).rearrange("p (k c) -> p k c", k=KD)
                    for pair in range(2):
                        name = f"{part}{2 * n + pair}"
                        o = take(name)
                        for half in range(2):
                            c = (2 * pair + half) * P
                            for k in range(KD):
                                last = mm(o[:, half * T:(half + 1) * T], w[:, k, c:c + P], rhs[:, k, :],
                                          k == 0, k == KD - 1)
                        give(last, name)
                    release(item, name)

            def column_sums(name, src, nblocks, scope=None):
                o = take(name, scope)
                for k in range(nblocks):
                    last = mm(o[:, 0:T], ones, src[:, k, :], k == 0, k == nblocks - 1)
                give(last, name)

            def norm(nm, src, squares, nblocks, mean):
                if mean:
                    column_sums(f"{nm}_mu", src, nblocks)
                pe.wait_ge(*V(f"{nm}_squared", 2 if nblocks == KD else 1))
                column_sums(f"{nm}_var", squares, nblocks)

            def transposes(name, srcs, bank=None):
                o = take(name, bank)
                for j, s in enumerate(srcs):
                    last = pe.transpose(o[:, j * P:(j + 1) * P], s, ident)
                give(last, name)

            pe.wait_ge(*V("constants", 16 * 6))
            pe.wait_ge(*V("x_landed", 16))
            norm("ln_in", fm(1), fm(2), KD, True)
            h = fm(0)
            pe.wait_ge(*V("ln_in_out", KD))
            project("gm_v", h, [("gm_v", 0), ("gm_v", 1)])
            project("gm_u", h, [("gm_u", 0), ("gm_u", 1)])
            pe.wait_ge(*V("gm_v_ready", 4))
            column_sums("gm_mu", fm(2), KD)
            project("gate_a", h, [("gate_a", 0)])
            pe.wait_ge(*V("gm_squared", 2))
            column_sums("gm_var", fm(4), KD)
            w = ("gate_a", 1)
            project("gate_a_", h, [w])
            for b in range(NB):
                for half in range(2):
                    pe.wait_ge(*V("gm_out", 4 * half + 4))
                    transposes(f"gm_t{b}{half}", [fm(2)[:, 4 * half + j, b * P:(b + 1) * P] for j in range(4)])
            pe.wait_ge(*V("gate_masked", 1))
            pe.wait_ge(*V("bs_landed", 16))
            vtm = page(4).rearrange("p (b c) -> p b c", b=NB)
            wgt = page(3)[:, 0:KD * P].rearrange("p (g t) -> p g t", t=P)
            pe.wait_ge(*V("gm_vtm", 4))
            for g2 in range(KD // 2):
                o = take(f"spatial{g2}")
                for half in range(2):
                    g = 2 * g2 + half
                    for b in range(NB):
                        dst = o[:, half * T + b * P:half * T + (b + 1) * P]
                        mm(dst, vtm[:, b, g * P:(g + 1) * P], wgt[:, g, :], True, False)
                        last = mm(dst, ones[0:1, :], page(3)[0:1, KD * P + g * P:KD * P + (g + 1) * P], False, True)
                give(last, f"spatial{g2}")
            pe.wait_ge(*V("ya_ready", 4))
            project("w_pa", fm(5), [("w_pa", 0), ("w_pa", 1)])
            project("dn_q", h, [("dn_q", 0), ("dn_q", 1)])
            project("dn_k", h, [("dn_k", 0), ("dn_k", 1)])
            o = take("ab")
            wab = ab[:, 0:P].rearrange("p (k c) -> p k c", k=KD)
            for b in range(NB):
                for k in range(KD):
                    last = mm(o[:, b * 16:(b + 1) * 16], h[:, k, b * P:(b + 1) * P], wab[:, k, :], k == 0, k == KD - 1)
            give(last, "ab")
            project("dn_v", h, [("dn_v", 0), ("dn_v", 1)])
            pe.wait_ge(*V("g_ready", 1))
            g_tm = ab[:, 0:16]
            o = take("G")
            give(mm(o[:, 0:16], table("cumulate"), g_tm, True, True), "G")
            for q4 in range(4):
                o = take(f"Gb{q4}", 4 + q4)
                for j in range(4):
                    u = 4 * q4 + j
                    hd, b = u // NB, u % NB
                    c = b * HEADS + hd
                    last = mm(o[:, j * P:(j + 1) * P], g_tm[:, c:c + 1].broadcast_to([P, P]), table("cumulate"), True, True)
                give(last, f"Gb{q4}")
            for part, pg in (("q", 7), ("k", 8)):
                for q4 in range(4):
                    pe.wait_ge(*V(f"{part}_squared", q4 + 1))
                    name = f"{part}_ss{q4}"
                    o = take(name)
                    for half in range(2):
                        last = mm(o[:, half * T:(half + 1) * T], ones, fm(pg)[:, 2 * q4 + half, :], True, True)
                    give(last, name)
            project("dn_z", h, [("dn_z", 0)])
            for q4 in range(4):
                pe.wait_ge(*V("k_normed", q4 + 1))
                transposes(f"k_t{q4}", [units(3)[:, 4 * q4 + j, :] for j in range(4)])
                pe.wait_ge(*V("v_ready", 2 * q4 + 2))
                transposes(f"v_t{q4}", [units(4)[:, 4 * q4 + j, :] for j in range(4)])
            for q4 in range(4):
                name = f"kk{q4}"
                o = take(name, 4 + q4)
                for j in range(4):
                    k = units(3)[:, 4 * q4 + j, :]
                    last = mm(o[:, j * P:(j + 1) * P], k, k, True, True)
                give(last, name)
            for q4 in range(4):
                name = f"qk{q4}"
                pe.wait_ge(*V("q_normed", q4 + 1))
                o = take(name)
                for j in range(4):
                    u = 4 * q4 + j
                    last = mm(o[:, j * P:(j + 1) * P], units(3)[:, u, :], units(2)[:, u, :], True, True)
                give(last, name)
            for q4 in range(4):
                pe.wait_ge(*V("L_ready", q4 + 1))
                transposes(f"L_t{q4}", [units(11)[:, 4 * q4 + j, :] for j in range(4)], 4 + q4)
            X, XT, Y, LT = units(5), units(4), units(9), units(12)
            for lv in range(5):
                for q4 in range(4):
                    pe.wait_ge(*V("X_ready", 4 * lv + q4 + 1))
                    name = f"Y{lv}_{q4}"
                    o = take(name, 4 + q4)
                    for j in range(4):
                        u = 4 * q4 + j
                        last = mm(o[:, j * P:(j + 1) * P], LT[:, u, :], X[:, u, :], True, True)
                    give(last, name)
                for q4 in range(4):
                    pe.wait_ge(*V("Y_ready", 4 * lv + q4 + 1))
                    name = f"ZT{lv}_{q4}"
                    o = take(name, q4)
                    for j in range(4):
                        u = 4 * q4 + j
                        last = mm(o[:, j * P:(j + 1) * P], Y[:, u, :], XT[:, u, :], True, True)
                    give(last, name)
                    if lv < 4:
                        name = f"Z{lv}_{q4}"
                        o = take(name, 4 + q4)
                        for j in range(4):
                            u = 4 * q4 + j
                            last = mm(o[:, j * P:(j + 1) * P], XT[:, u, :], Y[:, u, :], True, True)
                        give(last, name)
                if lv == 1:
                    project("dn_z_", h, [("dn_z", 1)])
            pe.wait_ge(*V("XT_final", 4))
            pe.wait_ge(*V("vb_ready", 1))
            for q4 in range(4):
                name = f"uc{q4}"
                o = take(name, 4 + q4)
                for j in range(4):
                    u = 4 * q4 + j
                    last = mm(o[:, j * P:(j + 1) * P], XT[:, u, :], units(8)[:, u, :], True, True)
                give(last, name)
            pe.wait_ge(*V("kbg_ready", 1))
            for q4 in range(4):
                name = f"wc{q4}"
                o = take(name, q4)
                for j in range(4):
                    u = 4 * q4 + j
                    last = mm(o[:, j * P:(j + 1) * P], units(3)[:, u, :], XT[:, u, :], True, True)
                give(last, name)
            state = page(5)[:, 0:HEADS * P].rearrange("p (h d) -> p h d", d=P)
            vnew, wT, qd, aT, kdec = units(11), units(12), units(2), units(10), units(7)
            pe.wait_ge(*V("wc_ready", 4))
            pe.wait_ge(*V("qd_ready", 1))
            pe.wait_ge(*V("kdec_ready", 1))
            for c in range(T // CHUNK):
                b, r = c // 2, CHUNK * (c % 2)
                if c > 0:
                    pe.wait_ge(*V("state_ready", c))
                    for hh in range(2):
                        name = f"ws{c}_{hh}"
                        o = take(name, 4 + hh)
                        for j in range(4):
                            hd = 4 * hh + j
                            last = mm(o[r:r + CHUNK, j * P:(j + 1) * P], wT[:, hd * NB + b, r:r + CHUNK],
                                      state[:, hd, :], True, True)
                        give(last, name)
                pe.wait_ge(*V("vnew_ready", 2 * c + 2))
                if c < T // CHUNK - 1:
                    for hh in range(2):
                        name = f"ds{c}_{hh}"
                        o = take(name, 6 + hh)
                        for j in range(4):
                            u = (4 * hh + j) * NB + b
                            last = mm(o[:, j * P:(j + 1) * P], kdec[r:r + CHUNK, u, :], vnew[r:r + CHUNK, u, :], True, True)
                        give(last, name)
                name = f"o{c}"
                o = take(name)
                for hd in range(HEADS):
                    u = hd * NB + b
                    dst = o[:, hd * CHUNK:(hd + 1) * CHUNK]
                    if c > 0:
                        mm(dst, state[:, hd, :], qd[:, u, r:r + CHUNK], True, False)
                    last = mm(dst, vnew[r:r + CHUNK, u, :], aT[r:r + CHUNK, u, r:r + CHUNK], c == 0, True)
                give(last, name)
                if c in (0, 1):
                    project(f"gate_b{'_' * c}", h, [("gate_b", c)])
            for q4 in range(4):
                pe.wait_ge(*V("o_squared", q4 + 1))
                name = f"o_ss{q4}"
                o = take(name)
                for half in range(2):
                    last = mm(o[:, half * T:(half + 1) * T], ones, fm(3)[:, 2 * q4 + half, :], True, True)
                give(last, name)
            pe.wait_ge(*V("yb_ready", KD))
            project("w_pb", fm(4), [("w_pb", 0), ("w_pb", 1)])
            pe.wait_ge(*V("merged", 4))
            project("w_o", fm(1), [("w_o", 0), ("w_o", 1)])
            pe.wait_ge(*V("res1", 4))
            norm("ln1", fm(0), fm(2), KD, True)
            if phases < 2:
                return

            pe.wait_ge(*V("ln1_out", KD))
            pe.wait_ge(*V("router_landed", 32))
            h = fm(0)
            wr = page(10)[:, 0:KD * 36].rearrange("p (k c) -> p k c", k=KD)
            o = take("router")
            for b in range(NB):
                for k in range(KD):
                    last = mm(o[:, b * 36:(b + 1) * 36], h[:, k, b * P:(b + 1) * P], wr[:, k, :], k == 0, k == KD - 1)
            give(last, "router")
            for b in range(NB):
                for half in range(2):
                    transposes(f"h_t{b}{half}", [h[:, 4 * half + j, b * P:(b + 1) * P] for j in range(4)])
            pick = page(11)[:, 512:576].rearrange("p (b e) -> p b e", b=NB)
            pe.wait_ge(*V("picked", 1))
            o = take("rank")
            mm(o[:, 0:32], table("before"), pick[:, 0, :], True, True)
            mm(o[:, 32:64], ones, pick[:, 0, :], True, False)
            mm(o[:, 32:64], table("before"), pick[:, 1, :], False, True)
            mm(o[:, 64:96], ones, pick[:, 0, :], True, False)
            mm(o[:, 64:96], ones, pick[:, 1, :], False, True)
            mm(o[0:EXPERTS, 96:97], pick[:, 0, :], ones[:, 0:1], True, False)
            give(mm(o[0:EXPERTS, 96:97], pick[:, 1, :], ones[:, 0:1], False, True), "rank")
            pe.wait_ge(*V("counts_spread", 1))
            o = take("start")
            give(mm(o[:, 0:EXPERTS], page(11)[0:EXPERTS, 640:640 + P], table("before")[0:EXPERTS, 0:EXPERTS], True, True), "start")
            onehot = page(8)[:, 0:NB * ASSIGN].rearrange("p (b s) -> p b s", b=NB)
            gated = page(8)[:, NB * ASSIGN:2 * NB * ASSIGN].rearrange("p (b s) -> p b s", b=NB)
            htm = page(1).rearrange("p (b c) -> p b c", b=NB)
            pe.wait_ge(*V("htm_ready", 4))
            pe.wait_ge(*V("onehot_ready", NB))
            for k in range(KD):
                name = f"xs{k}"
                o = take(name)
                for b in range(NB):
                    last = mm(o, htm[:, b, k * P:(k + 1) * P], onehot[:, b, :], b == 0, b == NB - 1)
                give(last, name)
            pe.wait_ge(*V("gated_ready", NB))
            for b in range(NB):
                transposes(f"gt{b}", [gated[:, b, s * P:(s + 1) * P] for s in range(4)])

            xe = page(9)[:, 1024:2048].rearrange("p (r k s) -> p r k s", r=2, k=KD)
            act = page(10)[:, 1536:2048].rearrange("p (r s) -> p r s", r=2)
            actT = page(8)[:, 1024:1536].rearrange("p (r s) -> p r s", r=2)
            yrow = page(8)[:, 0:1024].rearrange("p (r s) -> p r s", r=2)

            def expert_h(r, w, half):
                w = w.rearrange("p (k c) -> p k c", k=KD)
                for k in range(KD):
                    for g in range(2):
                        last = mm(psum[g * CAP:(g + 1) * CAP, r, half * T:(half + 1) * T], xe[:, r, k, :],
                                  w[:, k, g * T:(g + 1) * T], k == 0, k == KD - 1)
                return last

            def expert_t(r):
                for c in range(2):
                    last = pe.transpose(psum[:, 2 + r, c * P:(c + 1) * P], act[:, r, c * P:(c + 1) * P], ident)
                return last

            def expert_y(r, w2):
                w = w2.rearrange("p (f c) -> p f c", c=D)
                for f in range(FE // P):
                    for g in range(2):
                        a = (f % 2) * P + (f // 2) * CAP
                        last = mm(psum[g * CAP:(g + 1) * CAP, 4 + r, :], actT[:, r, a:a + CAP],
                                  w[:, f, g * 512:(g + 1) * 512], f == 0, f == FE // P - 1)
                return last

            def expert_z(r):
                for c in range(4):
                    last = pe.transpose(psum[:, 6 + r, c * P:(c + 1) * P], yrow[:, r, c * P:(c + 1) * P], ident)
                return last

            pe.wait_ge(*V("starts_ready", 1))
            base = list(uses)
            place["moe_base"] = tuple(base)
            with pe.Fori(0, EXPERTS // 2) as it:
                land = lambda n: pe.wait_ge(landed[n % SLOTS], it * 16 + 16 * (n // SLOTS + 1))
                for r in range(2):
                    n = moe_first + 3 * r
                    pe.wait_ge(free[r], it + base[r])
                    pe.wait_ge(*V("xe_ready", it * 2 + r + 1))
                    land(n)
                    expert_h(r, slot(n), 0).then_inc(S("w1_read"), 1)
                    land(n + 1)
                    expert_h(r, slot(n + 1), 1).then_inc(full[r], 1)
                for r in range(2):
                    pe.wait_ge(free[2 + r], it + base[2 + r])
                    pe.wait_ge(free[r], it + base[r] + 1)
                    expert_t(r).then_inc(full[2 + r], 1)
                for r in range(2):
                    pe.wait_ge(free[4 + r], it + base[4 + r])
                    pe.wait_ge(free[2 + r], it + base[2 + r] + 1)
                    land(moe_first + 3 * r + 2)
                    expert_y(r, slot(moe_first + 3 * r + 2)).then_inc(full[4 + r], 1)
                for r in range(2):
                    pe.wait_ge(free[6 + r], it + base[6 + r])
                    pe.wait_ge(free[4 + r], it + base[4 + r] + 1)
                    expert_z(r).then_inc(full[6 + r], 1)
            for b in range(8):
                uses[b] += EXPERTS // 2
            for r in range(2):
                n = moe_first + 3 * (EXPERTS - 2 + r)
                released[n] = (S("w1_read"), EXPERTS - 1 + r)
                released[n + 1] = (full[r], uses[r])
                released[n + 2] = (full[4 + r], uses[4 + r])
            most = pe.value_load(starts[0:1, EXPERTS:EXPERTS + 1], min_val=0, max_val=T)
            for b in range(8):
                pe.wait_ge(free[b], uses[b])
            with pe.If(most > CAP):
                pe.sem_inc(S("more_y"), 1)
                with pe.Fori(0, EXPERTS) as e:
                    pe.wait_ge(*V("more_landed", e * 48 + 48))
                    for c in range(MAX_PASSES):
                        n = e * MAX_PASSES + c + 1
                        pe.wait_ge(*V("more_xe", n))
                        expert_h(0, slot(0), 0)
                        expert_h(0, slot(1), 1).then_inc(S("more_h"), 1)
                        pe.wait_ge(*V("more_act", n))
                        expert_t(0).then_inc(S("more_t"), 1)
                        pe.wait_ge(*V("more_actT", n))
                        expert_y(0, slot(2)).then_inc(S("more_y"), 1)
                        pe.wait_ge(*V("more_yrow", n))
                        pe.wait_ge(*V("more_out", n))
                        expert_z(0).then_inc(S("more_z"), 1)
            ys = page(5, 3).rearrange("p (k s) -> p k s", k=KD)
            pe.wait_ge(*V("experts_done", 1))
            for s in range(4):
                for half in range(2):
                    transposes(f"y_t{s}{half}", [ys[:, 4 * half + j, s * P:(s + 1) * P] for j in range(4)])
            ytm = page(11, 2).rearrange("p (s c) -> p s c", s=4)
            gt = page(9)[:, 0:4 * T].rearrange("p (s t) -> p s t", t=T)
            pe.wait_ge(*V("ytm_ready", 8))
            pe.wait_ge(*V("gt_ready", 2))
            for m in range(4):
                name = f"moe{m}"
                o = take(name)
                for half in range(2):
                    k = 2 * m + half
                    for s in range(4):
                        last = mm(o[:, half * T:(half + 1) * T], ytm[:, s, k * P:(k + 1) * P], gt[:, s, :], s == 0, s == 3)
                give(last, name)
            pe.wait_ge(*V("res2", 4))
            norm("ln2", fm(0), fm(2), KD, True)
            if phases < 3:
                return

            def rms(nm, src, squares, nblocks=KD):
                norm(nm, src, squares, nblocks, False)

            def score(name, pairs):
                o = take(name)
                q, k = pairs
                mm(o[:, 0:P], q[:, 0:P], k[:, 0:P], True, True)
                give(mm(o[:, P:SPAN], q[:, P:T], k, True, True), name)

            def attend(sec, nheads, operands, values):
                e = lambda g: page(6)[:, (g % 3) * SPAN:(g % 3 + 1) * SPAN]
                pT = lambda g: page(7)[:, (g % 2) * SPAN:(g % 2 + 1) * SPAN]
                for i in range(nheads + 2):
                    if i < nheads:
                        score(f"{sec}s{i}", operands(i))
                    if 1 <= i <= nheads:
                        g = i - 1
                        pe.wait_ge(*V(f"{sec}_probs", g + 1))
                        transposes(f"{sec}t{g}", [e(g)[:, j * P:(j + 1) * P] for j in range(3)], 4 + g % 2)
                    if i >= 2:
                        g = i - 2
                        r = VDIM * (g % 2)
                        pe.wait_ge(*V(f"{sec}_pT", g + 1))
                        name = f"{sec}o{g // 2}"
                        o = take(name, 6 + g // 2 % 2) if g % 2 == 0 else bank_of(name)
                        dst = o[r:r + VDIM, :]
                        mm(dst[:, 0:P], values(g, 0), pT(g)[:, 0:P], True, True)
                        mm(dst[:, P:T], values(g, 0), pT(g)[:, P:2 * P], True, False)
                        last = mm(dst[:, P:T], values(g, 1), pT(g)[:, 2 * P:3 * P], False, True)
                        if g % 2:
                            give(last, name)
                        else:
                            last.then_inc(S(f"{sec}_even_o"), 1)

            def ffn(nm, layer):
                first = item_no[(nm, 0)]
                base = list(uses)
                for b in range(3):
                    if base[b]:
                        pe.wait_ge(free[b], base[b])
                place[nm] = tuple(base)

                def gate_up(j, steps):
                    steps.step(pe, "gu_split", j)
                    if j:
                        steps.bank(pe, free, base, j, 0)
                    w = {p_: gu_part[p_][j % 2].rearrange("p (k c) -> p k c", k=KD) for p_ in ("hi", "lo")}
                    for half in range(2):
                        for k in range(KD):
                            for n, (wp, xp) in enumerate(PARTS):
                                last = mm(psum[:, j % 3, half * T:(half + 1) * T], w[wp][:, k, half * P:(half + 1) * P],
                                          x_part[xp][:, k, :], k == 0 and n == 0, k == KD - 1 and n == 2)
                    last.then_inc(full[j % 3], 1)

                def down(j, steps):
                    steps.step(pe, "hidden_split", j)
                    steps.step(pe, "down_split", j)
                    end = j == FF_BLOCKS - 1
                    for m in range(KD):
                        for n, (wp, xp) in enumerate(PARTS):
                            last = mm(psum[:, 4 + m // 2, (m % 2) * T:(m % 2 + 1) * T],
                                      down_part[wp][j % 2][:, m * P:(m + 1) * P], hidden_part[xp][:, j % 3, :],
                                      False, end and n == 2)
                        if end and m % 2:
                            last.then_inc(full[4 + m // 2], 1)
                    if not end:
                        last.then_inc(S(f"{nm}_down"), 1)

                pe.wait_ge(S("x_split"), layer + 1)
                gate_up(0, LayerSteps(layer))
                with pe.Fori(0, 3) as it:
                    for j in range(1, 7):
                        gate_up(j, LayerSteps(layer, it))
                        down(j - 1, LayerSteps(layer, it))
                for j in range(19, FF_BLOCKS):
                    gate_up(j, LayerSteps(layer))
                    down(j - 1, LayerSteps(layer))
                down(FF_BLOCKS - 1, LayerSteps(layer))
                for b in range(3):
                    uses[b] += (FF_BLOCKS - b + 2) // 3
                for b in range(4, 8):
                    uses[b] += 1
                for j in range(FF_BLOCKS):
                    released[first + j] = (S("down_split"), layer * FF_BLOCKS + j + 1)

            def clear_sums(nth):
                for b in range(4, 8):
                    if uses[b]:
                        pe.wait_ge(free[b], uses[b])
                pe.wait_ge(*V("zeros_ready", nth))
                for b in range(4, 8):
                    mm(psum[:, b, :], page(2)[:, 768:768 + P], page(2)[:, 768:768 + BANK], True, False)

            rms("att0", fm(0), fm(11))
            pe.wait_ge(*V("att0_scaled", KD))
            hn = fm(1)
            w = weights(("e_in", 0))[:, 0:KD * 448].rearrange("p (k c) -> p k c", k=KD)
            for nm_, c0, c1, r in (("cq", 0, 256, 0), ("ckv", 256, 384, 0), ("kr", 384, 448, NOPE)):
                o = take(nm_)
                if nm_ == "kr":
                    for half in range(2):
                        for k in range(KD):
                            c = c0 + half * ROPE
                            last = mm(o[r:r + ROPE, half * T:(half + 1) * T], w[:, k, c:c + ROPE], hn[:, k, :],
                                      k == 0, k == KD - 1)
                else:
                    for half in range((c1 - c0) // P):
                        for k in range(KD):
                            last = mm(o[:, half * T:(half + 1) * T], w[:, k, c0 + half * P:c0 + (half + 1) * P],
                                      hn[:, k, :], k == 0, k == KD - 1)
                give(last, nm_)
            release(("e_in", 0), "kr")
            project("qB", hn, [("e_in", 1)])
            project("kB", hn, [("e_in", 2)])
            rms("cqn", page(9)[:, 0:512].rearrange("p (k t) -> p k t", t=T),
                page(11)[:, 0:512].rearrange("p (k t) -> p k t", t=T), 2)
            rms("ckvn", page(9)[:, 512:768].rearrange("p (k t) -> p k t", t=T),
                page(11)[:, 512:768].rearrange("p (k t) -> p k t", t=T), 1)
            w = weights(("e_in", 3)).rearrange("p (k c) -> p k c", k=KD)
            for b in range(NB):
                o = take(f"vB{b}")
                for k in range(KD):
                    last = mm(o, hn[:, k, b * P:(b + 1) * P], w[:, k, :], k == 0, k == KD - 1)
                give(last, f"vB{b}")
            release(("e_in", 3), "vB1")
            w = weights(("mla_up", 0))
            wq = w[:, 0:2 * D].rearrange("p (k c) -> p k c", k=2)
            wkv = w[:, 2 * D:3 * D]
            cq = page(9)[:, 768:1280].rearrange("p (k t) -> p k t", t=T)
            ckv = page(9)[:, 1280:1536]
            pe.wait_ge(*V("cqn_scaled", 2))
            for hd in range(HEADS):
                name = f"qA{hd}"
                o = take(name)
                for k in range(2):
                    mm(o[0:NOPE + ROPE, 0:T], wq[:, k, hd * 96:(hd + 1) * 96], cq[:, k, :], k == 0, k == 1)
                for k in range(2):
                    c = 768 + hd * ROPE
                    last = mm(o[NOPE:NOPE + ROPE, T:2 * T], wq[:, k, c:c + ROPE], cq[:, k, :], k == 0, k == 1)
                give(last, name)
            pe.wait_ge(*V("ckvn_scaled", 1))
            for h2 in range(HEADS // 2):
                name = f"kA{h2}"
                o = take(name)
                for half in range(2):
                    c = (2 * h2 + half) * NOPE
                    last = mm(o[0:NOPE, half * T:(half + 1) * T], wkv[:, c:c + NOPE], ckv, True, True)
                give(last, name)
            for b in range(NB):
                o = take(f"vA{b}")
                last = mm(o, ckv[:, b * P:(b + 1) * P], wkv[:, 512:D], True, True)
                give(last, f"vA{b}")
            release(("mla_up", 0), "vA1")
            qA, kA = fm(2), fm(3)
            vA = page(4)[:, 0:D].rearrange("p (b c) -> p b c", b=NB)
            vB = page(4)[:, D:2 * D].rearrange("p (b c) -> p b c", b=NB)
            qB = page(5)[:, 0:D].rearrange("p (k t) -> p k t", t=T)
            kB = page(5)[:, D:2 * D].rearrange("p (k t) -> p k t", t=T)
            pe.wait_ge(*V("qA_ready", HEADS))
            pe.wait_ge(*V("kA_ready", 5))
            pe.wait_ge(*V("vA_ready", NB))
            attend("mla", HEADS, lambda i: (qA[0:96, i, :], kA[0:96, i, :]),
                   lambda g, b: vA[:, b, g * VDIM:(g + 1) * VDIM])
            pe.wait_ge(*V("qkB_ready", 4))
            pe.wait_ge(*V("vB_ready", NB))
            half_of = lambda i: slice(VDIM * (i % 2), VDIM * (i % 2) + VDIM)
            attend("dil", HEADS, lambda i: (qB[half_of(i), i // 2, :], kB[half_of(i), i // 2, :]),
                   lambda g, b: vB[:, b, g * VDIM:(g + 1) * VDIM])
            pe.wait_ge(*V("mla_o_ready", 4))
            pe.wait_ge(*V("dil_o_ready", 4))
            project("e_out", fm(8), [("e_out", 0), ("e_out", 1)])
            pe.wait_ge(*V("res3", 4))
            rms("ffn0n", fm(0), fm(11))
            clear_sums(1)
            ffn("ffn0", 0)
            pe.wait_ge(*V("res4", 4))
            rms("att1", fm(0), fm(11))
            pe.wait_ge(*V("att1_scaled", KD))
            project("qS", hn, [("o_in", 0), ("o_in", 1)])
            w = weights(("o_kv", 0))[:, 0:KD * T].rearrange("p (k c) -> p k c", k=KD)
            o = take("kS")
            for k in range(KD):
                last = mm(o[:, 0:T], w[:, k, 0:P], hn[:, k, :], k == 0, k == KD - 1)
            give(last, "kS")
            o = take("vS")
            for b in range(NB):
                for k in range(KD):
                    last = mm(o[:, b * P:(b + 1) * P], hn[:, k, b * P:(b + 1) * P], w[:, k, P:2 * P], k == 0, k == KD - 1)
            give(last, "vS")
            release(("o_kv", 0), "vS")
            qS, kS = fm(2), page(3)[:, 0:T]
            vS = page(4)[:, 0:T].rearrange("p (b c) -> p b c", b=NB)
            pe.wait_ge(*V("qS_ready", 4))
            pe.wait_ge(*V("kvS_ready", 2))
            attend("swa", SWA_HEADS, lambda i: (qS[half_of(i), i // 2, :], kS[half_of(i), :]),
                   lambda g, b: vS[:, b, half_of(g)])
            pe.wait_ge(*V("swa_o_ready", 8))
            project("o_out", fm(8), [("o_out", 0), ("o_out", 1)])
            pe.wait_ge(*V("res5", 4))
            rms("ffn1n", fm(0), fm(11))
            clear_sums(2)
            ffn("ffn1", 1)
            pe.wait_ge(*V("res6", 4))
            rms("final", fm(0), fm(11))

        @block.scalar
        def _(act_e):
            st = Steps(act_e, "act_step")

            tables_at = [None]

            def use_tables(name):
                if tables_at[0] != name:
                    tables_at[0] = name
                    if name == "ln_exp":
                        act_e.preload_act_table_set("natural_log_exp_and_others")
                    else:
                        act_e.preload_act_table(name)

            def act(o, i, func, name=None, **kw):
                if func in (ACT.Ln, ACT.Exp):
                    use_tables("ln_exp")
                elif func in (ACT.Silu, ACT.Gelu, ACT.Sigmoid):
                    use_tables(func)
                st.do(act_e.activation(o, i, func, **kw), name)

            def norm(nm, src, squares, small, nblocks, width, eps, dst=None, bias=None, between=None):
                nh = 2 if nblocks == KD else 1
                for i in range(nh):
                    if bias is not None:
                        act_e.wait_ge(*V(f"{nm}_centered", i + 1))
                    sl = slice(i * nblocks // nh, (i + 1) * nblocks // nh)
                    act(squares[:, sl, :], src[:, sl, :], ACT.Square, f"{nm}_squared")
                use_tables("ln_exp")
                if between:
                    between()
                v = await_full(act_e, f"{nm}_var")
                act(small, v[:, 0:T], ACT.Ln, f"{nm}_var", scale=1.0 / width, bias=col(eps))
                st.settle()
                act(small, small, ACT.Exp, f"{nm}_rstd", scale=-0.5)
                if bias is not None:
                    add_bias(nm, dst, bias)

            def add_bias(nm, dst, bias):
                for k in range(KD):
                    act_e.wait_ge(*V(f"{nm}_scaled", k + 1))
                    act(dst[:, k, :], dst[:, k, :], ACT.Identity, f"{nm}_out", bias=col(bias, k))

            def evacuate(part, npairs, dst, func, bias, done, first=0):
                for n in range(npairs):
                    v = await_full(act_e, f"{part}{n}")
                    k = first + 2 * n
                    act(dst[:, k, :], v[:, 0:T], func, bias=col("b_in", bias + k))
                    act(dst[:, k + 1, :], v[:, T:2 * T], func, f"{part}{n}", bias=col("b_in", bias + k + 1))

            for dst, src in ((tables[:], io["c_tables"]), (masks[:], io["c_masks"]), (cols[:], io["cols"]),
                             (rows[:], io["rows"][0:1, :].partition_broadcast(P)),
                             (ab[:, 0:P].rearrange("p (k c) -> p k c", k=KD), io["w_ab"].rearrange("(k p) c -> p k c", p=P)),
                             (page(3)[:, 0:KD * P].rearrange("p (g t) -> p g t", t=P), io["w_s"].rearrange("g s t -> s g t"))):
                act_e.dma_start(dst, src).then_inc(S("constants"), 16)
            act_e.dma_start(page(3)[0:1, KD * P:2 * KD * P], io["b_s"]).then_inc(S("bs_landed"), 16)
            act_e.wait_ge(*V("constants", 16 * 6))
            norm("ln_in", fm(0), fm(2), page(4)[:, 512:768], KD, D, "eps5", fm(0), "ln_in_b")
            evacuate("gm_v", 4, fm(2), ACT.Gelu, 8, None)
            act_e.wait_ge(*V("ln_in_out", KD))
            for n in range(4):
                v = await_full(act_e, f"gm_u{n}")
                for half in range(2):
                    act(fm(5)[:, 2 * n + half, :], v[:, half * T:(half + 1) * T], ACT.Gelu,
                        f"gm_u{n}" if half else None, bias=col("b_in", 2 * n + half))
            for i in range(2):
                act_e.wait_ge(*V("gm_centered", i + 1))
                act(fm(4)[:, 4 * i:4 * i + 4, :], fm(2)[:, 4 * i:4 * i + 4, :], ACT.Square, "gm_squared")
            evacuate("gate_a", 2, fm(6), ACT.Sigmoid, 48, None)
            v = await_full(act_e, "gm_var")
            act(page(7)[:, 256:512], v[:, 0:T], ACT.Ln, "gm_var", scale=1.0 / D, bias=col("eps5"))
            st.settle()
            act(page(7)[:, 256:512], page(7)[:, 256:512], ACT.Exp, "gm_rstd", scale=-0.5)
            add_bias("gm", fm(2), "gm_b")
            evacuate("gate_a_", 2, fm(6), ACT.Sigmoid, 48, None, first=4)
            stage = lambda n: page(5)[:, n % 6 * 260:n % 6 * 260 + 260]
            for part, pg, base in (("dn_q", 2, 0), ("dn_k", 3, 8), ("dn_v", 4, 16)):
                if part == "dn_q":
                    act_e.wait_ge(*V("stage_zero", 6))
                for n in range(4):
                    v = await_full(act_e, f"{part}{n}")
                    for half in range(2):
                        blk = base + 2 * n + half
                        if blk >= 6:
                            act_e.wait_ge(*V("conv_done", blk - 5))
                        act(stage(blk)[:, 4:260], v[:, half * T:(half + 1) * T], ACT.Identity, "staged",
                            bias=col("b_in", 16 + blk))
                    act_e.wait_ge(*V("staged", blk + 1))
                    act_e.sem_inc(free[place[f"{part}{n}"][0]], 1)
                    for b2 in (blk - 3, blk - 2):
                        if b2 >= 0:
                            silu_block(act_e, act, S, fm, b2)
                if part == "dn_k":
                    v = await_full(act_e, "ab")
            for b2 in (22, 23):
                silu_block(act_e, act, S, fm, b2)
            for part, pg, src in (("q", 7, 2), ("k", 8, 3)):
                for q4 in range(4):
                    act(fm(pg)[:, 2 * q4:2 * q4 + 2, :], fm(src)[:, 2 * q4:2 * q4 + 2, :], ACT.Square, f"{part}_squared")
            act_e.wait_ge(*V("ab_ready", 1))
            act(ab[:, 32:48], ab[:, 32:48], ACT.Exp, scale=-1.0)
            act(ab[:, 48:64], ab[:, 48:64], ACT.Exp, scale=-1.0)
            act(ab[:, 64:72], row("a_log", 8), ACT.Exp)
            st.settle()
            act(ab[:, 48:64], ab[:, 48:64], ACT.Ln, "ab_exps", bias=1.0)
            for q4 in range(4):
                v = await_full(act_e, f"Gb{q4}")
                act(page(9)[:, q4 * BANK:(q4 + 1) * BANK], v, ACT.Exp, "expG_row")
            act_e.wait_ge(*V("G_small", 1))
            act(ab[:, 96:128], ab[:, 96:128], ACT.Exp, "expG_col")
            act_e.wait_ge(*V("decay_clipped", 1))
            act(page(10, 2), page(10, 2), ACT.Exp, "decay_ready")
            for part, pg in (("q", 7), ("k", 8)):
                for q4 in range(4):
                    v = await_full(act_e, f"{part}_ss{q4}")
                    dst = page(pg)[:, q4 * BANK:(q4 + 1) * BANK]
                    act(dst, v, ACT.Ln, f"{part}_ss{q4}", bias=col("eps6"))
                    st.settle()
                    if part == "q":
                        act(dst, dst, ACT.Exp, "q_inv", scale=-0.5, bias=col("qscale"))
                    else:
                        act(dst, dst, ACT.Exp, "k_inv", scale=-0.5)
            for n in range(2):
                v = await_full(act_e, f"dn_z{n}")
                for half in range(2):
                    k = 2 * n + half
                    act(fm(6)[:, k, :], v[:, half * T:(half + 1) * T], ACT.Silu, f"dn_z{n}" if half else None,
                        bias=col("b_in", 40 + k))
            for q4 in range(4):
                act_e.wait_ge(*V("k_normed", 4))
                v = await_full(act_e, f"k_t{q4}")
                act(page(7)[:, q4 * BANK:(q4 + 1) * BANK], v, ACT.Copy, f"k_t{q4}")
                v = await_full(act_e, f"v_t{q4}")
                act(page(8)[:, q4 * BANK:(q4 + 1) * BANK], v, ACT.Copy, f"v_t{q4}")
            act_e.wait_ge(*st.last)
            act_e.sem_inc(S("tm_ready"), 1)
            for q4 in range(4):
                v = await_full(act_e, f"L_t{q4}")
                act(page(12)[:, q4 * BANK:(q4 + 1) * BANK], v, ACT.Copy, "LT_ready")
            for n in range(2):
                v = await_full(act_e, f"dn_z_{n}")
                for half in range(2):
                    k = 4 + 2 * n + half
                    act(fm(6)[:, k, :], v[:, half * T:(half + 1) * T], ACT.Silu, f"dn_z_{n}" if half else None,
                        bias=col("b_in", 40 + k))
            act_e.wait_ge(*st.last)
            act_e.sem_inc(S("z_ready"), 1)
            for q4 in range(4):
                v = await_full(act_e, f"wc{q4}")
                act(page(12)[:, q4 * BANK:(q4 + 1) * BANK], v, ACT.Copy, "wc_evac")
            act_e.wait_ge(*V("wc_evac", 4))
            for q4 in range(4):
                act_e.sem_inc(free[place[f"wc{q4}"][0]], 1)
                act_e.sem_inc(S("wc_ready"), 1)
            oT = fm(4)
            for c in range(T // CHUNK):
                v = await_full(act_e, f"o{c}")
                act(oT[:, :, c * CHUNK:(c + 1) * CHUNK], v.rearrange("p (h t) -> p h t", h=HEADS), ACT.Copy, f"o{c}")
                if c in (0, 1):
                    part = "gate_b" + "_" * c
                    for n in range(2):
                        v = await_full(act_e, f"{part}{n}")
                        for half in range(2):
                            k = 4 * c + 2 * n + half
                            act(fm(9)[:, k, :], v[:, half * T:(half + 1) * T], ACT.Sigmoid,
                                f"{part}{n}" if half else None, bias=col("b_in", 56 + k))
            st.settle()
            for q4 in range(4):
                act(fm(3)[:, 2 * q4:2 * q4 + 2, :], oT[:, 2 * q4:2 * q4 + 2, :], ACT.Square, "o_squared")
            for q4 in range(4):
                v = await_full(act_e, f"o_ss{q4}")
                dst = page(7)[:, q4 * BANK:(q4 + 1) * BANK]
                act(dst, v, ACT.Ln, f"o_ss{q4}", scale=1.0 / P, bias=col("eps6"))
                st.settle()
                act(dst, dst, ACT.Exp, "o_inv", scale=-0.5)
            if phases >= 2:
                act_e.dma_start(page(10)[:, 0:KD * 36].rearrange("p (k c) -> p k c", k=KD),
                                io["w_router"].rearrange("(k p) c -> p k c", p=P)).then_inc(S("router_landed"), 16)
                act_e.dma_start(page(10)[:, KD * 36:N_ROUTER], io["c_iota"]).then_inc(S("router_landed"), 16)
            norm("ln1", fm(0), fm(2), page(12)[:, 256:512], KD, D, "eps5", fm(0), "ln1_b")
            if phases < 2:
                return

            for b in range(NB):
                for half in range(2):
                    v = await_full(act_e, f"h_t{b}{half}")
                    act(page(1)[:, b * D + half * 512:b * D + (half + 1) * 512], v, ACT.Copy, "htm_evac")
                    act_e.wait_ge(*V("htm_evac", 2 * b + half + 1))
                    act_e.sem_inc(free[place[f"h_t{b}{half}"][0]], 1)
                    act_e.sem_inc(S("htm_ready"), 1)
            act_e.wait_ge(*V("group_centered", 1))
            act(page(11)[:, 80:96].rearrange("p (b g) -> p b g", b=NB)[:, :, 0:GROUPS],
                page(11)[:, 80:96].rearrange("p (b g) -> p b g", b=NB)[:, :, 0:GROUPS], ACT.Exp, "group_exp")
            act_e.wait_ge(*V("top_diff", 1))
            act(page(11)[:, 240:242], page(11)[:, 240:242], ACT.Exp, "top_exp")
            for k in range(KD):
                if k % 2 == 0:
                    v = await_full(act_e, f"xs{k}")
                    act(page(2, 3).rearrange("p (k s) -> p k s", k=KD)[:, k, 0:ASSIGN], v, ACT.Copy, f"xs{k}")
            act_e.wait_ge(*st.last)
            act_e.wait_ge(*V("xs_odd", 4))
            act_e.sem_inc(S("xs_ready"), KD)
            for b in range(NB):
                v = await_full(act_e, f"gt{b}")
                act(page(9)[:, 0:4 * T].rearrange("p (s t) -> p s t", t=T)[:, :, b * P:(b + 1) * P],
                    v.rearrange("p (s t) -> p s t", s=4), ACT.Copy, f"gt{b}")
            act_e.wait_ge(*st.last)
            act_e.sem_inc(S("gt_ready"), 2)
            silu = page(10)[:, 1024:1536].rearrange("p (r s) -> p r s", r=2)
            base = place["moe_base"]
            actT = page(8)[:, 1024:1536].rearrange("p (r s) -> p r s", r=2)
            yrow = page(8)[:, 0:1024].rearrange("p (r s) -> p r s", r=2)
            use_tables(ACT.Silu)
            with act_e.Fori(0, EXPERTS // 2) as it:
                for r in range(2):
                    act_e.wait_ge(full[r], it + base[r] + 1)
                    act_e.wait_ge(free[r], it + base[r])
                    act_e.activation(silu[:, r, :], psum[:, r, 0:T], ACT.Silu).then_inc(S("silu_ready"), 1)
                for r in range(2):
                    act_e.wait_ge(full[2 + r], it + base[2 + r] + 1)
                    act_e.wait_ge(full[4 + r], it + base[4 + r])
                    act_e.activation(actT[:, r, :], psum[:, 2 + r, 0:T], ACT.Copy).then_inc(free[2 + r], 1)
                for r in range(2):
                    act_e.wait_ge(full[4 + r], it + base[4 + r] + 1)
                    act_e.wait_ge(full[6 + r], it + base[6 + r])
                    act_e.activation(yrow[:, r, :], psum[:, 4 + r, :], ACT.Copy).then_inc(free[4 + r], 1)
            tables_at[0] = None
            most = act_e.value_load(starts[0:1, EXPERTS:EXPERTS + 1], min_val=0, max_val=T)
            act_e.wait_ge(full[7], base[7] + EXPERTS // 2)
            with act_e.If(most > CAP):
                with act_e.Fori(0, EXPERTS) as e:
                    for c in range(MAX_PASSES):
                        n = e * MAX_PASSES + c + 1
                        act_e.wait_ge(*V("more_h", n + 1))
                        act_e.activation(silu[:, 0, :], psum[:, 0, 0:T], ACT.Silu).then_inc(S("more_silu"), 1)
                        act_e.wait_ge(*V("more_t", n))
                        act_e.activation(actT[:, 0, :], psum[:, 2, 0:T], ACT.Copy).then_inc(S("more_actT"), 1)
                        act_e.wait_ge(*V("more_y", n + 1))
                        act_e.activation(yrow[:, 0, :], psum[:, 4, :], ACT.Copy).then_inc(S("more_yrow"), 1)
            if phases >= 3:
                act_e.wait_ge(*V("experts_done", 1))
                act_e.dma_start(page(10), io["c_attn"]).then_inc(S("attn_tables"), 16)
            for s in range(4):
                for half in range(2):
                    v = await_full(act_e, f"y_t{s}{half}")
                    if half == 0:
                        act(page(11, 2)[:, s * D:s * D + 512], v, ACT.Copy, f"y_t{s}{half}")
            act_e.wait_ge(*st.last)
            act_e.wait_ge(*V("ytm_odd", 4))
            act_e.sem_inc(S("ytm_ready"), 8)
            norm("ln2", fm(0), fm(2), page(12)[:, 256:512], KD, D, "eps5", fm(0), "ln2_b")
            if phases < 3:
                return

            def rms(nm, src, squares, small, nblocks, width, before=None, between=None):
                if before:
                    act_e.wait_ge(*before)
                norm(nm, src, squares, small, nblocks, width, "eps6", between=between)

            def attend(sec, nheads, sink=False):
                stats = page(7)[:, 1024:1024 + 64]
                e = lambda g: page(6)[:, (g % 3) * SPAN:(g % 3 + 1) * SPAN]
                pT = lambda g: page(7)[:, (g % 2) * SPAN:(g % 2 + 1) * SPAN]
                for i in range(nheads + 1):
                    if i < nheads:
                        g = i
                        negm = stats[:, (g % 3) * 8:(g % 3) * 8 + 2]
                        z = stats[:, (g % 3) * 8 + 2:(g % 3) * 8 + 4]
                        act_e.wait_ge(*V(f"{sec}_max", 2 * g + 2))
                        if sec == "dil":
                            act(e(g)[:, 0:P], e(g)[:, 0:P], ACT.Exp, bias=negm[:, 0:1])
                            act(e(g)[:, P:SPAN], e(g)[:, P:SPAN], ACT.Exp, f"{sec}_exp", bias=negm[:, 1:2])
                        else:
                            act(e(g)[:, 0:P], e(g)[:, 0:P], ACT.Exp, bias=negm[:, 0:1], accum_out=z[:, 0:1])
                            if sink:
                                hd = g // 2 + HEADS * (g % 2)
                                act(stats[:, (g % 3) * 8 + 4:(g % 3) * 8 + 6], negm, ACT.Exp,
                                    bias=rows[:, ROWS["sinks"] + hd:ROWS["sinks"] + hd + 1])
                            act(e(g)[:, P:SPAN], e(g)[:, P:SPAN], ACT.Exp, f"{sec}_exp", bias=negm[:, 1:2],
                                accum_out=z[:, 1:2])
                    if i >= 1:
                        g = i - 1
                        v = await_full(act_e, f"{sec}t{g}")
                        if g >= 2:
                            if g % 2:
                                b_, n_ = place[f"{sec}o{(g - 2) // 2}"]
                                act_e.wait_ge(full[b_], n_)
                            else:
                                act_e.wait_ge(*V(f"{sec}_even_o", (g - 2) // 2 + 1))
                        act(pT(g), v[:, 0:SPAN], ACT.Copy, f"{sec}_pT")
                        act_e.wait_ge(*V(f"{sec}_pT", g + 1))
                        act_e.sem_inc(free[place[f"{sec}t{g}"][0]], 1)

            def gate_up_high(nm, layer, j, steps):
                n = item_no[(nm, 0)] + j
                steps.landed(act_e, n)
                if j >= 2:
                    steps.bank(act_e, full, place[nm], j - 2, 1)
                act_e.activation(gu_part["hi"][j % 2], slot(n)[:, 0:gu_size], ACT.Copy).then_inc(S("gu_high"), 1)

            def ffn(nm, layer):
                silu_buf = page(2)[:, 1280:2048].rearrange("p (r t) -> p r t", t=T)

                def one(j, steps):
                    if j + 1 < FF_BLOCKS:
                        gate_up_high(nm, layer, j + 1, steps)
                    if j >= 2:
                        act_e.wait_ge(S(f"{nm}_down"), steps.at(j - 1, 6))
                    src = slot(item_no[(nm, 0)] + j)[:, gu_size:gu_size + down_size]
                    act_e.activation(down_part["hi"][j % 2], src, ACT.Copy).then_inc(S("down_high"), 1)
                    steps.bank(act_e, full, place[nm], j, 1)
                    if j >= 3:
                        steps.step(act_e, "hidden_split", j - 3)
                    act_e.activation(silu_buf[:, j % 3, :], psum[:, j % 3, 0:T], ACT.Silu).then_inc(S(f"{nm}_silu"), 1)

                use_tables(ACT.Silu)
                one(0, LayerSteps(layer))
                one(1, LayerSteps(layer))
                with act_e.Fori(0, 3) as it:
                    for j in range(2, 8):
                        one(j, LayerSteps(layer, it))
                for j in range(20, FF_BLOCKS):
                    one(j, LayerSteps(layer))
                st.last = (S(f"{nm}_silu"), FF_BLOCKS)

            def ffn_norm(nm, layer, before):
                rms(f"{nm}n", fm(0), fm(11), page(12)[:, 256:512], KD, D, before,
                    lambda: gate_up_high(nm, layer, 0, LayerSteps(layer)))
                for i in range(2):
                    act_e.wait_ge(*V(f"{nm}n_scaled", 4 * i + 4))
                    act_e.activation(x_part["hi"][:, 4 * i:4 * i + 4, :], fm(1)[:, 4 * i:4 * i + 4, :], ACT.Copy)\
                        .then_inc(S("x_high"), 1)

            rms("att0", fm(0), fm(11), page(12)[:, 256:512], KD, D, V("ln2_out", KD))
            q9 = page(9)[:, 0:512].rearrange("p (k t) -> p k t", t=T)
            v = await_full(act_e, "cq")
            act(page(9)[:, 0:512], v, ACT.Copy, "cq")
            v = await_full(act_e, "ckv")
            act(page(9)[:, 512:768], v[:, 0:T], ACT.Copy, "ckv")
            for part, off, scale in (("qB", 0, DIL_SCALE), ("kB", D, 1.0)):
                for n in range(2):
                    v = await_full(act_e, f"{part}{n}")
                    act(page(5)[:, off + n * 512:off + (n + 1) * 512], v, ACT.Copy, f"{part}{n}", scale=scale)
            st.settle()
            act_e.sem_inc(S("qkB_ready"), 4)
            rms("cqn", q9, page(11)[:, 0:512].rearrange("p (k t) -> p k t", t=T), page(12)[:, 512:768], 2, MLA_Q)
            rms("ckvn", page(9)[:, 512:768].rearrange("p (k t) -> p k t", t=T),
                page(11)[:, 512:768].rearrange("p (k t) -> p k t", t=T), page(12)[:, 768:1024], 1, MLA_KV)
            for b in range(NB):
                v = await_full(act_e, f"vB{b}")
                act(page(4)[:, D + b * 512:D + (b + 1) * 512], v, ACT.Copy, f"vB{b}")
            st.settle()
            act_e.sem_inc(S("vB_ready"), NB)
            for hd in range(HEADS):
                v = await_full(act_e, f"qA{hd}")
                act(fm(2)[0:NOPE, hd, :], v[0:NOPE, 0:T], ACT.Copy, "qA_nope", scale=MLA_SCALE)
            for h2 in range(HEADS // 2):
                v = await_full(act_e, f"kA{h2}")
                act(fm(3)[0:NOPE, 2 * h2:2 * h2 + 2, :], v[0:NOPE, :].rearrange("p (a t) -> p a t", a=2), ACT.Copy,
                    "kA_nope")
                act_e.wait_ge(*V("kA_nope", h2 + 1))
                act_e.sem_inc(free[place[f"kA{h2}"][0]], 1)
                act_e.sem_inc(S("kA_ready"), 1)
            for b in range(NB):
                v = await_full(act_e, f"vA{b}")
                act(page(4)[:, b * 512:(b + 1) * 512], v, ACT.Copy, f"vA{b}")
            st.settle()
            act_e.sem_inc(S("vA_ready"), NB)
            attend("mla", HEADS)
            attend("dil", HEADS)
            ffn_norm("ffn0", 0, (S("res3"), 4))
            ffn("ffn0", 0)
            rms("att1", fm(0), fm(11), page(12)[:, 256:512], KD, D, (S("res4"), 4))
            for n in range(4):
                v = await_full(act_e, f"qS{n}")
                act(page(2)[:, n * 512:(n + 1) * 512], v, ACT.Copy, "qS_evac", scale=DIL_SCALE)
                act_e.wait_ge(*V("qS_evac", n + 1))
                act_e.sem_inc(free[place[f"qS{n}"][0]], 1)
                act_e.sem_inc(S("qS_ready"), 1)
            v = await_full(act_e, "kS")
            act(page(3)[:, 0:T], v[:, 0:T], ACT.Copy, "kS")
            v = await_full(act_e, "vS")
            act(page(4)[:, 0:T], v[:, 0:T], ACT.Copy, "vS")
            st.settle()
            act_e.sem_inc(S("kvS_ready"), 2)
            attend("swa", SWA_HEADS, sink=True)
            ffn_norm("ffn1", 1, (S("res5"), 4))
            ffn("ffn1", 1)
            rms("final", fm(0), fm(11), page(12)[:, 256:512], KD, D, (S("res6"), 4))

        @block.vector
        def _(ve):
            st = Steps(ve, "dve_step")
            do, settle = st.do, st.settle

            def bc(ap, axis, shape):
                return ap.unsqueeze(axis).broadcast_to(shape)

            def center(nm, src, dst, small):
                v = await_full(ve, f"{nm}_mu")
                do(ve.tensor_scalar(small, v[:, 0:T], 1.0 / D, None, ALU.mult), f"{nm}_mu")
                settle()
                for i in range(2):
                    sl = slice(4 * i, 4 * i + 4)
                    do(ve.tensor_tensor(dst[:, sl, :], src[:, sl, :], bc(small, 1, [P, 4, T]), ALU.subtract),
                       f"{nm}_centered")

            def scale_rows(nm, src, dst, small, gain, nblocks, done):
                ve.wait_ge(*V(f"{nm}_rstd", 1))
                for k in range(nblocks):
                    do(ve.scalar_tensor_tensor(dst[:, k, :], src[:, k, :], col(gain, k), small, ALU.mult, ALU.mult), done)

            def layer_norm(nm, src, dst, mean, rstd, gain):
                center(nm, src, dst, mean)
                scale_rows(nm, dst, dst, rstd, gain, KD, f"{nm}_scaled")

            for n in range(6):
                pass
            ve.wait_ge(*V("constants", 16 * 6))
            ve.wait_ge(*V("x_landed", 16))
            layer_norm("ln_in", fm(1), fm(0), page(4)[:, 256:512], page(4)[:, 512:768], "ln_in_g")
            do(ve.memset(page(3)[CHUNK:P, 0:KD * P].rearrange("p (g t) -> p g t", t=P)[:, :, 0:CHUNK], 0.0), "gate_masked")
            for n in range(4):
                b_, n_ = place[f"gm_v{n}"]
                ve.wait_ge(free[b_], n_)
            ve.sem_inc(S("gm_v_ready"), 4)
            layer_norm("gm", fm(2), fm(2), page(7)[:, 0:256], page(7)[:, 256:512], "gm_g")
            for b in range(NB):
                for half in range(2):
                    v = await_full(ve, f"gm_t{b}{half}")
                    do(ve.tensor_copy(page(4)[:, b * D + half * 512:b * D + (half + 1) * 512], v), f"gm_t{b}{half}")
            settle()
            ve.sem_inc(S("gm_vtm"), 4)
            for n in range(4):
                v = await_full(ve, f"spatial{n}")
                b_, n_ = place[f"gm_u{n}"]
                ve.wait_ge(free[b_], n_)
                do(ve.tensor_tensor(page(5)[:, n * 512:(n + 1) * 512], v, page(5)[:, n * 512:(n + 1) * 512], ALU.mult),
                   f"spatial{n}")
            settle()
            ve.sem_inc(S("ya_ready"), 4)
            for part, off in (("gate_a", 0), ("gate_a_", 2)):
                for n in range(2):
                    b_, n_ = place[f"{part}{n}"]
                    ve.wait_ge(free[b_], n_)
            for n in range(4):
                v = await_full(ve, f"w_pa{n}")
                do(ve.tensor_tensor(page(1)[:, n * 512:(n + 1) * 512], v, page(6)[:, n * 512:(n + 1) * 512], ALU.mult),
                   f"w_pa{n}")
            settle()
            stage = lambda n: page(5)[:, n % 6 * 260:n % 6 * 260 + 260]
            for n in range(6):
                do(ve.memset(stage(n)[:, 0:4], 0.0), "stage_zero")
            for blk in range(24):
                if blk == 16:
                    ab_stage(ve, st, S, ab, row, await_full, bc)
                dst = fm(2 + blk // 8)[:, blk % 8, :]
                s = stage(blk)
                ve.wait_ge(*V("staged", blk + 1))
                tap = lambda j: col("conv", j * 24 + blk)
                do(ve.tensor_scalar(dst, s[:, 4:260], tap(3), None, ALU.mult))
                for j in range(3):
                    settle()
                    do(ve.scalar_tensor_tensor(dst, s[:, 1 + j:257 + j], tap(j), dst, ALU.mult, ALU.add),
                       "conv_done" if j == 2 else None)
            ve.wait_ge(*V("ab_exps", 1))
            ab_finish(ve, st, S, ab)
            v = await_full(ve, "G")
            G = ab[:, 80:96]
            do(ve.tensor_copy(G, v[:, 0:16]), "G")
            settle()
            D_, DT = page(11), page(10)
            for q4 in range(4):
                v = await_full(ve, f"Gb{q4}")
                ve.wait_ge(*V("expG_row", q4 + 1))
                v4 = v.rearrange("p (h b t) -> p h b t", h=2, b=NB)
                last = ab[:, 160 + 4 * q4:164 + 4 * q4].rearrange("p (h b) -> p h b", h=2)
                do(ve.tensor_copy(last[0:CHUNK], v4[0:CHUNK, :, :, CHUNK - 1]))
                do(ve.tensor_copy(last[CHUNK:P], v4[CHUNK:P, :, :, P - 1]))
                gcol = G.rearrange("p (b h) -> p h b", b=NB)[:, 2 * q4:2 * q4 + 2, :]
                gcol = gcol.unsqueeze(3).broadcast_to([P, 2, NB, P])
                view = lambda pg: pg[:, q4 * BANK:(q4 + 1) * BANK].rearrange("p (h b t) -> p h b t", h=2, b=NB)
                for hh in range(2):
                    do(ve.tensor_tensor(view(DT)[:, hh], v4[:, hh], gcol[:, hh], ALU.subtract))
                    do(ve.tensor_tensor(view(D_)[:, hh], gcol[:, hh], v4[:, hh], ALU.subtract),
                       f"Gb{q4}" if hh else None)
            settle()
            do(ve.tensor_scalar(page(10, 2), page(10, 2), 0.0, None, ALU.min), "decay_clipped")
            do(ve.tensor_copy(ab[:, 96:112], G))
            do(ve.tensor_tensor(ab[:, 112:128].rearrange("p (b h) -> p h b", b=NB), ab[:, 160:176].rearrange("p (h b) -> p h b", b=NB),
                                G.rearrange("p (b h) -> p h b", b=NB), ALU.subtract), "G_small")
            for part, pg, src in (("q", 7, 2), ("k", 8, 3)):
                for q4 in range(4):
                    ve.wait_ge(*V(f"{part}_inv", q4 + 1))
                    sl = slice(q4 * BANK, (q4 + 1) * BANK)
                    do(ve.tensor_tensor(page(src)[:, sl], page(src)[:, sl], page(pg)[:, sl], ALU.mult), f"{part}_normed")
            ve.wait_ge(*V("decay_masked", 2))
            for q4 in range(4):
                v = await_full(ve, f"kk{q4}")
                sl = slice(q4 * BANK, (q4 + 1) * BANK)
                do(ve.tensor_tensor(page(11)[:, sl], v, page(11)[:, sl], ALU.mult), f"kk{q4}")
                settle()
                ve.sem_inc(S("L_ready"), 1)
            ve.wait_ge(*V("tm_ready", 1))
            idb = bc(ident, 1, [P, 4, P])
            for q4 in range(4):
                sl = slice(q4 * BANK, (q4 + 1) * BANK)
                v3 = lambda pg: page(pg)[:, sl].rearrange("p (u t) -> p u t", t=P)
                do(ve.tensor_tensor(v3(5), v3(11), bc(mask("first"), 1, [P, 4, P]), ALU.mult))
                ve.wait_ge(*V("LT_ready", q4 + 1))
                do(ve.tensor_tensor(v3(4), v3(12), bc(mask("first_t"), 1, [P, 4, P]), ALU.mult))
                settle()
                do(ve.tensor_tensor(v3(5), idb, v3(5), ALU.subtract))
                do(ve.tensor_tensor(v3(4), idb, v3(4), ALU.subtract), "X_ready")
                b_, n_ = place[f"L_t{q4}"]
                ve.sem_inc(free[b_], 1)
            for q4 in range(4):
                v = await_full(ve, f"qk{q4}")
                sl = slice(q4 * BANK, (q4 + 1) * BANK)
                do(ve.tensor_tensor(page(10)[:, sl], v, page(10)[:, sl], ALU.mult), f"qk{q4}")
            settle()
            do(ve.tensor_tensor(page(2), page(2), page(9), ALU.mult), "qd_ready")
            cd = ab[:, 128:160]
            do(ve.tensor_copy(cd, page(9).rearrange("p (x t) -> p x t", t=CHUNK)[:, :, CHUNK - 1]))
            settle()
            for lv in range(5):
                for q4 in range(4):
                    sl = slice(q4 * BANK, (q4 + 1) * BANK)
                    v3 = lambda pg: page(pg)[:, sl].rearrange("p (u t) -> p u t", t=P)
                    name = f"Y{lv}_{q4}"
                    v = await_full(ve, name)
                    do(ve.tensor_tensor(v3(9), v.rearrange("p (u t) -> p u t", t=P),
                                        bc(mask(f"level{2 << lv}"), 1, [P, 4, P]), ALU.mult), "Y_evac")
                    ve.wait_ge(*V("Y_evac", 4 * lv + q4 + 1))
                    ve.sem_inc(free[place[name][0]], 1)
                    ve.sem_inc(S("Y_ready"), 1)
                for q4 in range(4):
                    sl = slice(q4 * BANK, (q4 + 1) * BANK)
                    if lv < 4:
                        v = await_full(ve, f"Z{lv}_{q4}")
                    w = await_full(ve, f"ZT{lv}_{q4}")
                    do(ve.tensor_tensor(page(4)[:, sl], page(4)[:, sl], w, ALU.subtract), f"ZT{lv}_{q4}")
                    if lv < 4:
                        do(ve.tensor_tensor(page(5)[:, sl], page(5)[:, sl], v, ALU.subtract), f"Z{lv}_{q4}")
                        settle()
                        ve.sem_inc(S("X_ready"), 1)
            settle()
            ve.sem_inc(S("XT_final"), 4)
            for q4 in range(4):
                v = await_full(ve, f"uc{q4}")
                do(ve.tensor_copy(page(11)[:, q4 * BANK:(q4 + 1) * BANK], v), f"uc{q4}")
            settle()
            ve.sem_inc(S("vnew_ready"), 2)
            state = page(5)[:, 0:HEADS * P]
            vn = page(11).rearrange("p (h b d) -> p h b d", b=NB, d=P)
            for c in range(T // CHUNK):
                b, r = c // 2, CHUNK * (c % 2)
                if c > 0:
                    for hh in range(2):
                        v = await_full(ve, f"ws{c}_{hh}")
                        dst = vn[r:r + CHUNK, 4 * hh:4 * hh + 4, b, :]
                        do(ve.tensor_tensor(dst, dst, v[r:r + CHUNK, :].rearrange("p (h d) -> p h d", h=4), ALU.subtract),
                           "vnew_evac")
                        ve.wait_ge(*V("vnew_evac", 2 * (c - 1) + hh + 1))
                        ve.sem_inc(free[place[f"ws{c}_{hh}"][0]], 1)
                        ve.sem_inc(S("vnew_ready"), 1)
                if c < T // CHUNK - 1:
                    if c > 0:
                        b_, n_ = place[f"o{c}"]
                        ve.wait_ge(full[b_], n_)
                    for hh in range(2):
                        v = await_full(ve, f"ds{c}_{hh}")
                        if c == 0:
                            do(ve.tensor_copy(state[:, hh * 512:(hh + 1) * 512], v), f"ds{c}_{hh}")
                        else:
                            for j in range(4):
                                hd = 4 * hh + j
                                sl = slice(hd * P, (hd + 1) * P)
                                x = hd * 4 + c
                                do(ve.scalar_tensor_tensor(state[:, sl], state[:, sl], cd[:, x:x + 1],
                                                           v[:, j * P:(j + 1) * P], ALU.mult, ALU.add),
                                   f"ds{c}_{hh}" if j == 3 else None)
                    settle()
                    ve.sem_inc(S("state_ready"), 1)
            b_, n_ = place["o3"]
            ve.wait_ge(free[b_], n_)
            ve.wait_ge(*V("z_ready", 1))
            for q4 in range(4):
                ve.wait_ge(*V("o_inv", q4 + 1))
                sl = slice(q4 * BANK, (q4 + 1) * BANK)
                do(ve.scalar_tensor_tensor(page(4)[:, sl], page(4)[:, sl], col("dn_norm"), page(7)[:, sl], ALU.mult,
                                           ALU.mult))
                settle()
                do(ve.tensor_tensor(page(4)[:, sl], page(4)[:, sl], page(6)[:, sl], ALU.mult))
                settle()
                ve.sem_inc(S("yb_ready"), 2)
            for n in range(4):
                v = await_full(ve, f"w_pb{n}")
                sl = slice(n * BANK, (n + 1) * BANK)
                do(ve.tensor_tensor(page(9)[:, sl], v, page(9)[:, sl], ALU.mult), f"w_pb{n}")
                settle()
                do(ve.tensor_tensor(page(1)[:, sl], page(1)[:, sl], page(9)[:, sl], ALU.add), "merged")

            def residual(part, alpha, done, names):
                for n, name in enumerate(names):
                    v = await_full(ve, name)
                    sl = slice(n * BANK, (n + 1) * BANK)
                    if alpha is None:
                        do(ve.tensor_tensor(page(0)[:, sl], page(0)[:, sl], v, ALU.add), name)
                    else:
                        do(ve.scalar_tensor_tensor(page(0)[:, sl], page(0)[:, sl], alpha, v, ALU.mult, ALU.add), name)
                    settle()
                    ve.sem_inc(S(done), 1)

            residual("w_o", ALPHA, "res1", [f"w_o{n}" for n in range(4)])
            layer_norm("ln1", fm(0), fm(0), page(12)[:, 0:256], page(12)[:, 256:512], "ln1_g")
            if phases < 2:
                return

            r11 = page(11)
            logits = r11[:, 0:72].rearrange("p (b c) -> p b c", b=NB)
            v = await_full(ve, "router")
            ve.wait_ge(*V("ln1_out", KD))
            ve.wait_ge(*V("router_landed", 32))
            do(ve.tensor_tensor(logits, v[:, 0:72].rearrange("p (b c) -> p b c", b=NB), bc(row("b_router", 36), 1, [P, NB, 36]),
                                ALU.add), "router")
            ge = r11[:, 80:96].rearrange("p (b g) -> p b g", b=NB)
            do(ve.memset(r11[:, 80:96], -1.0))
            settle()
            two = lambda n: r11[:, 96 + 2 * n:98 + 2 * n]
            col2 = lambda ap, b: ap[:, b:b + 1]
            do(ve.tensor_reduce(two(0), logits[:, :, 0:GROUPS], AX.X, ALU.max))
            settle()
            do(ve.tensor_tensor(ge[:, :, 0:GROUPS], logits[:, :, 0:GROUPS], bc(two(0), 2, [P, NB, GROUPS]), ALU.subtract),
               "group_centered")
            ve.wait_ge(*V("group_exp", 1))
            do(ve.tensor_reduce(two(1), ge[:, :, 0:GROUPS], AX.X, ALU.add))
            settle()
            do(ve.reciprocal(two(2), two(1)))
            iota = page(10)[:, KD * 36:KD * 36 + ASSIGN]
            expert_row = page(10)[:, KD * 36 + ASSIGN:KD * 36 + ASSIGN + 32]
            group_row = page(10)[:, KD * 36 + ASSIGN + 32:KD * 36 + ASSIGN + 64]
            idx = r11[:, 128:192].bitcast(U32)
            masked = r11[:, 256:320].rearrange("p (b e) -> p b e", b=NB)
            for b in range(NB):
                do(ve.max(r11[:, 192:200], ge[:, b, :]))
                settle()
                do(ve.max_index(idx[:, 0:8], r11[:, 192:200], ge[:, b, :]))
                settle()
                do(ve.tensor_copy(r11[:, 112 + b:113 + b], idx[:, 0:1]))
                settle()
                do(ve.tensor_scalar(masked[:, b, :], group_row, r11[:, 112 + b:113 + b], None, ALU.is_equal))
                settle()
                do(ve.tensor_scalar(masked[:, b, :], masked[:, b, :], 1.0, 1e30, ALU.subtract, ALU.mult))
                settle()
                do(ve.tensor_tensor(masked[:, b, :], masked[:, b, :], logits[:, b, GROUPS:36], ALU.add))
                settle()
                do(ve.max(r11[:, 200 + 8 * b:208 + 8 * b], masked[:, b, :]))
                settle()
                do(ve.max_index(idx[:, 8 + 8 * b:16 + 8 * b], r11[:, 200 + 8 * b:208 + 8 * b], masked[:, b, :]))
                settle()
                do(ve.tensor_copy(r11[:, 120 + 2 * b:122 + 2 * b], idx[:, 8 + 8 * b:10 + 8 * b]))
            best = r11[:, 200:216].rearrange("p (b x) -> p b x", b=NB)
            settle()
            do(ve.tensor_tensor(r11[:, 240:242], best[:, :, 1], best[:, :, 0], ALU.subtract), "top_diff")
            eh = lambda s: r11[:, 320 + 64 * s:384 + 64 * s].rearrange("p (b e) -> p b e", b=NB)
            pick = r11[:, 512:576]
            for b in range(NB):
                for s in range(2):
                    do(ve.tensor_scalar(eh(s)[:, b, :], expert_row, r11[:, 120 + 2 * b + s:121 + 2 * b + s], None, ALU.is_equal))
            settle()
            do(ve.tensor_tensor(pick, r11[:, 320:384], r11[:, 384:448], ALU.add), "picked")
            ve.wait_ge(*V("top_exp", 1))
            do(ve.tensor_scalar(r11[:, 242:244], r11[:, 240:242], 1.0, None, ALU.add))
            settle()
            do(ve.reciprocal(r11[:, 244:246], r11[:, 242:244]))
            settle()
            do(ve.tensor_tensor(r11[:, 246:248], r11[:, 244:246], two(2), ALU.mult))
            settle()
            do(ve.tensor_tensor(r11[:, 248:250], r11[:, 246:248], r11[:, 240:242], ALU.mult))
            v = await_full(ve, "rank")
            do(ve.tensor_copy(r11[0:EXPERTS, 640:640 + P], v[0:EXPERTS, 96:97].broadcast_to([EXPERTS, P])), "counts_spread")
            do(ve.tensor_reduce(r11[0:1, 252:253], v[0:1, 64:96], AX.X, ALU.max))
            settle()
            do(ve.tensor_copy(starts[0:1, EXPERTS:EXPERTS + 1], r11[0:1, 252:253]))
            do(ve.tensor_copy(r11[:, 576:640], v[:, 0:64]), "rank")
            v = await_full(ve, "start")
            do(ve.tensor_copy(starts[0:1, 0:EXPERTS], v[0:1, 0:EXPERTS]))
            settle()
            ve.sem_inc(S("starts_ready"), 1)
            where = r11[:, 576:640].rearrange("p (b e) -> p b e", b=NB)
            do(ve.tensor_tensor(where, where, bc(v[:, 0:EXPERTS], 1, [P, NB, EXPERTS]), ALU.add), "start")
            settle()
            for s in range(2):
                do(ve.tensor_tensor(eh(s), eh(s), where, ALU.mult))
            settle()
            for s in range(2):
                do(ve.tensor_reduce(r11[:, 224 + 2 * s:226 + 2 * s], eh(s), AX.X, ALU.add))
            settle()
            onehot = page(8)[:, 0:NB * ASSIGN].rearrange("p (b s) -> p b s", b=NB)
            gated = page(8)[:, NB * ASSIGN:2 * NB * ASSIGN].rearrange("p (b s) -> p b s", b=NB)
            pos = lambda s, b: r11[:, 224 + 2 * s + b:225 + 2 * s + b]
            gate = lambda s, b: r11[:, 246 + 2 * s + b:247 + 2 * s + b]
            for b in range(NB):
                do(ve.tensor_scalar(onehot[:, b, :], iota, pos(0, b), None, ALU.is_equal))
                settle()
                do(ve.scalar_tensor_tensor(onehot[:, b, :], iota, pos(1, b), onehot[:, b, :], ALU.is_equal, ALU.add),
                   "onehot_ready")
            spare = r11[:, 1024:1536]
            for b in range(NB):
                do(ve.tensor_scalar(gated[:, b, :], iota, pos(0, b), gate(0, b), ALU.is_equal, ALU.mult))
                do(ve.tensor_scalar(spare, iota, pos(1, b), gate(1, b), ALU.is_equal, ALU.mult))
                settle()
                do(ve.tensor_tensor(gated[:, b, :], gated[:, b, :], spare, ALU.add), "gated_ready")
                settle()
            for k in range(1, KD, 2):
                v = await_full(ve, f"xs{k}")
                do(ve.tensor_copy(page(2, 3).rearrange("p (k s) -> p k s", k=KD)[:, k, 0:ASSIGN], v), f"xs{k}")
            settle()
            ve.sem_inc(S("xs_odd"), 4)
            silu = page(10)[:, 1024:1536].rearrange("p (r s) -> p r s", r=2)
            acts = page(10)[:, 1536:2048].rearrange("p (r s) -> p r s", r=2)
            ys = page(5, 3).rearrange("p (k s) -> p k s", k=KD)
            base = place["moe_base"]
            def place_output(r, start):
                return ve.tensor_copy(ys.rearrange("p (g c) s -> p g c s", g=2)[:, :, :, bass.ds(start, CAP)],
                                      psum[:, 6 + r, :].rearrange("p (c g s) -> p g c s", c=4, g=2))

            with ve.Fori(0, EXPERTS // 2) as it:
                for r in range(2):
                    ve.wait_ge(*V("silu_ready", it * 2 + r + 1))
                    ve.wait_ge(full[2 + r], it + base[2 + r])
                    ve.tensor_tensor(acts[:, r, :], silu[:, r, :], psum[:, r, T:2 * T], ALU.mult).then_inc(free[r], 1)
                for r in range(2):
                    start = ve.value_load(starts[0:1, bass.ds(it * 2 + r, 1)], min_val=0, max_val=ASSIGN)
                    ve.wait_ge(full[6 + r], it + base[6 + r] + 1)
                    if r:
                        ve.wait_ge(free[6], it + base[6] + 1)
                    else:
                        ve.wait_ge(free[7], it + base[7])
                    place_output(r, start).then_inc(free[6 + r], 1)
            st.last = (free[7], base[7] + EXPERTS // 2)
            settle()
            most = ve.value_load(starts[0:1, EXPERTS:EXPERTS + 1], min_val=0, max_val=T)
            with ve.If(most > CAP):
                ve.sem_inc(S("more_out"), 1)
                with ve.Fori(0, EXPERTS) as e:
                    start = ve.value_load(starts[0:1, bass.ds(e, 1)], min_val=0, max_val=ASSIGN)
                    for c in range(MAX_PASSES):
                        n = e * MAX_PASSES + c + 1
                        ve.wait_ge(*V("more_silu", n))
                        ve.tensor_tensor(acts[:, 0, :], silu[:, 0, :], psum[:, 0, T:2 * T], ALU.mult).then_inc(S("more_act"), 1)
                        ve.wait_ge(*V("more_z", n))
                        ve.wait_ge(*V("more_out", n))
                        place_output(0, start + c * CAP).then_inc(S("more_out"), 1)
                ve.wait_ge(*V("more_out", EXPERTS * MAX_PASSES + 1))
            do(ve.memset(ab[:, 0:1], 0.0), "experts_done")
            for s in range(4):
                v = await_full(ve, f"y_t{s}1")
                do(ve.tensor_copy(page(11, 2)[:, s * D + 512:(s + 1) * D], v), f"y_t{s}1")
            settle()
            ve.sem_inc(S("ytm_odd"), 4)
            residual("moe", ALPHA, "res2", [f"moe{m}" for m in range(4)])
            layer_norm("ln2", fm(0), fm(0), page(12)[:, 0:256], page(12)[:, 256:512], "ln2_g")
            if phases < 3:
                return

            attn = lambda n: page(10)[:, n * SPAN:(n + 1) * SPAN]
            dil_t, mult_t, swa_t, causal_t = (attn(n) for n in range(4))
            cos = page(10)[:, 4 * SPAN:4 * SPAN + T]
            sin = page(10)[:, 4 * SPAN + T:4 * SPAN + 2 * T]
            rope = slice(NOPE, NOPE + ROPE)

            def attend(sec, nheads, bias, slope, sink=False):
                stats = page(7)[:, 1024:1024 + 64]
                e = lambda g: page(6)[:, (g % 3) * SPAN:(g % 3 + 1) * SPAN]
                for i in range(nheads + 1):
                    if i < nheads:
                        g = i
                        v = await_full(ve, f"{sec}s{g}")
                        if g >= 3:
                            b_, n_ = place[f"{sec}t{g - 3}"]
                            ve.wait_ge(full[b_], n_)
                        negm = stats[:, (g % 3) * 8:(g % 3) * 8 + 2]
                        do(ve.scalar_tensor_tensor(e(g), bias, slope(g), v[:, 0:SPAN], ALU.mult, ALU.add), f"{sec}s{g}")
                        settle()
                        if sink:
                            hd = g // 2 + HEADS * (g % 2)
                            do(ve.tensor_reduce(negm[:, 0:1], e(g)[:, 0:P], AX.X, ALU.max))
                            do(ve.tensor_reduce(negm[:, 1:2], e(g)[:, P:SPAN], AX.X, ALU.max))
                            settle()
                            do(ve.tensor_scalar(negm, negm, rows[:, ROWS["sinks"] + hd:ROWS["sinks"] + hd + 1], -1.0,
                                                ALU.max, ALU.mult))
                            settle()
                            ve.sem_inc(S(f"{sec}_max"), 2)
                        else:
                            do(ve.tensor_reduce(negm[:, 0:1], e(g)[:, 0:P], AX.X, ALU.max, negate=True))
                            do(ve.tensor_reduce(negm[:, 1:2], e(g)[:, P:SPAN], AX.X, ALU.max, negate=True))
                            settle()
                            ve.sem_inc(S(f"{sec}_max"), 2)
                    if i >= 1:
                        g = i - 1
                        z = stats[:, (g % 3) * 8 + 2:(g % 3) * 8 + 4]
                        ve.wait_ge(*V(f"{sec}_exp", g + 1))
                        if sec == "dil":
                            for a, b, n in ((0, P, 0), (P, SPAN, 1)):
                                do(ve.tensor_tensor_reduce(e(g)[:, a:b], e(g)[:, a:b], mult_t[:, a:b], 1.0, 0.0,
                                                           ALU.mult, ALU.add, z[:, n:n + 1]))
                            settle()
                        if sink:
                            do(ve.tensor_tensor(z, z, stats[:, (g % 3) * 8 + 4:(g % 3) * 8 + 6], ALU.add))
                            settle()
                        do(ve.reciprocal(z, z))
                        settle()
                        do(ve.tensor_scalar(e(g)[:, 0:P], e(g)[:, 0:P], z[:, 0:1], None, ALU.mult))
                        do(ve.tensor_scalar(e(g)[:, P:SPAN], e(g)[:, P:SPAN], z[:, 1:2], None, ALU.mult), f"{sec}_probs")
                    if i >= 3 and i % 2 == 1:
                        output(sec, (i - 3) // 2)
                output(sec, nheads // 2 - 1)

            def output(sec, n):
                name = f"{sec}o{n}"
                v = await_full(ve, name)
                first = {"mla": 0, "dil": 4, "swa": 0}[sec]
                do(ve.tensor_copy(fm(8)[:, first + n, :], v[:, 0:T]), name)
                settle()
                ve.sem_inc(S(f"{sec}_o_ready"), 1)

            def gate_up_low(nm, j, steps):
                steps.step(ve, "gu_high", j)
                ve.tensor_tensor(gu_part["lo"][j % 2], slot(item_no[(nm, 0)] + j)[:, 0:gu_size],
                                 gu_part["hi"][j % 2], ALU.subtract).then_inc(S("gu_split"), 1)

            def ffn(nm, layer, done):
                base = place[nm]
                silu_buf = page(2)[:, 1280:2048].rearrange("p (r t) -> p r t", t=T)
                for i in range(2):
                    ve.wait_ge(S("x_high"), 2 * layer + i + 1)
                    sl = slice(4 * i, 4 * i + 4)
                    ins = ve.tensor_tensor(x_part["lo"][:, sl, :], fm(1)[:, sl, :], x_part["hi"][:, sl, :], ALU.subtract)
                ins.then_inc(S("x_split"), 1)

                def one(j, steps):
                    if j + 1 < FF_BLOCKS:
                        gate_up_low(nm, j + 1, steps)
                    steps.step(ve, "down_high", j)
                    ve.tensor_tensor(down_part["lo"][j % 2], slot(item_no[(nm, 0)] + j)[:, gu_size:gu_size + down_size],
                                     down_part["hi"][j % 2], ALU.subtract).then_inc(S("down_split"), 1)
                    j3 = j % 3
                    ve.wait_ge(S(f"{nm}_silu"), steps.at(j + 1, 6))
                    ve.tensor_tensor(hidden[:, j3, :], silu_buf[:, j3, :], psum[:, j3, T:2 * T], ALU.mult).then_inc(free[j3], 1)
                    steps.bank(ve, free, base, j, 1)
                    if j >= 3:
                        ve.wait_ge(S(f"{nm}_down"), steps.at(j - 2, 6))
                    ve.tensor_copy(hidden_part["hi"][:, j3, :], hidden[:, j3, :]).then_inc(S("hidden_high"), 1)
                    steps.step(ve, "hidden_high", j)
                    ve.tensor_tensor(hidden_part["lo"][:, j3, :], hidden[:, j3, :], hidden_part["hi"][:, j3, :],
                                     ALU.subtract).then_inc(S("hidden_split"), 1)

                for j in range(3):
                    one(j, LayerSteps(layer))
                with ve.Fori(0, 3) as it:
                    for j in range(3, 9):
                        one(j, LayerSteps(layer, it))
                one(21, LayerSteps(layer))
                for n in range(4):
                    b = 4 + n
                    ve.wait_ge(full[b], base[b] + 1)
                    sl = slice(n * BANK, (n + 1) * BANK)
                    do(ve.tensor_tensor(page(0)[:, sl], page(0)[:, sl], psum[:, b, :], ALU.add), "ffn_sum")
                    settle()
                    ve.sem_inc(free[b], 1)
                    ve.sem_inc(S(done), 1)

            ve.wait_ge(*V("ln2_out", KD))
            scale_rows("att0", fm(0), fm(1), page(12)[:, 256:512], "att0", KD, "att0_scaled")
            ve.wait_ge(*V("attn_tables", 16))
            v = await_full(ve, "kr")
            t1, t2 = page(7)[rope, 1536:1792], page(7)[rope, 1792:2048]
            do(ve.tensor_tensor(t1, v[rope, 0:T], cos[rope, :], ALU.mult))
            do(ve.tensor_tensor(t2, v[rope, T:2 * T], sin[rope, :], ALU.mult), "kr")
            settle()
            do(ve.tensor_tensor(t1, t1, t2, ALU.add))
            settle()
            do(ve.tensor_copy(fm(3)[rope, :, :], bc(t1, 1, [ROPE, HEADS, T])))
            settle()
            ve.sem_inc(S("kA_ready"), 1)
            scale_rows("cqn", page(9)[:, 0:512].rearrange("p (k t) -> p k t", t=T),
                       page(9)[:, 768:1280].rearrange("p (k t) -> p k t", t=T), page(12)[:, 512:768], "q_norm", 2, "cqn_scaled")
            scale_rows("ckvn", page(9)[:, 512:768].rearrange("p (k t) -> p k t", t=T),
                       page(9)[:, 1280:1536].rearrange("p (k t) -> p k t", t=T), page(12)[:, 768:1024], "kv_norm", 1, "ckvn_scaled")
            for hd in range(HEADS):
                v = await_full(ve, f"qA{hd}")
                ve.wait_ge(*V("qA_nope", hd + 1))
                do(ve.scalar_tensor_tensor(t1, v[rope, 0:T], MLA_SCALE, cos[rope, :], ALU.mult, ALU.mult))
                do(ve.scalar_tensor_tensor(t2, v[rope, T:2 * T], MLA_SCALE, sin[rope, :], ALU.mult, ALU.mult), f"qA{hd}")
                settle()
                do(ve.tensor_tensor(fm(2)[rope, hd, :], t1, t2, ALU.add), "qA_ready")
                settle()
            attend("mla", HEADS, causal_t, lambda g: 1.0)
            attend("dil", HEADS, dil_t, lambda g: 2.0 ** -(g + 1))
            residual("e_out", None, "res3", [f"e_out{n}" for n in range(4)])
            do(ve.memset(page(2)[:, 768:1280], 0.0), "zeros_ready")
            gate_up_low("ffn0", 0, LayerSteps(0))
            scale_rows("ffn0n", fm(0), fm(1), page(12)[:, 256:512], "ffn0", KD, "ffn0n_scaled")
            ffn("ffn0", 0, "res4")
            scale_rows("att1", fm(0), fm(1), page(12)[:, 256:512], "att1", KD, "att1_scaled")
            attend("swa", SWA_HEADS, swa_t, lambda g: 2.0 ** (-0.5 * (g // 2 + HEADS * (g % 2) + 1)), sink=True)
            residual("o_out", None, "res5", [f"o_out{n}" for n in range(4)])
            do(ve.memset(page(2)[:, 768:1280], 0.0), "zeros_ready")
            gate_up_low("ffn1", 0, LayerSteps(1))
            scale_rows("ffn1n", fm(0), fm(1), page(12)[:, 256:512], "ffn1", KD, "ffn1n_scaled")
            ffn("ffn1", 1, "res6")
            scale_rows("final", fm(0), fm(1), page(12)[:, 256:512], "final", KD, "final_scaled")

        @block.gpsimd
        def _(pool):
            st = Steps(pool, "pool_step")
            pool.wait_ge(*V("decay_ready", 1))
            beta = ab[:, 16:32].rearrange("p (b h) -> p h b", b=NB)
            v3 = lambda pg: units(pg)
            bcu = lambda ap: ap.unsqueeze(1).broadcast_to([P, UNITS, P])
            st.do(pool.tensor_tensor(v3(11), v3(11), bcu(mask("strict_low")), ALU.mult))
            st.do(pool.tensor_tensor(v3(10), v3(10), bcu(mask("incl_up")), ALU.mult), "decay_masked")
            st.settle()

            def per_token(dst, src, what, name):
                for b in range(NB):
                    d = dst.rearrange("p (h b) t -> p h b t", b=NB)[:, :, b, :]
                    s = src.rearrange("p (h b) t -> p h b t", b=NB)[:, :, b, :]
                    w = what[:, b * HEADS:(b + 1) * HEADS].unsqueeze(2).broadcast_to([P, HEADS, P])
                    st.do(pool.tensor_tensor(d, s, w, ALU.mult), name if b else None)

            per_token(v3(11), v3(11), ab[:, 16:32], "decay_masked")
            pool.wait_ge(*V("tm_ready", 1))
            per_token(v3(8), v3(8), ab[:, 16:32], "vb_ready")
            pool.wait_ge(*V("expG_col", 1))
            st.do(pool.tensor_tensor(ab[:, 96:112], ab[:, 96:112], ab[:, 16:32], ALU.mult))
            st.settle()
            for q4 in range(4):
                b_, n_ = place[f"qk{q4}"]
                pool.wait_ge(full[b_], n_)
            per_token(v3(3), v3(7), ab[:, 96:112], "kbg_ready")
            st.settle()
            per_token(v3(7), v3(7), ab[:, 112:128], "kdec_ready")
            if phases >= 2:
                pool.wait_ge(*V("ln1_out", KD))
                st.do(pool.memset(page(2, 3).rearrange("p (k s) -> p k s", k=KD)[:, :, ASSIGN:SORTED], 0.0), "xs_tail")
                xs = page(2, 3).rearrange("p (k s) -> p k s", k=KD)
                xe = page(9)[:, 1024:2048].rearrange("p (r k s) -> p r k s", r=2, k=KD)
                pool.wait_ge(*V("xs_tail", 1))
                pool.wait_ge(*V("xs_ready", KD))
                pool.wait_ge(*V("starts_ready", 1))
                base = place["moe_base"]
                with pool.Fori(0, EXPERTS // 2) as it:
                    for r in range(2):
                        start = pool.value_load(starts[0:1, bass.ds(it * 2 + r, 1)], min_val=0, max_val=ASSIGN)
                        pool.wait_ge(full[r], it + base[r])
                        pool.tensor_copy(xe[:, r, :, :], xs[:, :, bass.ds(start, CAP)]).then_inc(S("xe_ready"), 1)
                most = pool.value_load(starts[0:1, EXPERTS:EXPERTS + 1], min_val=0, max_val=T)
                pool.wait_ge(full[0], base[0] + EXPERTS // 2)
                with pool.If(most > CAP):
                    pool.sem_inc(S("more_h"), 1)
                    with pool.Fori(0, EXPERTS) as e:
                        start = pool.value_load(starts[0:1, bass.ds(e, 1)], min_val=0, max_val=ASSIGN)
                        for c in range(MAX_PASSES):
                            pool.wait_ge(*V("more_h", e * MAX_PASSES + c + 1))
                            pool.tensor_copy(xe[:, 0, :, :], xs[:, :, bass.ds(start + c * CAP, CAP)])\
                                .then_inc(S("more_xe"), 1)

        @block.sync
        def _(sp):
            sp.dma_start(fm(1), io["xT"].rearrange("(k p) t -> p k t", p=P)).then_inc(S("x_landed"), 16)

            def columns(name, c0, width):
                return io[name].rearrange("(k p) c -> p k c", p=P)[:, :, c0:c0 + width]

            first_column = {"gm_u": 0, "gm_v": 1024, "dn_q": 2048, "dn_k": 3072, "dn_v": 4096, "dn_z": 5120,
                            "gate_a": 6160, "gate_b": 7184}

            def source(name, i):
                if name in first_column:
                    return columns("w_in", first_column[name] + 512 * i, 512)
                if name in ("w_pa", "w_pb", "w_o", "e_out", "o_out"):
                    return columns(name, 512 * i, 512)
                if name == "e_in":
                    return columns("e_in", 0, 448) if i == 0 else columns("e_in", 448 + 512 * (i - 1), 512)
                if name == "mla_up":
                    return io["mla_up"]
                if name == "o_in":
                    return columns("o_in", 512 * i, 512)
                if name == "o_kv":
                    return columns("o_in", 1024, 256)
                return io[name][i]

            def load(n, name, i, wait=True):
                if wait and n >= SLOTS:
                    sp.wait_ge(*released[n - SLOTS])
                src = source(name, i)
                floats = int(np.prod(src.shape[1:]))
                dst = slot(n, floats)
                if len(src.shape) == 3:
                    dst = dst.rearrange("p (k c) -> p k c", k=src.shape[1])
                sp.dma_start(dst, src).then_inc(landed[n % SLOTS], 16)

            expert_src = lambda name, e: io[name][bass.ds(e, 1)].rearrange("e (k p) c -> p (e k) c", p=P)

            def load_expert(n, name, e):
                src = expert_src(name, e)
                sp.dma_start(slot(n).rearrange("p (k c) -> p k c", k=src.shape[1]), src)\
                    .then_inc(landed[n % SLOTS], 16)

            for n, (name, i) in enumerate(items[:moe_first]):
                load(n, name, i)
            if phases >= 2:
                for r in range(2):
                    for x, name in enumerate(("w1", "w3", "w2")):
                        n = moe_first + 3 * r + x
                        sp.wait_ge(*released[n - SLOTS])
                        src = io[name][r].rearrange("(k p) c -> p k c", p=P)
                        sp.dma_start(slot(n).rearrange("p (k c) -> p k c", k=src.shape[1]), src)\
                            .then_inc(landed[n % SLOTS], 16)
                base = place["moe_base"]
                with sp.Fori(1, EXPERTS // 2) as it:
                    for r in range(2):
                        n = moe_first + 3 * r
                        sp.wait_ge(*V("w1_read", it * 2 + r - 1))
                        src = expert_src("w1", it * 2 + r)
                        sp.dma_start(slot(n).rearrange("p (k c) -> p k c", k=KD), src).then_inc(landed[n % SLOTS], 16)
                        sp.wait_ge(full[r], it + base[r])
                        src = expert_src("w3", it * 2 + r)
                        sp.dma_start(slot(n + 1).rearrange("p (k c) -> p k c", k=KD), src).then_inc(landed[(n + 1) % SLOTS], 16)
                        sp.wait_ge(full[4 + r], it + base[4 + r])
                        src = expert_src("w2", it * 2 + r)
                        sp.dma_start(slot(n + 2).rearrange("p (k c) -> p k c", k=FE // P), src).then_inc(landed[(n + 2) % SLOTS], 16)
                sp.wait_ge(*V("starts_ready", 1))
                most = sp.value_load(starts[0:1, EXPERTS:EXPERTS + 1], min_val=0, max_val=T)
                with sp.If(most > CAP):
                    for n in range(moe_first + 3 * EXPERTS - SLOTS, moe_first + 3 * EXPERTS):
                        sp.wait_ge(*released[n])
                    with sp.Fori(0, EXPERTS) as e:
                        sp.wait_ge(*V("more_y", e * MAX_PASSES + 1))
                        for s, name in enumerate(("w1", "w3", "w2")):
                            src = expert_src(name, e)
                            sp.dma_start(slot(s).rearrange("p (k c) -> p k c", k=src.shape[1]), src)\
                                .then_inc(S("more_landed"), 16)
                    sp.wait_ge(*V("more_y", EXPERTS * MAX_PASSES + 1))
            if phases >= 3:
                for n in range(moe_first + 3 * EXPERTS, len(items)):
                    load(n, *items[n])
            if phases == 3:
                sp.wait_ge(*V("final_scaled", KD))
                result = fm(1)
            else:
                sp.wait_ge(*V("ln1_out" if phases == 1 else "ln2_out", KD))
                result = fm(0)
            sp.dma_start(out.rearrange("(k p) t -> p k t", p=P), result).then_inc(S("stored"), 16)
            sp.wait_ge(*V("stored", 16))


MLA_SCALE = 1.0 / float(np.sqrt(NOPE + ROPE))
DIL_SCALE = 0.125


def silu_block(act_e, act, S, fm, blk):
    act_e.wait_ge(S("conv_done"), blk + 1)
    dst = fm(2 + blk // 8)[:, blk % 8, :]
    act(dst, dst, ACT.Silu, "v_ready" if blk >= 16 else "qk_silu")


def ab_stage(ve, st, S, ab, row, await_full, bc):
    v = await_full(ve, "ab")
    v3 = v[:, 0:32].rearrange("p (b c) -> p b c", b=NB)
    view = lambda c: ab[:, c:c + 16].rearrange("p (b h) -> p b h", b=NB)
    st.do(ve.tensor_tensor(view(144), v3[:, :, 0:8], bc(row("b_a", 8), 1, [P, NB, 8]), ALU.add))
    st.do(ve.tensor_tensor(view(32), v3[:, :, 8:16], bc(row("b_b", 8), 1, [P, NB, 8]), ALU.add), "ab")
    st.settle()
    st.do(ve.tensor_tensor(view(144), view(144), bc(row("dt_bias", 8), 1, [P, NB, 8]), ALU.add))
    st.settle()
    st.do(ve.tensor_scalar(ab[:, 128:144], ab[:, 144:160], -1.0, None, ALU.mult))
    st.settle()
    st.do(ve.tensor_tensor(ab[:, 48:64], ab[:, 128:144], ab[:, 144:160], ALU.max), "ab_ready")


def ab_finish(ve, st, S, ab):
    st.do(ve.tensor_scalar(ab[:, 32:48], ab[:, 32:48], 1.0, None, ALU.add))
    st.do(ve.scalar_tensor_tensor(ab[:, 144:160], ab[:, 144:160], 0.0, ab[:, 48:64], ALU.max, ALU.add))
    st.settle()
    st.do(ve.reciprocal(ab[:, 16:32], ab[:, 32:48]))
    view = lambda c: ab[:, c:c + 16].rearrange("p (b h) -> p b h", b=NB)
    st.do(ve.scalar_tensor_tensor(view(0), view(144), -1.0, ab[:, 64:72].unsqueeze(1).broadcast_to([P, NB, HEADS]),
                                  ALU.mult, ALU.mult), "g_ready")


def lay_out(inputs):
    f = {k: np.asarray(v) for k, v in inputs.items()}
    blocks = lambda v: np.ascontiguousarray(v).reshape(-1, P).T
    b_in = f["b_in"][0]
    ab0 = 6 * D
    main = np.concatenate([b_in[:ab0], b_in[ab0 + 16:]])
    cols = np.concatenate([
        blocks(f["ln_in_g"]), blocks(f["ln_in_b"]), blocks(f["gm_ln_g"]), blocks(f["gm_ln_b"]),
        blocks(f["ln1_g"]), blocks(f["ln1_b"]), blocks(f["ln2_g"]), blocks(f["ln2_b"]),
        blocks(f["attn_norm_2"][0]), blocks(f["attn_norm_2"][1]), blocks(f["ffn_norm_2"][0]),
        blocks(f["ffn_norm_2"][1]), blocks(f["final_norm_2"]), blocks(main), blocks(f["dn_conv_w"][0]),
        blocks(f["dn_norm_w"]), blocks(f["e_q_norm_2"]), blocks(f["e_kv_norm_2"]),
        np.full((P, 1), 1e-5, np.float32), np.full((P, 1), 1e-6, np.float32),
        np.full((P, 1), -0.5 * np.log(float(P)), np.float32)], axis=1)
    rows = np.concatenate([f["dn_a_log"][0], f["dn_dt_bias"][0], b_in[ab0:ab0 + 16], f["b_rg"][0], f["b_re"][0],
                           f["o_sinks_2"][0]])[None, :]
    e_in = f["e_w_in_2"][0]
    swap = lambda w: np.concatenate([w[..., ROPE // 2:], w[..., :ROPE // 2]], axis=-1)
    kr = e_in[:, 384:416]
    e_in = np.concatenate([e_in[:, 0:416], swap(kr), e_in[:, 416:]], axis=1)
    uq = f["e_w_uq_2"][0]
    uq_rope = swap(uq.reshape(MLA_Q, HEADS, 96)[:, :, NOPE:]).reshape(MLA_Q, HEADS * ROPE)
    uq = np.concatenate([uq, uq_rope], axis=1).reshape(2, P, D).transpose(1, 0, 2).reshape(P, 2 * D)
    ukv = f["e_w_ukv_2"][0].reshape(MLA_KV, HEADS, 2, NOPE).transpose(0, 2, 1, 3).reshape(MLA_KV, D)
    pairs = lambda w: w.reshape(2, HEADS, 64, -1).transpose(1, 0, 2, 3).reshape(w.shape)
    o_in = f["o_w_qkv_2"][0]
    o_in = np.concatenate([pairs(np.ascontiguousarray(o_in[:, :D].T)).T, o_in[:, D:]], axis=1)

    def ffn(layer):
        gu = f["f_w_gate_up_2"][layer].reshape(KD, P, 2, FF_BLOCKS, P).transpose(3, 1, 0, 2, 4)
        down = f["f_w_down_2"][layer].reshape(FF_BLOCKS, P, D)
        return np.concatenate([gu.reshape(FF_BLOCKS, P, 2 * KD * P), down], axis=2)

    return {
        "xT": f["x"][0].T, "cols": cols, "rows": rows,
        "w_in": f["w_in"][0], "w_ab": f["w_in"][0][:, ab0:ab0 + 16],
        "w_s": f["gm_w_s"][0].transpose(0, 2, 1), "b_s": f["gm_b_s"][0].reshape(1, -1),
        "w_pa": f["w_pa"][0], "w_pb": f["w_pb"][0], "w_o": f["w_o"][0],
        "w_router": np.concatenate([f["w_rg"][0], f["w_re"][0]], axis=1),
        "w1": f["w1"][0], "w3": f["w3"][0], "w2": f["w2"][0],
        "e_in": e_in, "mla_up": np.concatenate([uq, ukv], axis=1), "e_out": f["e_w_out_2"][0],
        "o_in": o_in, "o_out": pairs(f["o_w_out_2"][0]), "ffn0": ffn(0), "ffn1": ffn(1),
    }


def kernel(phases=3, **inputs):
    import concourse.bacc as bacc
    from concourse.bass_utils import run_bass_kernel_spmd

    nc = bacc.Bacc("TRN2", target_bir_lowering=False, num_devices=1)
    arrays, io = {}, {}
    for name, a in {**lay_out(inputs), **shape_tables()}.items():
        arrays[f"in_{name}"] = np.ascontiguousarray(a)
        io[name] = nc.dram_tensor(f"in_{name}", a.shape, mybir.dt.from_np(a.dtype), kind="ExternalInput").ap()
    out = nc.dram_tensor("out", (D, T), F32, kind="ExternalOutput").ap()
    build(nc, io, out, phases)
    got = run_bass_kernel_spmd(nc, [arrays], core_ids=[0]).results[0]["out"]
    return np.ascontiguousarray(got.T)[None]
```

```python
from contextlib import ExitStack

import numpy as np

import concourse.bass as bass
from concourse import mybir

F32 = mybir.dt.float32
F16 = mybir.dt.float16
I32 = mybir.dt.int32
U32 = mybir.dt.uint32
F32R = mybir.dt.float32r
ALU = mybir.AluOpType
ACT = mybir.ActivationFunctionType
AX = mybir.AxisListType

P = 128
T = 256
NB = T // P
D = 1024
KD = D // P
HEADS = 8
CHUNK = 64
UNITS = HEADS * NB
EXPERTS = 32
GROUPS = 4
FE = 512
CAP = 64
MAX_PASSES = T // CAP
ASSIGN = 2 * T
SORTED = ASSIGN + MAX_PASSES * CAP
D_FF = 2816
FF_BLOCKS = D_FF // P
MLA_Q, MLA_KV, NOPE, ROPE, VDIM = 256, 128, 64, 32, 64
SWA_HEADS = 16
ALPHA = 2.0 ** 0.25
NEG = -1e30
NORMS = {"ln_in": KD, "gm": KD, "ln1": KD, "ln2": KD, "att0": KD, "cqn": 2, "ckvn": 1, "ffn0n": KD,
         "att1": KD, "ffn1n": KD, "final": KD}
LAYER_NORMS = ("ln_in", "gm", "ln1", "ln2")
SECTIONS = {"mla": HEADS, "dil": HEADS, "swa": SWA_HEADS}

SLOTS = 6
MIXER_PAIRS = 40
MIXER_SLOTS = 4
SLOT = 4096
PAGES = 13
PAGE = KD * T
BANK = 512

COLS = {}
_at = 0
for _name, _n in (("ln_in_g", 8), ("ln_in_b", 8), ("gm_g", 8), ("gm_b", 8), ("ln1_g", 8), ("ln1_b", 8),
                  ("ln2_g", 8), ("ln2_b", 8), ("att0", 8), ("att1", 8), ("ffn0", 8), ("ffn1", 8),
                  ("final", 8), ("b_in", 64), ("conv", 96), ("dn_norm", 1), ("q_norm", 2),
                  ("kv_norm", 1), ("eps5", 1), ("eps6", 1), ("qscale", 1)):
    COLS[_name] = _at
    _at += _n
NCOLS = _at
ROWS = {"a_log": 0, "dt_bias": 8, "b_a": 16, "b_b": 24, "b_router": 32, "sinks": 68}
NROWS = 84
TABLES = ("identity", "ones", "cumulate", "before")
MASKS = ("strict_low", "incl_up", "first", "first_t", "level2", "level4", "level8", "level16", "level32")
N_ROUTER = KD * 36 + ASSIGN + 64
SPAN = P + T


def shape_tables():
    i = np.arange(P)[:, None]
    j = np.arange(P)[None, :]
    same = i // CHUNK == j // CHUNK
    f32 = [np.eye(P), np.ones((P, P)), same & (i <= j), i < j]
    masks = [same & (i > j), same & (i <= j)]
    level = lambda s: (i // (2 * s) == j // (2 * s)) & (i // s % 2 == 1) & (j // s % 2 == 0)
    masks += [level(1), level(1).T] + [level(s) for s in (2, 4, 8, 16, 32)]
    experts = np.arange(EXPERTS)
    iota = np.concatenate([np.arange(ASSIGN), experts, experts // (EXPERTS // GROUPS)])
    dist = np.concatenate([i - j, i - j + P, i - j], axis=1)
    mult = sum(((dist >= 0) & (dist <= w) & (dist % r == 0)).astype(int) for w, r in ((128, 1), (512, 4), (2048, 16)))
    dil = np.where(mult > 0, -dist, NEG)
    swa = np.where((dist >= 0) & (dist < 128), -dist, NEG)
    causal = np.where(dist >= 0, 0, NEG)
    ang = np.arange(T)[None, :] * (10000.0 ** (-np.arange(0, ROPE, 2) / ROPE))[:, None]
    cos = np.zeros((P, T))
    sin = np.zeros((P, T))
    cos[NOPE:NOPE + ROPE] = np.concatenate([np.cos(ang), np.cos(ang)])
    sin[NOPE:NOPE + ROPE] = np.concatenate([-np.sin(ang), np.sin(ang)])
    return {
        "c_tables": np.concatenate(f32, axis=1).astype(np.float32),
        "c_masks": np.concatenate(masks, axis=1).astype(np.float16),
        "c_iota": np.tile(iota[None, :], (P, 1)).astype(np.float32),
        "c_attn": np.concatenate([dil, mult, swa, causal, cos, sin], axis=1).astype(np.float32),
    }


def stream_items():
    items = []
    for part in ("gm_v", "gm_u", "gate_a"):
        items += [(part, 0), (part, 1)]
    items += [("w_pa", 0), ("w_pa", 1)]
    for part in ("dn_q", "dn_k", "dn_v", "dn_z", "gate_b"):
        items += [(part, 0), (part, 1)]
    items += [("w_pb", 0), ("w_pb", 1), ("w_o", 0), ("w_o", 1)]
    before = len(items)
    for e in range(EXPERTS):
        items += [("w1", e), ("w3", e), ("w2", e)]
    items += [("e_in", n) for n in range(4)] + [("mla_up", 0), ("e_out", 0), ("e_out", 1)]
    items += [("ffn0", j) for j in range(FF_BLOCKS)]
    items += [("o_in", 0), ("o_in", 1), ("o_kv", 0), ("o_out", 0), ("o_out", 1)]
    items += [("ffn1", j) for j in range(FF_BLOCKS)]
    return items, before


def build(nc, io, out, phases=3):
    items, moe_first = stream_items()
    item_no = {it: n for n, it in enumerate(items)}
    with ExitStack() as ctx:
        sb = lambda name, shape, dt=F32: ctx.enter_context(nc.sbuf_tensor(name, shape, dt))
        sems = {}

        def shared(name):
            owner, _, kind = name.partition("_") if not name.startswith("ln_in") else ("ln_in", "", name[6:])
            if owner in NORMS:
                size = {"squared": lambda n: 4 if n == KD else 1, "centered": lambda n: 4, "rstd": lambda n: 1,
                        "scaled": lambda n: n, "out": lambda n: n}.get(kind)
                if size is None:
                    return name, 0
                named = [n for n in NORMS if kind not in ("centered", "out") or n in LAYER_NORMS]
                return f"norm_{kind}", sum(size(NORMS[n]) for n in named[:named.index(owner)])
            if owner in SECTIONS and kind in ("probs", "pT", "max", "exp", "o_ready"):
                before = sum(list(SECTIONS.values())[:list(SECTIONS).index(owner)]) // 2
                return f"heads_{kind}", before
            return name, 0

        def S(name):
            name = shared(name)[0]
            if name not in sems:
                sems[name] = ctx.enter_context(nc.semaphore(name))
            return sems[name]

        def V(name, n):
            return S(name), shared(name)[1] + n

        ring_at = -(-nc.sbuf_base // 32) * 32
        ring = sb("ring", [P, SLOTS * SLOT])
        pages_at = -(-nc.sbuf_base // 32) * 32
        pages = sb("pages", [P, PAGES * PAGE])
        tables = sb("tables", [P, len(TABLES) * P])
        masks = sb("masks", [P, len(MASKS) * P], F16)
        cols = sb("cols", [P, NCOLS])
        rows = sb("rows", [P, NROWS])
        ab = sb("ab", [P, 16 * 12])
        starts = sb("starts", [1, EXPERTS + 2], I32)
        psum = ctx.enter_context(nc.psum_tensor("psum", [P, 8, BANK], F32))

        def table(name):
            n = TABLES.index(name)
            return tables[:, n * P:(n + 1) * P]

        def mask(name):
            n = MASKS.index(name)
            return masks[:, n * P:(n + 1) * P]

        def page(n, count=1):
            return pages[:, n * PAGE:(n + count) * PAGE]

        def fm(n):
            return page(n).rearrange("p (k t) -> p k t", t=T)

        def units(n):
            return page(n).rearrange("p (u t) -> p u t", t=P)

        def col(name, k=0):
            c = COLS[name] + k
            return cols[:, c:c + 1]

        def row(name, n):
            return rows[:, ROWS[name]:ROWS[name] + n]

        def slot_no(n):
            return n % MIXER_SLOTS if n < moe_first else (n - moe_first) % SLOTS

        def nth_landing(n):
            before = [m for m in range(moe_first) if m % MIXER_SLOTS == slot_no(n) and m <= n]
            return len(before) + (0 if n < moe_first else (n - moe_first) // SLOTS + 1)

        def slot(n, floats=SLOT):
            s = slot_no(n)
            return ring[:, s * SLOT:s * SLOT + floats]

        ident, ones = table("identity"), table("ones")
        full = [S(f"bank{b}_full") for b in range(8)]
        free = [S(f"bank{b}_free") for b in range(8)]
        landed = [S(f"slot{s}_landed") for s in range(SLOTS)]
        uses = [0] * 8
        place = {}
        released = {}

        def bank_of(name, use=0):
            return psum[:, place[name][0], :]

        def await_full(eng, name):
            b, n = place[name]
            eng.wait_ge(full[b], n)
            return psum[:, b, :]

        def empty(ins, name):
            ins.then_inc(free[place[name][0]], 1)

        probs = page(6, 2)[:, 0:6 * SPAN].rearrange("p (n h s) -> p n h s", n=3, h=2)
        probs_t = page(6, 2)[:, 6 * SPAN:10 * SPAN].rearrange("p (n h s) -> p n h s", n=2, h=2)
        stats = page(6, 2)[:, 10 * SPAN:10 * SPAN + 3 * 12].rearrange("p (n w h b) -> p n w h b", n=3, w=3, h=2)
        NEG_MAX, TOTAL, SINK_EXP = range(3)

        def part(name, start, size):
            return nc.alloc_sbuf_tensor_at(name, [P, size], F32R, offset=pages_at + 4 * start)[:]

        x_part = {"hi": part("x_hi", 9 * PAGE, PAGE).rearrange("p (k t) -> p k t", t=T),
                  "lo": part("x_lo", PAGE, PAGE).rearrange("p (k t) -> p k t", t=T)}
        gu_size, down_size = 2 * KD * P, KD * P
        gu_part = {"hi": [part(f"gu_hi{b}", 3 * PAGE + 2 * b * gu_size, gu_size) for b in range(2)],
                   "lo": [part(f"gu_lo{b}", 3 * PAGE + (2 * b + 1) * gu_size, gu_size) for b in range(2)]}
        down_part = {"hi": [part(f"down_hi{b}", 7 * PAGE + 2 * b * down_size, down_size) for b in range(2)],
                     "lo": [part(f"down_lo{b}", 7 * PAGE + (2 * b + 1) * down_size, down_size) for b in range(2)]}
        hidden = page(12)[:, 2 * T:5 * T].rearrange("p (r t) -> p r t", t=T)
        hidden_part = {"hi": part("hidden_hi", 2 * PAGE, 3 * T).rearrange("p (r t) -> p r t", t=T),
                       "lo": part("hidden_lo", 12 * PAGE + 5 * T, 3 * T).rearrange("p (r t) -> p r t", t=T)}
        PARTS = (("hi", "hi"), ("hi", "lo"), ("lo", "hi"))

        def ring_part(name, start, size):
            return nc.alloc_sbuf_tensor_at(name, [P, size], F32R, offset=ring_at + 4 * start)[:]

        slot_low = [ring_part(f"slot_lo{n}", n * SLOT, SLOT) for n in range(SLOTS)]
        mix_high = ring_part("mix_hi", MIXER_SLOTS * SLOT, SLOT)
        h_part = {p_: ring_part(f"h_{p_}", (MIXER_SLOTS + 1) * SLOT + n * PAGE, PAGE).rearrange("p (k t) -> p k t", t=T)
                  for n, p_ in enumerate(("hi", "lo"))}
        htm_part = {"hi": part("htm_hi", PAGE, PAGE), "lo": part("htm_lo", 5 * PAGE, PAGE)}
        onehot = part("onehot", 8 * PAGE, NB * ASSIGN).rearrange("p (b s) -> p b s", b=NB)
        split_pairs = []
        page_high = {n: part(f"w_hi{n}", n * PAGE, PAGE).rearrange("p (k c) -> p k c", k=KD) for n in (1, 2, 3, 4, 5)}
        page_part = {n: part(f"in{n}", n * PAGE, PAGE).rearrange("p (k t) -> p k t", t=T) for n in (1, 2, 3, 4, 6, 8, 9)}

        def pair_of(ap, pair):
            return ap.rearrange("p (k c) -> p k c", k=KD)[:, :, 2 * P * pair:2 * P * pair + 2 * P]

        class LayerSteps:

            def __init__(self, layer, it=None):
                self.layer, self.it = layer, it

            def at(self, n, each):
                return n if self.it is None else self.it * each + n

            def landed(self, eng, n):
                eng.wait_ge(landed[slot_no(n)], self.at(16 * nth_landing(n), 16))

            def bank(self, eng, sem, base, j, extra):
                eng.wait_ge(sem[j % 3], self.at(base[j % 3] + j // 3 + extra, 2))

            def step(self, eng, name, j):
                eng.wait_ge(S(name), self.at(self.layer * FF_BLOCKS + j + 1, 6))

        class Steps:

            def __init__(self, eng, name):
                self.eng, self.sem, self.n, self.last = eng, S(name), 0, None
                self.counts = {}

            def do(self, ins, name=None):
                if name is None:
                    self.n += 1
                    ins.then_inc(self.sem, 1)
                    self.last = (self.sem, self.n)
                elif name in place:
                    empty(ins, name)
                    self.last = (free[place[name][0]], place[name][1])
                else:
                    own = shared(name)[0]
                    self.counts[own] = self.counts.get(own, 0) + 1
                    ins.then_inc(S(name), 1)
                    self.last = (S(name), self.counts[own])

            def settle(self):
                self.eng.wait_ge(*self.last)

        PROJ_BANKS = (0, 1, 2, 3)

        block = ctx.enter_context(nc.Block())

        @block.tensor
        def _(pe):
            turn = [0]

            def take(name, bank=None):
                if bank is None:
                    bank = PROJ_BANKS[turn[0] % len(PROJ_BANKS)]
                    turn[0] += 1
                if uses[bank]:
                    pe.wait_ge(free[bank], uses[bank])
                uses[bank] += 1
                place[name] = (bank, uses[bank])
                return psum[:, bank, :]

            def give(ins, name):
                ins.then_inc(full[place[name][0]], 1)

            def weights(item):
                n = item_no[item]
                pe.wait_ge(landed[slot_no(n)], 16 * nth_landing(n))
                return slot(n)

            def release(item, name):
                released[item_no[item]] = (full[place[name][0]], place[name][1])

            def mm(o, lhsT, rhs, start, stop):
                return pe.matmul(o, lhsT, rhs, start=start, stop=stop, skip_group_check=True)

            def project(part, rhs, item_names):
                for n, item in enumerate(item_names):
                    w = weights(item).rearrange("p (k c) -> p k c", k=KD)
                    for pair in range(2):
                        name = f"{part}{2 * n + pair}"
                        o = take(name)
                        for half in range(2):
                            c = (2 * pair + half) * P
                            for k in range(KD):
                                last = mm(o[:, half * T:(half + 1) * T], w[:, k, c:c + P], rhs[:, k, :],
                                          k == 0, k == KD - 1)
                        give(last, name)
                    release(item, name)

            def project_split(part, item_names, highs=None, x=h_part, x_no=None):
                for i, item in enumerate(item_names):
                    for pair in range(2):
                        name = f"{part}{2 * i + pair}"
                        high = page_high[highs[pair]] if highs else pair_of(mix_high, pair)
                        split_pairs.append((name, item, pair, high))
                        pe.wait_ge(S("w_split"), len(split_pairs))
                        o = take(name)
                        w = {"hi": high, "lo": pair_of(slot_low[slot_no(item_no[item])], pair)}
                        for half in range(2):
                            for k in range(KD):
                                if x_no is not None and i + pair + half == 0 and k % 2 == 0:
                                    pe.wait_ge(S("h_split"), 4 * x_no + k // 2 + 1)
                                for n, (wp, xp) in enumerate(PARTS):
                                    last = mm(o[:, half * T:(half + 1) * T], w[wp][:, k, half * P:(half + 1) * P],
                                              x[xp][:, k, :], k == 0 and n == 0, k == KD - 1 and n == 2)
                        give(last, name)
                    release(item, name)

            def column_sums(name, src, nblocks, ready=None):
                o = take(name)
                for k in range(nblocks):
                    if ready and k % 2 == 0:
                        ready(k // 2)
                    last = mm(o[:, 0:T], ones, src[:, k, :], k == 0, k == nblocks - 1)
                give(last, name)

            def norm(nm, src, squares, nblocks, mean, before=None):
                if mean:
                    column_sums(f"{nm}_mu", src, nblocks, before)
                column_sums(f"{nm}_var", squares, nblocks, lambda i: pe.wait_ge(*V(f"{nm}_squared", i + 1)))

            def transposes(name, srcs, bank=None):
                o = take(name, bank)
                for j, s in enumerate(srcs):
                    last = pe.transpose(o[:, j * P:(j + 1) * P], s, ident)
                give(last, name)

            pe.wait_ge(*V("x_landed", 16 * 3))
            norm("ln_in", fm(1), fm(2), KD, True)
            h = fm(0)
            project_split("gm_v", [("gm_v", 0), ("gm_v", 1)], x_no=0)
            project_split("gm_u", [("gm_u", 0), ("gm_u", 1)])
            pe.wait_ge(*V("gm_v_ready", 4))
            column_sums("gm_mu", fm(2), KD)
            project_split("gate_a", [("gate_a", 0)])
            column_sums("gm_var", fm(4), KD, lambda i: pe.wait_ge(*V("gm_squared", i + 1)))
            project_split("gate_a_", [("gate_a", 1)])
            for b in range(NB):
                for half in range(2):
                    pe.wait_ge(*V("gm_out", 4 * half + 4))
                    transposes(f"gm_t{b}{half}", [fm(2)[:, 4 * half + j, b * P:(b + 1) * P] for j in range(4)])
            pe.wait_ge(*V("gate_masked", 1))
            pe.wait_ge(*V("mixer_landed", 16 * 5))
            vtm = page(4).rearrange("p (b c) -> p b c", b=NB)
            wgt = page(3)[:, 0:KD * P].rearrange("p (g t) -> p g t", t=P)
            pe.wait_ge(*V("gm_vtm", 4))
            for g2 in range(KD // 2):
                o = take(f"spatial{g2}")
                for half in range(2):
                    g = 2 * g2 + half
                    for b in range(NB):
                        dst = o[:, half * T + b * P:half * T + (b + 1) * P]
                        mm(dst, vtm[:, b, g * P:(g + 1) * P], wgt[:, g, :], True, False)
                        last = mm(dst, ones[0:1, :], page(3)[0:1, KD * P + g * P:KD * P + (g + 1) * P], False, True)
                give(last, f"spatial{g2}")
            pe.wait_ge(*V("ya_ready", 4))
            project("w_pa", fm(5), [("w_pa", 0), ("w_pa", 1)])
            project_split("dn_q", [("dn_q", 0), ("dn_q", 1)])
            project_split("dn_k", [("dn_k", 0), ("dn_k", 1)])
            o = take("ab")
            wab = ab[:, 0:P].rearrange("p (k c) -> p k c", k=KD)
            for b in range(NB):
                for k in range(KD):
                    last = mm(o[:, b * 16:(b + 1) * 16], h[:, k, b * P:(b + 1) * P], wab[:, k, :], k == 0, k == KD - 1)
            give(last, "ab")
            project_split("dn_v", [("dn_v", 0), ("dn_v", 1)])
            pe.wait_ge(*V("g_ready", 1))
            g_tm = ab[:, 0:16]
            o = take("G")
            give(mm(o[:, 0:16], table("cumulate"), g_tm, True, True), "G")
            for q4 in range(4):
                o = take(f"Gb{q4}", 4 + q4)
                for j in range(4):
                    u = 4 * q4 + j
                    hd, b = u // NB, u % NB
                    c = b * HEADS + hd
                    last = mm(o[:, j * P:(j + 1) * P], g_tm[:, c:c + 1].broadcast_to([P, P]), table("cumulate"), True, True)
                give(last, f"Gb{q4}")
            project_split("dn_z", [("dn_z", 0)])
            for part, pg in (("q", 7), ("k", 8)):
                for q4 in range(4):
                    pe.wait_ge(*V(f"{part}_squared", q4 + 1))
                    name = f"{part}_ss{q4}"
                    o = take(name)
                    for half in range(2):
                        last = mm(o[:, half * T:(half + 1) * T], ones, fm(pg)[:, 2 * q4 + half, :], True, True)
                    give(last, name)
            project_split("dn_z_", [("dn_z", 1)])
            for q4 in range(4):
                pe.wait_ge(*V("k_normed", q4 + 1))
                transposes(f"k_t{q4}", [units(3)[:, 4 * q4 + j, :] for j in range(4)])
                pe.wait_ge(*V("v_ready", 2 * q4 + 2))
                transposes(f"v_t{q4}", [units(4)[:, 4 * q4 + j, :] for j in range(4)])
            for q4 in range(4):
                name = f"kk{q4}"
                o = take(name, 4 + q4)
                for j in range(4):
                    k = units(3)[:, 4 * q4 + j, :]
                    last = mm(o[:, j * P:(j + 1) * P], k, k, True, True)
                give(last, name)
            for q4 in range(4):
                name = f"qk{q4}"
                pe.wait_ge(*V("q_normed", q4 + 1))
                o = take(name)
                for j in range(4):
                    u = 4 * q4 + j
                    last = mm(o[:, j * P:(j + 1) * P], units(3)[:, u, :], units(2)[:, u, :], True, True)
                give(last, name)
            for q4 in range(4):
                pe.wait_ge(*V("L_ready", q4 + 1))
                transposes(f"L_t{q4}", [units(11)[:, 4 * q4 + j, :] for j in range(4)], 4 + q4)
            X, XT, Y, LT = units(5), units(4), units(9), units(12)
            for lv in range(5):
                for q4 in range(4):
                    pe.wait_ge(*V("X_ready", 4 * lv + q4 + 1))
                    name = f"Y{lv}_{q4}"
                    o = take(name, 4 + q4)
                    for j in range(4):
                        u = 4 * q4 + j
                        last = mm(o[:, j * P:(j + 1) * P], LT[:, u, :], X[:, u, :], True, True)
                    give(last, name)
                for q4 in range(4):
                    pe.wait_ge(*V("Y_ready", 4 * lv + q4 + 1))
                    name = f"ZT{lv}_{q4}"
                    o = take(name, q4)
                    for j in range(4):
                        u = 4 * q4 + j
                        last = mm(o[:, j * P:(j + 1) * P], Y[:, u, :], XT[:, u, :], True, True)
                    give(last, name)
                    if lv < 4:
                        name = f"Z{lv}_{q4}"
                        o = take(name, 4 + q4)
                        for j in range(4):
                            u = 4 * q4 + j
                            last = mm(o[:, j * P:(j + 1) * P], XT[:, u, :], Y[:, u, :], True, True)
                        give(last, name)
            pe.wait_ge(*V("XT_final", 4))
            pe.wait_ge(*V("vb_ready", 1))
            for q4 in range(4):
                name = f"uc{q4}"
                o = take(name, 4 + q4)
                for j in range(4):
                    u = 4 * q4 + j
                    last = mm(o[:, j * P:(j + 1) * P], XT[:, u, :], units(8)[:, u, :], True, True)
                give(last, name)
            pe.wait_ge(*V("kbg_ready", 1))
            for q4 in range(4):
                name = f"wc{q4}"
                o = take(name, q4)
                for j in range(4):
                    u = 4 * q4 + j
                    last = mm(o[:, j * P:(j + 1) * P], units(3)[:, u, :], XT[:, u, :], True, True)
                give(last, name)
            state = page(5)[:, 0:HEADS * P].rearrange("p (h d) -> p h d", d=P)
            vnew, wT, qd, aT, kdec = units(11), units(12), units(2), units(10), units(7)
            pe.wait_ge(*V("wc_ready", 4))
            pe.wait_ge(*V("qd_ready", 1))
            pe.wait_ge(*V("kdec_ready", 1))
            for c in range(T // CHUNK):
                b, r = c // 2, CHUNK * (c % 2)
                if c > 0:
                    pe.wait_ge(*V("state_ready", c))
                    for hh in range(2):
                        name = f"ws{c}_{hh}"
                        o = take(name, 4 + hh)
                        for j in range(4):
                            hd = 4 * hh + j
                            last = mm(o[r:r + CHUNK, j * P:(j + 1) * P], wT[:, hd * NB + b, r:r + CHUNK],
                                      state[:, hd, :], True, True)
                        give(last, name)
                pe.wait_ge(*V("vnew_ready", 2 * c + 2))
                if c < T // CHUNK - 1:
                    for hh in range(2):
                        name = f"ds{c}_{hh}"
                        o = take(name, 6 + hh)
                        for j in range(4):
                            u = (4 * hh + j) * NB + b
                            last = mm(o[:, j * P:(j + 1) * P], kdec[r:r + CHUNK, u, :], vnew[r:r + CHUNK, u, :], True, True)
                        give(last, name)
                name = f"o{c}"
                o = take(name)
                for hd in range(HEADS):
                    u = hd * NB + b
                    dst = o[:, hd * CHUNK:(hd + 1) * CHUNK]
                    if c > 0:
                        mm(dst, state[:, hd, :], qd[:, u, r:r + CHUNK], True, False)
                    last = mm(dst, vnew[r:r + CHUNK, u, :], aT[r:r + CHUNK, u, r:r + CHUNK], c == 0, True)
                give(last, name)
                if c in (0, 1):
                    project_split(f"gate_b{'_' * c}", [("gate_b", c)])
            for q4 in range(4):
                pe.wait_ge(*V("o_squared", q4 + 1))
                name = f"o_ss{q4}"
                o = take(name)
                for half in range(2):
                    last = mm(o[:, half * T:(half + 1) * T], ones, fm(3)[:, 2 * q4 + half, :], True, True)
                give(last, name)
            project_split("w_pb", [("w_pb", 0), ("w_pb", 1)], None, {"hi": page_part[2], "lo": page_part[4]}, 1)
            project_split("w_o", [("w_o", 0), ("w_o", 1)], None, {"hi": page_part[3], "lo": page_part[1]}, 2)
            norm("ln1", fm(0), fm(2), KD, True, lambda i: pe.wait_ge(*V("res1", i + 1)))
            if phases < 2:
                return

            pe.wait_ge(*V("router_landed", 32))
            h = fm(0)
            wr = page(10)[:, 0:KD * 36].rearrange("p (k c) -> p k c", k=KD)
            o = take("router")
            for b in range(NB):
                for k in range(KD):
                    if b == 0:
                        pe.wait_ge(*V("ln1_out", k + 1))
                    last = mm(o[:, b * 36:(b + 1) * 36], h[:, k, b * P:(b + 1) * P], wr[:, k, :], k == 0, k == KD - 1)
            give(last, "router")
            for b in range(NB):
                for half in range(2):
                    transposes(f"h_t{b}{half}", [h[:, 4 * half + j, b * P:(b + 1) * P] for j in range(4)])
            pick = page(11)[:, 512:576].rearrange("p (b e) -> p b e", b=NB)
            pe.wait_ge(*V("picked", 1))
            o = take("rank", 4)
            mm(o[:, 0:32], table("before"), pick[:, 0, :], True, True)
            mm(o[:, 32:64], ones, pick[:, 0, :], True, False)
            mm(o[:, 32:64], table("before"), pick[:, 1, :], False, True)
            mm(o[:, 64:96], ones, pick[:, 0, :], True, False)
            mm(o[:, 64:96], ones, pick[:, 1, :], False, True)
            mm(o[0:EXPERTS, 96:97], pick[:, 0, :], ones[:, 0:1], True, False)
            give(mm(o[0:EXPERTS, 96:97], pick[:, 1, :], ones[:, 0:1], False, True), "rank")
            pe.wait_ge(*V("counts_spread", 1))
            o = take("start", 5)
            give(mm(o[:, 0:EXPERTS], page(11)[0:EXPERTS, 640:640 + P], table("before")[0:EXPERTS, 0:EXPERTS], True, True), "start")
            gated = page(8)[:, NB * ASSIGN:2 * NB * ASSIGN].rearrange("p (b s) -> p b s", b=NB)
            htm = {p_: htm_part[p_].rearrange("p (b c) -> p b c", b=NB) for p_ in ("hi", "lo")}
            pe.wait_ge(*V("onehot_ready", NB))
            for k in range(KD):
                name = f"xs{k}"
                o = take(name)
                for b in range(NB):
                    for p_ in ("hi", "lo"):
                        last = mm(o, htm[p_][:, b, k * P:(k + 1) * P], onehot[:, b, :], b == 0 and p_ == "hi",
                                  b == NB - 1 and p_ == "lo")
                give(last, name)
            pe.wait_ge(*V("gated_ready", NB))
            for b in range(NB):
                transposes(f"gt{b}", [gated[:, b, s * P:(s + 1) * P] for s in range(4)])

            xe = page(9)[:, 1024:2048].rearrange("p (r k s) -> p r k s", r=2, k=KD)
            act = page(10)[:, 1536:2048].rearrange("p (r s) -> p r s", r=2)
            actT = page(8)[:, 1024:1536].rearrange("p (r s) -> p r s", r=2)
            yrow = page(8)[:, 0:1024].rearrange("p (r s) -> p r s", r=2)

            def expert_h(r, w, half):
                w = w.rearrange("p (k c) -> p k c", k=KD)
                for k in range(KD):
                    for g in range(2):
                        last = mm(psum[g * CAP:(g + 1) * CAP, r, half * T:(half + 1) * T], xe[:, r, k, :],
                                  w[:, k, g * T:(g + 1) * T], k == 0, k == KD - 1)
                return last

            def expert_t(r):
                for c in range(2):
                    last = pe.transpose(psum[:, 2 + r, c * P:(c + 1) * P], act[:, r, c * P:(c + 1) * P], ident)
                return last

            def expert_y(r, w2):
                w = w2.rearrange("p (f c) -> p f c", c=D)
                for f in range(FE // P):
                    for g in range(2):
                        a = (f % 2) * P + (f // 2) * CAP
                        last = mm(psum[g * CAP:(g + 1) * CAP, 4 + r, :], actT[:, r, a:a + CAP],
                                  w[:, f, g * 512:(g + 1) * 512], f == 0, f == FE // P - 1)
                return last

            def expert_z(r):
                for c in range(4):
                    last = pe.transpose(psum[:, 6 + r, c * P:(c + 1) * P], yrow[:, r, c * P:(c + 1) * P], ident)
                return last

            pe.wait_ge(*V("starts_ready", 1))
            base = list(uses)
            place["moe_base"] = tuple(base)
            with pe.Fori(0, EXPERTS // 2) as it:
                land = lambda n: pe.wait_ge(landed[slot_no(n)], it * 16 + 16 * nth_landing(n))
                for r in range(2):
                    n = moe_first + 3 * r
                    pe.wait_ge(free[r], it + base[r])
                    pe.wait_ge(*V("xe_ready", it * 2 + r + 1))
                    land(n)
                    expert_h(r, slot(n), 0).then_inc(S("w1_read"), 1)
                    land(n + 1)
                    expert_h(r, slot(n + 1), 1).then_inc(full[r], 1)
                for r in range(2):
                    pe.wait_ge(free[2 + r], it + base[2 + r])
                    pe.wait_ge(free[r], it + base[r] + 1)
                    expert_t(r).then_inc(full[2 + r], 1)
                for r in range(2):
                    pe.wait_ge(free[4 + r], it + base[4 + r])
                    pe.wait_ge(free[2 + r], it + base[2 + r] + 1)
                    land(moe_first + 3 * r + 2)
                    expert_y(r, slot(moe_first + 3 * r + 2)).then_inc(full[4 + r], 1)
                for r in range(2):
                    pe.wait_ge(free[6 + r], it + base[6 + r])
                    pe.wait_ge(free[4 + r], it + base[4 + r] + 1)
                    expert_z(r).then_inc(full[6 + r], 1)
            for b in range(8):
                uses[b] += EXPERTS // 2
            for r in range(2):
                n = moe_first + 3 * (EXPERTS - 2 + r)
                released[n] = (S("w1_read"), EXPERTS - 1 + r)
                released[n + 1] = (full[r], uses[r])
                released[n + 2] = (full[4 + r], uses[4 + r])
            most = pe.value_load(starts[0:1, EXPERTS:EXPERTS + 1], min_val=0, max_val=T)
            for b in range(8):
                pe.wait_ge(free[b], uses[b])
            with pe.If(most > CAP):
                pe.sem_inc(S("more_y"), 1)
                with pe.Fori(0, EXPERTS) as e:
                    pe.wait_ge(*V("more_landed", e * 48 + 48))
                    for c in range(MAX_PASSES):
                        n = e * MAX_PASSES + c + 1
                        pe.wait_ge(*V("more_xe", n))
                        expert_h(0, slot(0), 0)
                        expert_h(0, slot(1), 1).then_inc(S("more_h"), 1)
                        pe.wait_ge(*V("more_act", n))
                        expert_t(0).then_inc(S("more_t"), 1)
                        pe.wait_ge(*V("more_actT", n))
                        expert_y(0, slot(2)).then_inc(S("more_y"), 1)
                        pe.wait_ge(*V("more_yrow", n))
                        pe.wait_ge(*V("more_out", n))
                        expert_z(0).then_inc(S("more_z"), 1)
            ys = page(5, 3).rearrange("p (k s) -> p k s", k=KD)
            pe.wait_ge(*V("experts_done", 1))
            for s in range(4):
                for half in range(2):
                    transposes(f"y_t{s}{half}", [ys[:, 4 * half + j, s * P:(s + 1) * P] for j in range(4)])
            ytm = page(11, 2).rearrange("p (s c) -> p s c", s=4)
            gt = page(9)[:, 0:4 * T].rearrange("p (s t) -> p s t", t=T)
            pe.wait_ge(*V("ytm_ready", 8))
            pe.wait_ge(*V("gt_ready", 2))
            for m in range(4):
                name = f"moe{m}"
                o = take(name)
                for half in range(2):
                    k = 2 * m + half
                    for s in range(4):
                        last = mm(o[:, half * T:(half + 1) * T], ytm[:, s, k * P:(k + 1) * P], gt[:, s, :], s == 0, s == 3)
                give(last, name)
            norm("ln2", fm(0), fm(2), KD, True, lambda i: pe.wait_ge(*V("res2", i + 1)))
            if phases < 3:
                return

            def rms(nm, src, squares, nblocks=KD):
                norm(nm, src, squares, nblocks, False)

            def score(name, pairs):
                o = take(name)
                q, k = pairs
                mm(o[:, 0:P], q[:, 0:P], k[:, 0:P], True, True)
                give(mm(o[:, P:SPAN], q[:, P:T], k, True, True), name)

            def attend(sec, nheads, operands, values):
                pairs = nheads // 2

                def scores(n):
                    for h2 in range(2):
                        score(f"{sec}s{2 * n + h2}", operands(2 * n + h2))

                scores(0)
                for i in range(pairs + 2):
                    if i + 1 < pairs:
                        scores(i + 1)
                    if i >= 2:
                        n = i - 2
                        pe.wait_ge(*V(f"{sec}_pT", n + 1))
                        o = take(f"{sec}o{n}", 6 + n % 2)
                        for h2 in range(2):
                            g = 2 * n + h2
                            dst = o[VDIM * h2:VDIM * h2 + VDIM, :]
                            pT = probs_t[:, n % 2, h2, :]
                            mm(dst[:, 0:P], values(g, 0), pT[:, 0:P], True, True)
                            mm(dst[:, P:T], values(g, 0), pT[:, P:2 * P], True, False)
                            last = mm(dst[:, P:T], values(g, 1), pT[:, 2 * P:3 * P], False, True)
                        give(last, f"{sec}o{n}")
                    if 1 <= i <= pairs:
                        n = i - 1
                        pe.wait_ge(*V(f"{sec}_probs", n + 1))
                        for h2 in range(2):
                            transposes(f"{sec}t{n}_{h2}", [probs[:, n % 3, h2, j * P:(j + 1) * P] for j in range(3)], 4 + h2)

            def ffn(nm, layer):
                first = item_no[(nm, 0)]
                base = list(uses)
                for b in range(3):
                    if base[b]:
                        pe.wait_ge(free[b], base[b])
                place[nm] = tuple(base)

                def gate_up(j, steps):
                    steps.step(pe, "gu_split", j)
                    if j:
                        steps.bank(pe, free, base, j, 0)
                    w = {p_: gu_part[p_][j % 2].rearrange("p (k c) -> p k c", k=KD) for p_ in ("hi", "lo")}
                    for half in range(2):
                        for k in range(KD):
                            if j == 0 and half == 0 and k % 2 == 0:
                                pe.wait_ge(S("x_split"), 4 * layer + k // 2 + 1)
                            for n, (wp, xp) in enumerate(PARTS):
                                last = mm(psum[:, j % 3, half * T:(half + 1) * T], w[wp][:, k, half * P:(half + 1) * P],
                                          x_part[xp][:, k, :], k == 0 and n == 0, k == KD - 1 and n == 2)
                    last.then_inc(full[j % 3], 1)

                def down(j, steps):
                    steps.step(pe, "hidden_split", j)
                    steps.step(pe, "down_split", j)
                    end = j == FF_BLOCKS - 1
                    for m in range(KD):
                        for n, (wp, xp) in enumerate(PARTS):
                            last = mm(psum[:, 4 + m // 2, (m % 2) * T:(m % 2 + 1) * T],
                                      down_part[wp][j % 2][:, m * P:(m + 1) * P], hidden_part[xp][:, j % 3, :],
                                      False, end and n == 2)
                        if end and m % 2:
                            last.then_inc(full[4 + m // 2], 1)
                    if not end:
                        last.then_inc(S(f"{nm}_down"), 1)

                gate_up(0, LayerSteps(layer))
                with pe.Fori(0, 3) as it:
                    for j in range(1, 7):
                        gate_up(j, LayerSteps(layer, it))
                        down(j - 1, LayerSteps(layer, it))
                for j in range(19, FF_BLOCKS):
                    gate_up(j, LayerSteps(layer))
                    down(j - 1, LayerSteps(layer))
                down(FF_BLOCKS - 1, LayerSteps(layer))
                for b in range(3):
                    uses[b] += (FF_BLOCKS - b + 2) // 3
                for b in range(4, 8):
                    uses[b] += 1
                for j in range(FF_BLOCKS):
                    released[first + j] = (S("down_split"), layer * FF_BLOCKS + j + 1)

            def clear_sums(nth):
                for b in range(4, 8):
                    if uses[b]:
                        pe.wait_ge(free[b], uses[b])
                pe.wait_ge(*V("zeros_ready", nth))
                for b in range(4, 8):
                    mm(psum[:, b, :], page(2)[:, 768:768 + P], page(2)[:, 768:768 + BANK], True, False)

            rms("att0", fm(0), fm(11))
            hn = fm(1)
            w = weights(("e_in", 0))[:, 0:KD * 448].rearrange("p (k c) -> p k c", k=KD)
            for nm_, c0, c1, r in (("cq", 0, 256, 0), ("ckv", 256, 384, 0), ("kr", 384, 448, NOPE)):
                o = take(nm_)
                if nm_ == "kr":
                    for half in range(2):
                        for k in range(KD):
                            c = c0 + half * ROPE
                            last = mm(o[r:r + ROPE, half * T:(half + 1) * T], w[:, k, c:c + ROPE], hn[:, k, :],
                                      k == 0, k == KD - 1)
                else:
                    for half in range((c1 - c0) // P):
                        for k in range(KD):
                            if nm_ == "cq" and half == 0:
                                pe.wait_ge(*V("att0_scaled", k + 1))
                            last = mm(o[:, half * T:(half + 1) * T], w[:, k, c0 + half * P:c0 + (half + 1) * P],
                                      hn[:, k, :], k == 0, k == KD - 1)
                give(last, nm_)
            release(("e_in", 0), "kr")
            parts = {"hi": page_part[6], "lo": page_part[8]}
            project_split("qB", [("e_in", 1)], (2, 3), parts, 3)
            project_split("kB", [("e_in", 2)], (2, 3), parts)
            rms("cqn", page(9)[:, 0:512].rearrange("p (k t) -> p k t", t=T),
                page(11)[:, 0:512].rearrange("p (k t) -> p k t", t=T), 2)
            rms("ckvn", page(9)[:, 512:768].rearrange("p (k t) -> p k t", t=T),
                page(11)[:, 512:768].rearrange("p (k t) -> p k t", t=T), 1)
            w = weights(("e_in", 3)).rearrange("p (k c) -> p k c", k=KD)
            for b in range(NB):
                o = take(f"vB{b}")
                for k in range(KD):
                    last = mm(o, hn[:, k, b * P:(b + 1) * P], w[:, k, :], k == 0, k == KD - 1)
                give(last, f"vB{b}")
            release(("e_in", 3), "vB1")
            w = weights(("mla_up", 0))
            wq = w[:, 0:2 * D].rearrange("p (k c) -> p k c", k=2)
            wkv = w[:, 2 * D:3 * D]
            cq = page(9)[:, 768:1280].rearrange("p (k t) -> p k t", t=T)
            ckv = page(9)[:, 1280:1536]
            pe.wait_ge(*V("cqn_scaled", 2))
            for hd in range(HEADS):
                name = f"qA{hd}"
                o = take(name)
                for k in range(2):
                    mm(o[0:NOPE + ROPE, 0:T], wq[:, k, hd * 96:(hd + 1) * 96], cq[:, k, :], k == 0, k == 1)
                for k in range(2):
                    c = 768 + hd * ROPE
                    last = mm(o[NOPE:NOPE + ROPE, T:2 * T], wq[:, k, c:c + ROPE], cq[:, k, :], k == 0, k == 1)
                give(last, name)
            pe.wait_ge(*V("ckvn_scaled", 1))
            for h2 in range(HEADS // 2):
                name = f"kA{h2}"
                o = take(name)
                for half in range(2):
                    c = (2 * h2 + half) * NOPE
                    last = mm(o[0:NOPE, half * T:(half + 1) * T], wkv[:, c:c + NOPE], ckv, True, True)
                give(last, name)
            for b in range(NB):
                o = take(f"vA{b}")
                last = mm(o, ckv[:, b * P:(b + 1) * P], wkv[:, 512:D], True, True)
                give(last, f"vA{b}")
            release(("mla_up", 0), "vA1")
            qA, kA = fm(2), fm(3)
            vA = page(4)[:, 0:D].rearrange("p (b c) -> p b c", b=NB)
            vB = page(4)[:, D:2 * D].rearrange("p (b c) -> p b c", b=NB)
            qB = page(5)[:, 0:D].rearrange("p (k t) -> p k t", t=T)
            kB = page(5)[:, D:2 * D].rearrange("p (k t) -> p k t", t=T)
            pe.wait_ge(*V("qA_ready", HEADS))
            pe.wait_ge(*V("kA_ready", 5))
            pe.wait_ge(*V("vA_ready", NB))
            attend("mla", HEADS, lambda i: (qA[0:96, i, :], kA[0:96, i, :]),
                   lambda g, b: vA[:, b, g * VDIM:(g + 1) * VDIM])
            pe.wait_ge(*V("qkB_ready", 4))
            pe.wait_ge(*V("vB_ready", NB))
            half_of = lambda i: slice(VDIM * (i % 2), VDIM * (i % 2) + VDIM)
            attend("dil", HEADS, lambda i: (qB[half_of(i), i // 2, :], kB[half_of(i), i // 2, :]),
                   lambda g, b: vB[:, b, g * VDIM:(g + 1) * VDIM])
            parts = {"hi": page_part[9], "lo": page_part[8]}
            project_split("e_out", [("e_out", 0), ("e_out", 1)], (2, 3), parts, 4)
            rms("ffn0n", fm(0), fm(11))
            clear_sums(1)
            ffn("ffn0", 0)
            rms("att1", fm(0), fm(11))
            project_split("qS", [("o_in", 0), ("o_in", 1)], (3, 4), {"hi": page_part[8], "lo": page_part[9]}, 5)
            w = weights(("o_kv", 0))[:, 0:KD * T].rearrange("p (k c) -> p k c", k=KD)
            o = take("kS")
            for k in range(KD):
                last = mm(o[:, 0:T], w[:, k, 0:P], hn[:, k, :], k == 0, k == KD - 1)
            give(last, "kS")
            o = take("vS")
            for b in range(NB):
                for k in range(KD):
                    last = mm(o[:, b * P:(b + 1) * P], hn[:, k, b * P:(b + 1) * P], w[:, k, P:2 * P], k == 0, k == KD - 1)
            give(last, "vS")
            release(("o_kv", 0), "vS")
            qS, kS = fm(2), page(3)[:, 0:T]
            vS = page(4)[:, 0:T].rearrange("p (b c) -> p b c", b=NB)
            pe.wait_ge(*V("qS_ready", 4))
            pe.wait_ge(*V("kvS_ready", 2))
            attend("swa", SWA_HEADS, lambda i: (qS[half_of(i), i // 2, :], kS[half_of(i), :]),
                   lambda g, b: vS[:, b, half_of(g)])
            project_split("o_out", [("o_out", 0), ("o_out", 1)], (5, 1), parts, 6)
            rms("ffn1n", fm(0), fm(11))
            clear_sums(2)
            ffn("ffn1", 1)
            rms("final", fm(0), fm(11))

        @block.scalar
        def _(act_e):
            st = Steps(act_e, "act_step")

            tables_at = [None]

            def use_tables(name):
                if tables_at[0] != name:
                    tables_at[0] = name
                    if name == "ln_exp":
                        act_e.preload_act_table_set("natural_log_exp_and_others")
                    else:
                        act_e.preload_act_table(name)

            def act(o, i, func, name=None, **kw):
                if func in (ACT.Ln, ACT.Exp):
                    use_tables("ln_exp")
                elif func in (ACT.Silu, ACT.Gelu, ACT.Sigmoid):
                    use_tables(func)
                st.do(act_e.activation(o, i, func, **kw), name)

            def norm(nm, src, squares, small, nblocks, width, eps, dst=None, bias=None, between=None,
                     before=None):
                nh = 4 if nblocks == KD else 1
                for i in range(nh):
                    if bias is not None:
                        act_e.wait_ge(*V(f"{nm}_centered", i + 1))
                    elif before:
                        act_e.wait_ge(*before(i))
                    sl = slice(i * nblocks // nh, (i + 1) * nblocks // nh)
                    act(squares[:, sl, :], src[:, sl, :], ACT.Square, f"{nm}_squared")
                use_tables("ln_exp")
                if between:
                    between()
                v = await_full(act_e, f"{nm}_var")
                act(small, v[:, 0:T], ACT.Ln, f"{nm}_var", scale=1.0 / width, bias=col(eps))
                st.settle()
                act(small, small, ACT.Exp, f"{nm}_rstd", scale=-0.5)
                if bias is not None:
                    add_bias(nm, dst, bias)

            def add_bias(nm, dst, bias):
                for k in range(KD):
                    act_e.wait_ge(*V(f"{nm}_scaled", k + 1))
                    act(dst[:, k, :], dst[:, k, :], ACT.Identity, f"{nm}_out", bias=col(bias, k))

            highs = [0]

            def split_high(count):
                while highs[0] < count:
                    _, item, pair, high = split_pairs[highs[0]]
                    n = item_no[item]
                    act_e.wait_ge(landed[slot_no(n)], 16 * nth_landing(n))
                    if highs[0] >= 2:
                        await_full(act_e, split_pairs[highs[0] - 2][0])
                    act_e.activation(high, pair_of(slot(n), pair), ACT.Copy).then_inc(S("w_high"), 1)
                    highs[0] += 1

            def next_high():
                if highs[0] < MIXER_PAIRS:
                    split_high(highs[0] + 1)

            def input_high(dst, src, ready, splits={}):
                for i in range(4):
                    if i in splits:
                        split_high(splits[i])
                    act_e.wait_ge(*ready(i))
                    act_e.activation(dst[:, 2 * i:2 * i + 2, :], src[:, 2 * i:2 * i + 2, :], ACT.Copy).then_inc(S("h_high"), 1)

            def evacuate(part, npairs, dst, func, bias, first=0):
                for n in range(npairs):
                    v = await_full(act_e, f"{part}{n}")
                    k = first + 2 * n
                    act(dst[:, k, :], v[:, 0:T], func, bias=col("b_in", bias + k))
                    act(dst[:, k + 1, :], v[:, T:2 * T], func, f"{part}{n}", bias=col("b_in", bias + k + 1))
                    next_high()

            act_e.wait_ge(*V("x_landed", 16 * 3))
            for dst, src in ((page(3)[:, 0:KD * P].rearrange("p (g t) -> p g t", t=P), io["w_s"].rearrange("g s t -> s g t")),
                             (page(3)[0:1, KD * P:2 * KD * P], io["b_s"]), (rows[:], io["rows"][0:1, :].partition_broadcast(P)),
                             (ab[:, 0:P].rearrange("p (k c) -> p k c", k=KD), io["w_ab"].rearrange("(k p) c -> p k c", p=P)),
                             (masks[:], io["c_masks"])):
                act_e.dma_start(dst, src).then_inc(S("mixer_landed"), 16)
            norm("ln_in", fm(0), fm(2), page(4)[:, 512:768], KD, D, "eps5", fm(0), "ln_in_b", next_high)
            input_high(h_part["hi"], fm(0), lambda i: V("ln_in_out", 2 * i + 2))
            next_high()
            evacuate("gm_v", 4, fm(2), ACT.Gelu, 8)
            act_e.wait_ge(*V("ln_in_out", KD))
            for n in range(4):
                v = await_full(act_e, f"gm_u{n}")
                for half in range(2):
                    act(fm(5)[:, 2 * n + half, :], v[:, half * T:(half + 1) * T], ACT.Gelu,
                        f"gm_u{n}" if half else None, bias=col("b_in", 2 * n + half))
                next_high()
            for i in range(4):
                act_e.wait_ge(*V("gm_centered", i + 1))
                act(fm(4)[:, 2 * i:2 * i + 2, :], fm(2)[:, 2 * i:2 * i + 2, :], ACT.Square, "gm_squared")
            evacuate("gate_a", 2, fm(6), ACT.Sigmoid, 48)
            v = await_full(act_e, "gm_var")
            act(page(7)[:, 256:512], v[:, 0:T], ACT.Ln, "gm_var", scale=1.0 / D, bias=col("eps5"))
            st.settle()
            act(page(7)[:, 256:512], page(7)[:, 256:512], ACT.Exp, "gm_rstd", scale=-0.5)
            add_bias("gm", fm(2), "gm_b")
            evacuate("gate_a_", 2, fm(6), ACT.Sigmoid, 48, first=4)
            act_e.wait_ge(*V("mixer_landed", 16 * 5))
            stage = lambda n: page(5)[:, n % 6 * 260:n % 6 * 260 + 260]
            for part, pg, base in (("dn_q", 2, 0), ("dn_k", 3, 8), ("dn_v", 4, 16)):
                if part == "dn_q":
                    act_e.wait_ge(*V("stage_zero", 6))
                for n in range(4):
                    v = await_full(act_e, f"{part}{n}")
                    for half in range(2):
                        blk = base + 2 * n + half
                        if blk >= 6:
                            act_e.wait_ge(*V("conv_done", blk - 5))
                        act(stage(blk)[:, 4:260], v[:, half * T:(half + 1) * T], ACT.Identity, "staged",
                            bias=col("b_in", 16 + blk))
                    act_e.wait_ge(*V("staged", blk + 1))
                    act_e.sem_inc(free[place[f"{part}{n}"][0]], 1)
                    next_high()
                    if part == "dn_v" and n == 1:
                        act_e.wait_ge(*V("ab_ready", 1))
                        act(ab[:, 32:48], ab[:, 32:48], ACT.Exp, scale=-1.0)
                        act(ab[:, 48:64], ab[:, 48:64], ACT.Exp, scale=-1.0)
                        act(ab[:, 64:72], row("a_log", 8), ACT.Exp)
                        st.settle()
                        act(ab[:, 48:64], ab[:, 48:64], ACT.Ln, "ab_exps", bias=1.0)
                    for b2 in (blk - 3, blk - 2):
                        if b2 >= 0:
                            silu_block(act_e, act, S, fm, b2)
                if part == "dn_k":
                    v = await_full(act_e, "ab")
            for b2 in (22, 23):
                silu_block(act_e, act, S, fm, b2)
            for part, pg, src in (("q", 7, 2), ("k", 8, 3)):
                for q4 in range(4):
                    act(fm(pg)[:, 2 * q4:2 * q4 + 2, :], fm(src)[:, 2 * q4:2 * q4 + 2, :], ACT.Square, f"{part}_squared")
            for q4 in range(4):
                v = await_full(act_e, f"Gb{q4}")
                act(page(9)[:, q4 * BANK:(q4 + 1) * BANK], v, ACT.Exp, "expG_row")
            for n in range(2):
                v = await_full(act_e, f"dn_z{n}")
                for half in range(2):
                    k = 2 * n + half
                    act(fm(6)[:, k, :], v[:, half * T:(half + 1) * T], ACT.Silu, f"dn_z{n}" if half else None,
                        bias=col("b_in", 40 + k))
                next_high()
            for part, pg in (("q", 7), ("k", 8)):
                for q4 in range(4):
                    v = await_full(act_e, f"{part}_ss{q4}")
                    dst = page(pg)[:, q4 * BANK:(q4 + 1) * BANK]
                    act(dst, v, ACT.Ln, f"{part}_ss{q4}", bias=col("eps6"))
                    st.settle()
                    if part == "q":
                        act(dst, dst, ACT.Exp, "q_inv", scale=-0.5, bias=col("qscale"))
                    else:
                        act(dst, dst, ACT.Exp, "k_inv", scale=-0.5)
                if part == "q":
                    act_e.wait_ge(*V("G_small", 1))
                    act(ab[:, 96:128], ab[:, 96:128], ACT.Exp, "expG_col")
                    act_e.wait_ge(*V("decay_clipped", 1))
                    act(page(10, 2), page(10, 2), ACT.Exp, "decay_ready")
            for n in range(2):
                v = await_full(act_e, f"dn_z_{n}")
                for half in range(2):
                    k = 4 + 2 * n + half
                    act(fm(6)[:, k, :], v[:, half * T:(half + 1) * T], ACT.Silu, f"dn_z_{n}" if half else None,
                        bias=col("b_in", 40 + k))
                next_high()
            act_e.wait_ge(*st.last)
            act_e.sem_inc(S("z_ready"), 1)
            for q4 in range(4):
                act_e.wait_ge(*V("k_normed", 4))
                v = await_full(act_e, f"k_t{q4}")
                act(page(7)[:, q4 * BANK:(q4 + 1) * BANK], v, ACT.Copy, f"k_t{q4}")
                v = await_full(act_e, f"v_t{q4}")
                act(page(8)[:, q4 * BANK:(q4 + 1) * BANK], v, ACT.Copy, f"v_t{q4}")
            act_e.wait_ge(*st.last)
            act_e.sem_inc(S("tm_ready"), 1)
            for q4 in range(4):
                v = await_full(act_e, f"L_t{q4}")
                act(page(12)[:, q4 * BANK:(q4 + 1) * BANK], v, ACT.Copy, "LT_ready")
            for q4 in range(4):
                v = await_full(act_e, f"wc{q4}")
                act(page(12)[:, q4 * BANK:(q4 + 1) * BANK], v, ACT.Copy, "wc_evac")
            act_e.wait_ge(*V("wc_evac", 4))
            for q4 in range(4):
                act_e.sem_inc(free[place[f"wc{q4}"][0]], 1)
                act_e.sem_inc(S("wc_ready"), 1)
            oT = fm(4)
            for c in range(T // CHUNK):
                v = await_full(act_e, f"o{c}")
                act(oT[:, :, c * CHUNK:(c + 1) * CHUNK], v.rearrange("p (h t) -> p h t", h=HEADS), ACT.Copy, f"o{c}")
                if c in (0, 1):
                    part = "gate_b" + "_" * c
                    for n in range(2):
                        v = await_full(act_e, f"{part}{n}")
                        for half in range(2):
                            k = 4 * c + 2 * n + half
                            act(fm(9)[:, k, :], v[:, half * T:(half + 1) * T], ACT.Sigmoid,
                                f"{part}{n}" if half else None, bias=col("b_in", 56 + k))
                        next_high()
            st.settle()
            for q4 in range(4):
                act(fm(3)[:, 2 * q4:2 * q4 + 2, :], oT[:, 2 * q4:2 * q4 + 2, :], ACT.Square, "o_squared")
            for q4 in range(4):
                v = await_full(act_e, f"o_ss{q4}")
                dst = page(7)[:, q4 * BANK:(q4 + 1) * BANK]
                act(dst, v, ACT.Ln, f"o_ss{q4}", scale=1.0 / P, bias=col("eps6"))
                st.settle()
                act(dst, dst, ACT.Exp, "o_inv", scale=-0.5)
            input_high(page_part[2], fm(4), lambda i: V("yb_ready", 2 * i + 2))
            split_high(36)
            input_high(page_part[3], fm(1), lambda i: V("merged", i + 1), {1: 37})
            split_high(MIXER_PAIRS)
            if phases >= 2:
                act_e.dma_start(page(10)[:, 0:KD * 36].rearrange("p (k c) -> p k c", k=KD),
                                io["w_router"].rearrange("(k p) c -> p k c", p=P)).then_inc(S("router_landed"), 16)
                act_e.dma_start(page(10)[:, KD * 36:N_ROUTER], io["c_iota"]).then_inc(S("router_landed"), 16)
            norm("ln1", fm(0), fm(2), page(12)[:, 256:512], KD, D, "eps5", fm(0), "ln1_b")
            if phases < 2:
                return

            act_e.wait_ge(*V("group_centered", 1))
            act(page(11)[:, 80:96].rearrange("p (b g) -> p b g", b=NB)[:, :, 0:GROUPS],
                page(11)[:, 80:96].rearrange("p (b g) -> p b g", b=NB)[:, :, 0:GROUPS], ACT.Exp, "group_exp")
            for b in range(NB):
                for half in range(2):
                    v = await_full(act_e, f"h_t{b}{half}")
                    act(htm_part["hi"][:, b * D + half * 512:b * D + (half + 1) * 512], v, ACT.Copy, "htm_high")
            act_e.wait_ge(*V("top_diff", 1))
            act(page(11)[:, 240:242], page(11)[:, 240:242], ACT.Exp, "top_exp")
            for k in range(KD):
                if k % 2 == 0:
                    v = await_full(act_e, f"xs{k}")
                    act(page(2, 3).rearrange("p (k s) -> p k s", k=KD)[:, k, 0:ASSIGN], v, ACT.Copy, f"xs{k}")
            act_e.wait_ge(*st.last)
            act_e.wait_ge(*V("xs_odd", 4))
            act_e.sem_inc(S("xs_ready"), KD)
            for b in range(NB):
                v = await_full(act_e, f"gt{b}")
                act(page(9)[:, 0:4 * T].rearrange("p (s t) -> p s t", t=T)[:, :, b * P:(b + 1) * P],
                    v.rearrange("p (s t) -> p s t", s=4), ACT.Copy, f"gt{b}")
            act_e.wait_ge(*st.last)
            act_e.sem_inc(S("gt_ready"), 2)
            silu = page(10)[:, 1024:1536].rearrange("p (r s) -> p r s", r=2)
            base = place["moe_base"]
            actT = page(8)[:, 1024:1536].rearrange("p (r s) -> p r s", r=2)
            yrow = page(8)[:, 0:1024].rearrange("p (r s) -> p r s", r=2)
            use_tables(ACT.Silu)
            with act_e.Fori(0, EXPERTS // 2) as it:
                for r in range(2):
                    act_e.wait_ge(full[r], it + base[r] + 1)
                    act_e.wait_ge(free[r], it + base[r])
                    act_e.activation(silu[:, r, :], psum[:, r, 0:T], ACT.Silu).then_inc(S("silu_ready"), 1)
                for r in range(2):
                    act_e.wait_ge(full[2 + r], it + base[2 + r] + 1)
                    act_e.wait_ge(full[4 + r], it + base[4 + r])
                    act_e.activation(actT[:, r, :], psum[:, 2 + r, 0:T], ACT.Copy).then_inc(free[2 + r], 1)
                for r in range(2):
                    act_e.wait_ge(full[4 + r], it + base[4 + r] + 1)
                    act_e.wait_ge(full[6 + r], it + base[6 + r])
                    act_e.activation(yrow[:, r, :], psum[:, 4 + r, :], ACT.Copy).then_inc(free[4 + r], 1)
            tables_at[0] = None
            most = act_e.value_load(starts[0:1, EXPERTS:EXPERTS + 1], min_val=0, max_val=T)
            act_e.wait_ge(full[7], base[7] + EXPERTS // 2)
            with act_e.If(most > CAP):
                with act_e.Fori(0, EXPERTS) as e:
                    for c in range(MAX_PASSES):
                        n = e * MAX_PASSES + c + 1
                        act_e.wait_ge(*V("more_h", n + 1))
                        act_e.activation(silu[:, 0, :], psum[:, 0, 0:T], ACT.Silu).then_inc(S("more_silu"), 1)
                        act_e.wait_ge(*V("more_t", n))
                        act_e.activation(actT[:, 0, :], psum[:, 2, 0:T], ACT.Copy).then_inc(S("more_actT"), 1)
                        act_e.wait_ge(*V("more_y", n + 1))
                        act_e.activation(yrow[:, 0, :], psum[:, 4, :], ACT.Copy).then_inc(S("more_yrow"), 1)
            if phases >= 3:
                act_e.wait_ge(*V("experts_done", 1))
                act_e.dma_start(page(10), io["c_attn"]).then_inc(S("attn_tables"), 16)
            for s in range(4):
                for half in range(2):
                    v = await_full(act_e, f"y_t{s}{half}")
                    if half == 0:
                        act(page(11, 2)[:, s * D:s * D + 512], v, ACT.Copy, f"y_t{s}{half}")
            act_e.wait_ge(*st.last)
            act_e.wait_ge(*V("ytm_odd", 4))
            act_e.sem_inc(S("ytm_ready"), 8)
            norm("ln2", fm(0), fm(2), page(12)[:, 256:512], KD, D, "eps5", fm(0), "ln2_b")
            if phases < 3:
                return

            def rms(nm, src, squares, small, nblocks, width, before=None, between=None):
                norm(nm, src, squares, small, nblocks, width, "eps6", between=between, before=before)

            def attend(sec, nheads, sink=False, first_pair=None):
                for i in range(nheads // 2 + 1):
                    if first_pair is not None and i in (1, 2):
                        split_high(first_pair + i)
                    if i < nheads // 2:
                        act_e.wait_ge(*V(f"{sec}_max", i + 1))
                        for h2 in range(2):
                            for b, sl in enumerate((slice(0, P), slice(P, SPAN))):
                                e = probs[:, i % 3, h2, sl]
                                total = {} if sec == "dil" else {"accum_out": stats[:, i % 3, TOTAL, h2, b:b + 1]}
                                if sink and h2 + b == 2:
                                    for h3 in range(2):
                                        hd = ROWS["sinks"] + i + HEADS * h3
                                        act(stats[:, i % 3, SINK_EXP, h3, :], stats[:, i % 3, NEG_MAX, h3, :], ACT.Exp,
                                            bias=rows[:, hd:hd + 1])
                                act(e, e, ACT.Exp, f"{sec}_exp" if h2 + b == 2 else None,
                                    bias=stats[:, i % 3, NEG_MAX, h2, b:b + 1], **total)
                    if i >= 1:
                        n = i - 1
                        await_full(act_e, f"{sec}t{n}_0")
                        await_full(act_e, f"{sec}t{n}_1")
                        if n >= 2:
                            await_full(act_e, f"{sec}o{n - 2}")
                        act(probs_t[:, n % 2, :, :], psum[:, 4:6, 0:SPAN], ACT.Copy, f"{sec}_pT")
                        st.settle()
                        for h2 in range(2):
                            act_e.sem_inc(free[place[f"{sec}t{n}_{h2}"][0]], 1)

            def gate_up_high(nm, layer, j, steps):
                n = item_no[(nm, 0)] + j
                steps.landed(act_e, n)
                if j >= 2:
                    steps.bank(act_e, full, place[nm], j - 2, 1)
                act_e.activation(gu_part["hi"][j % 2], slot(n)[:, 0:gu_size], ACT.Copy).then_inc(S("gu_high"), 1)

            def ffn(nm, layer, next_pairs=None):
                silu_buf = page(2)[:, 1280:2048].rearrange("p (r t) -> p r t", t=T)

                def one(j, steps):
                    if j + 1 < FF_BLOCKS:
                        gate_up_high(nm, layer, j + 1, steps)
                    if j >= 2:
                        act_e.wait_ge(S(f"{nm}_down"), steps.at(j - 1, 6))
                    src = slot(item_no[(nm, 0)] + j)[:, gu_size:gu_size + down_size]
                    act_e.activation(down_part["hi"][j % 2], src, ACT.Copy).then_inc(S("down_high"), 1)
                    steps.bank(act_e, full, place[nm], j, 1)
                    if j >= 3:
                        steps.step(act_e, "hidden_split", j - 3)
                    act_e.activation(silu_buf[:, j % 3, :], psum[:, j % 3, 0:T], ACT.Silu).then_inc(S(f"{nm}_silu"), 1)

                use_tables(ACT.Silu)
                one(0, LayerSteps(layer))
                one(1, LayerSteps(layer))
                with act_e.Fori(0, 3) as it:
                    for j in range(2, 8):
                        one(j, LayerSteps(layer, it))
                one(20, LayerSteps(layer))
                if next_pairs:
                    split_high(next_pairs)
                one(21, LayerSteps(layer))
                st.last = (S(f"{nm}_silu"), FF_BLOCKS)

            def ffn_norm(nm, layer, before):
                rms(f"{nm}n", fm(0), fm(11), page(12)[:, 256:512], KD, D, before,
                    lambda: gate_up_high(nm, layer, 0, LayerSteps(layer)))
                for i in range(4):
                    act_e.wait_ge(*V(f"{nm}n_scaled", 2 * i + 2))
                    act_e.activation(x_part["hi"][:, 2 * i:2 * i + 2, :], fm(1)[:, 2 * i:2 * i + 2, :], ACT.Copy)\
                        .then_inc(S("x_high"), 1)

            rms("att0", fm(0), fm(11), page(12)[:, 256:512], KD, D, lambda i: V("ln2_out", 2 * i + 2),
                lambda: split_high(MIXER_PAIRS + 1))
            input_high(page_part[6], fm(1), lambda i: V("att0_scaled", 2 * i + 2))
            split_high(MIXER_PAIRS + 2)
            q9 = page(9)[:, 0:512].rearrange("p (k t) -> p k t", t=T)
            v = await_full(act_e, "cq")
            act(page(9)[:, 0:512], v, ACT.Copy, "cq")
            v = await_full(act_e, "ckv")
            act(page(9)[:, 512:768], v[:, 0:T], ACT.Copy, "ckv")
            for part, off, scale in (("qB", 0, DIL_SCALE), ("kB", D, 1.0)):
                for n in range(2):
                    v = await_full(act_e, f"{part}{n}")
                    act(page(5)[:, off + n * 512:off + (n + 1) * 512], v, ACT.Copy, f"{part}{n}", scale=scale)
                    if part == "qB":
                        split_high(MIXER_PAIRS + 3 + n)
            st.settle()
            act_e.sem_inc(S("qkB_ready"), 4)
            rms("cqn", q9, page(11)[:, 0:512].rearrange("p (k t) -> p k t", t=T), page(12)[:, 512:768], 2, MLA_Q)
            rms("ckvn", page(9)[:, 512:768].rearrange("p (k t) -> p k t", t=T),
                page(11)[:, 512:768].rearrange("p (k t) -> p k t", t=T), page(12)[:, 768:1024], 1, MLA_KV)
            for b in range(NB):
                v = await_full(act_e, f"vB{b}")
                act(page(4)[:, D + b * 512:D + (b + 1) * 512], v, ACT.Copy, f"vB{b}")
            st.settle()
            act_e.sem_inc(S("vB_ready"), NB)
            for hd in range(HEADS):
                v = await_full(act_e, f"qA{hd}")
                act(fm(2)[0:NOPE, hd, :], v[0:NOPE, 0:T], ACT.Copy, "qA_nope", scale=MLA_SCALE)
            for h2 in range(HEADS // 2):
                v = await_full(act_e, f"kA{h2}")
                act(fm(3)[0:NOPE, 2 * h2:2 * h2 + 2, :], v[0:NOPE, :].rearrange("p (a t) -> p a t", a=2), ACT.Copy,
                    "kA_nope")
                act_e.wait_ge(*V("kA_nope", h2 + 1))
                act_e.sem_inc(free[place[f"kA{h2}"][0]], 1)
                act_e.sem_inc(S("kA_ready"), 1)
            for b in range(NB):
                v = await_full(act_e, f"vA{b}")
                act(page(4)[:, b * 512:(b + 1) * 512], v, ACT.Copy, f"vA{b}")
            st.settle()
            act_e.sem_inc(S("vA_ready"), NB)
            attend("mla", HEADS)
            attend("dil", HEADS, first_pair=MIXER_PAIRS + 4)
            input_high(page_part[9], fm(8), lambda i: V("mla_o_ready", 2 * i + 2) if i < 2 else V("dil_o_ready", 2 * i - 2))
            split_high(MIXER_PAIRS + 8)
            ffn_norm("ffn0", 0, lambda i: V("res3", i + 1))
            ffn("ffn0", 0, MIXER_PAIRS + 10)
            rms("att1", fm(0), fm(11), page(12)[:, 256:512], KD, D, lambda i: V("res4", i + 1))
            input_high(page_part[8], fm(1), lambda i: V("att1_scaled", 2 * i + 2))
            for n in range(4):
                v = await_full(act_e, f"qS{n}")
                act(page(2)[:, n * 512:(n + 1) * 512], v, ACT.Copy, "qS_evac", scale=DIL_SCALE)
                act_e.wait_ge(*V("qS_evac", n + 1))
                act_e.sem_inc(free[place[f"qS{n}"][0]], 1)
                act_e.sem_inc(S("qS_ready"), 1)
                split_high(min(MIXER_PAIRS + 11 + n, MIXER_PAIRS + 12))
            v = await_full(act_e, "kS")
            act(page(3)[:, 0:T], v[:, 0:T], ACT.Copy, "kS")
            v = await_full(act_e, "vS")
            act(page(4)[:, 0:T], v[:, 0:T], ACT.Copy, "vS")
            st.settle()
            act_e.sem_inc(S("kvS_ready"), 2)
            attend("swa", SWA_HEADS, sink=True, first_pair=MIXER_PAIRS + 12)
            input_high(page_part[9], fm(8), lambda i: V("swa_o_ready", 2 * i + 2))
            split_high(MIXER_PAIRS + 16)
            ffn_norm("ffn1", 1, lambda i: V("res5", i + 1))
            ffn("ffn1", 1)
            rms("final", fm(0), fm(11), page(12)[:, 256:512], KD, D, lambda i: V("res6", i + 1))

        @block.vector
        def _(ve):
            st = Steps(ve, "dve_step")
            do, settle = st.do, st.settle

            def bc(ap, axis, shape):
                return ap.unsqueeze(axis).broadcast_to(shape)

            def center(nm, src, dst, small):
                v = await_full(ve, f"{nm}_mu")
                do(ve.tensor_scalar(small, v[:, 0:T], 1.0 / D, None, ALU.mult), f"{nm}_mu")
                settle()
                for i in range(4):
                    sl = slice(2 * i, 2 * i + 2)
                    do(ve.tensor_tensor(dst[:, sl, :], src[:, sl, :], bc(small, 1, [P, 2, T]), ALU.subtract),
                       f"{nm}_centered")

            def scale_rows(nm, src, dst, small, gain, nblocks, done):
                ve.wait_ge(*V(f"{nm}_rstd", 1))
                for k in range(nblocks):
                    do(ve.scalar_tensor_tensor(dst[:, k, :], src[:, k, :], col(gain, k), small, ALU.mult, ALU.mult), done)

            def layer_norm(nm, src, dst, mean, rstd, gain):
                center(nm, src, dst, mean)
                scale_rows(nm, dst, dst, rstd, gain, KD, f"{nm}_scaled")

            lows = [0]

            def split_low(count):
                while lows[0] < count:
                    _, item, pair, high = split_pairs[lows[0]]
                    n = item_no[item]
                    lows[0] += 1
                    ve.wait_ge(S("w_high"), lows[0])
                    ve.tensor_tensor(pair_of(slot_low[slot_no(n)], pair), pair_of(slot(n), pair), high,
                                     ALU.subtract).then_inc(S("w_split"), 1)

            def input_low(no, low, src, high):
                for i in range(4):
                    ve.wait_ge(S("h_high"), 4 * no + i + 1)
                    sl = slice(2 * i, 2 * i + 2)
                    ve.tensor_tensor(low[:, sl, :], src[:, sl, :], high[:, sl, :], ALU.subtract).then_inc(S("h_split"), 1)

            ve.wait_ge(*V("x_landed", 16 * 3))
            layer_norm("ln_in", fm(1), fm(0), page(4)[:, 256:512], page(4)[:, 512:768], "ln_in_g")
            split_low(1)
            input_low(0, h_part["lo"], fm(0), h_part["hi"])
            split_low(2)
            ve.wait_ge(*V("mixer_landed", 16 * 5))
            do(ve.memset(page(3)[CHUNK:P, 0:KD * P].rearrange("p (g t) -> p g t", t=P)[:, :, 0:CHUNK], 0.0), "gate_masked")
            for n in range(4):
                b_, n_ = place[f"gm_v{n}"]
                ve.wait_ge(free[b_], n_)
                split_low(n + 3)
            ve.sem_inc(S("gm_v_ready"), 4)
            split_low(10)
            center("gm", fm(2), fm(2), page(7)[:, 0:256])
            split_low(12)
            scale_rows("gm", fm(2), fm(2), page(7)[:, 256:512], "gm_g", KD, "gm_scaled")
            for b in range(NB):
                for half in range(2):
                    v = await_full(ve, f"gm_t{b}{half}")
                    do(ve.tensor_copy(page(4)[:, b * D + half * 512:b * D + (half + 1) * 512], v), f"gm_t{b}{half}")
            settle()
            ve.sem_inc(S("gm_vtm"), 4)
            for n in range(4):
                v = await_full(ve, f"spatial{n}")
                b_, n_ = place[f"gm_u{n}"]
                ve.wait_ge(free[b_], n_)
                do(ve.tensor_tensor(page(5)[:, n * 512:(n + 1) * 512], v, page(5)[:, n * 512:(n + 1) * 512], ALU.mult),
                   f"spatial{n}")
            settle()
            ve.sem_inc(S("ya_ready"), 4)
            split_low(14)
            for part, off in (("gate_a", 0), ("gate_a_", 2)):
                for n in range(2):
                    b_, n_ = place[f"{part}{n}"]
                    ve.wait_ge(free[b_], n_)
            for n in range(4):
                v = await_full(ve, f"w_pa{n}")
                do(ve.tensor_tensor(page(1)[:, n * 512:(n + 1) * 512], v, page(6)[:, n * 512:(n + 1) * 512], ALU.mult),
                   f"w_pa{n}")
            settle()
            stage = lambda n: page(5)[:, n % 6 * 260:n % 6 * 260 + 260]
            for n in range(6):
                do(ve.memset(stage(n)[:, 0:4], 0.0), "stage_zero")
            for blk in range(24):
                if blk == 16:
                    ab_stage(ve, st, S, ab, row, await_full, bc)
                if blk == 20:
                    ve.wait_ge(*V("ab_exps", 1))
                    ab_finish(ve, st, S, ab)
                if blk % 2 == 0:
                    split_low(15 + blk // 2)
                dst = fm(2 + blk // 8)[:, blk % 8, :]
                s = stage(blk)
                ve.wait_ge(*V("staged", blk + 1))
                tap = lambda j: col("conv", j * 24 + blk)
                do(ve.tensor_scalar(dst, s[:, 4:260], tap(3), None, ALU.mult))
                for j in range(3):
                    settle()
                    do(ve.scalar_tensor_tensor(dst, s[:, 1 + j:257 + j], tap(j), dst, ALU.mult, ALU.add),
                       "conv_done" if j == 2 else None)
            v = await_full(ve, "G")
            G = ab[:, 80:96]
            do(ve.tensor_copy(G, v[:, 0:16]), "G")
            settle()
            D_, DT = page(11), page(10)
            for q4 in range(4):
                v = await_full(ve, f"Gb{q4}")
                ve.wait_ge(*V("expG_row", q4 + 1))
                v4 = v.rearrange("p (h b t) -> p h b t", h=2, b=NB)
                last = ab[:, 160 + 4 * q4:164 + 4 * q4].rearrange("p (h b) -> p h b", h=2)
                do(ve.tensor_copy(last[0:CHUNK], v4[0:CHUNK, :, :, CHUNK - 1]))
                do(ve.tensor_copy(last[CHUNK:P], v4[CHUNK:P, :, :, P - 1]))
                gcol = G.rearrange("p (b h) -> p h b", b=NB)[:, 2 * q4:2 * q4 + 2, :]
                gcol = gcol.unsqueeze(3).broadcast_to([P, 2, NB, P])
                view = lambda pg: pg[:, q4 * BANK:(q4 + 1) * BANK].rearrange("p (h b t) -> p h b t", h=2, b=NB)
                for hh in range(2):
                    do(ve.tensor_tensor(view(DT)[:, hh], v4[:, hh], gcol[:, hh], ALU.subtract))
                    do(ve.tensor_tensor(view(D_)[:, hh], gcol[:, hh], v4[:, hh], ALU.subtract),
                       f"Gb{q4}" if hh else None)
            settle()
            do(ve.tensor_scalar(page(10, 2), page(10, 2), 0.0, None, ALU.min), "decay_clipped")
            split_low(28)
            do(ve.tensor_copy(ab[:, 96:112], G))
            do(ve.tensor_tensor(ab[:, 112:128].rearrange("p (b h) -> p h b", b=NB), ab[:, 160:176].rearrange("p (h b) -> p h b", b=NB),
                                G.rearrange("p (b h) -> p h b", b=NB), ALU.subtract), "G_small")
            for part, pg, src in (("q", 7, 2), ("k", 8, 3)):
                for q4 in range(4):
                    ve.wait_ge(*V(f"{part}_inv", q4 + 1))
                    sl = slice(q4 * BANK, (q4 + 1) * BANK)
                    do(ve.tensor_tensor(page(src)[:, sl], page(src)[:, sl], page(pg)[:, sl], ALU.mult), f"{part}_normed")
            ve.wait_ge(*V("decay_masked", 2))
            for q4 in range(4):
                v = await_full(ve, f"kk{q4}")
                sl = slice(q4 * BANK, (q4 + 1) * BANK)
                do(ve.tensor_tensor(page(11)[:, sl], v, page(11)[:, sl], ALU.mult), f"kk{q4}")
                settle()
                ve.sem_inc(S("L_ready"), 1)
            ve.wait_ge(*V("tm_ready", 1))
            idb = bc(ident, 1, [P, 4, P])
            for q4 in range(4):
                sl = slice(q4 * BANK, (q4 + 1) * BANK)
                v3 = lambda pg: page(pg)[:, sl].rearrange("p (u t) -> p u t", t=P)
                do(ve.tensor_tensor(v3(5), v3(11), bc(mask("first"), 1, [P, 4, P]), ALU.mult))
                ve.wait_ge(*V("LT_ready", q4 + 1))
                do(ve.tensor_tensor(v3(4), v3(12), bc(mask("first_t"), 1, [P, 4, P]), ALU.mult))
                settle()
                do(ve.tensor_tensor(v3(5), idb, v3(5), ALU.subtract))
                do(ve.tensor_tensor(v3(4), idb, v3(4), ALU.subtract), "X_ready")
                b_, n_ = place[f"L_t{q4}"]
                ve.sem_inc(free[b_], 1)
            for q4 in range(4):
                v = await_full(ve, f"qk{q4}")
                sl = slice(q4 * BANK, (q4 + 1) * BANK)
                do(ve.tensor_tensor(page(10)[:, sl], v, page(10)[:, sl], ALU.mult), f"qk{q4}")
            settle()
            do(ve.tensor_tensor(page(2), page(2), page(9), ALU.mult), "qd_ready")
            cd = ab[:, 128:160]
            do(ve.tensor_copy(cd, page(9).rearrange("p (x t) -> p x t", t=CHUNK)[:, :, CHUNK - 1]))
            settle()
            for lv in range(5):
                if lv in (1, 3):
                    split_low(29 + lv // 2)
                for q4 in range(4):
                    sl = slice(q4 * BANK, (q4 + 1) * BANK)
                    v3 = lambda pg: page(pg)[:, sl].rearrange("p (u t) -> p u t", t=P)
                    name = f"Y{lv}_{q4}"
                    v = await_full(ve, name)
                    do(ve.tensor_tensor(v3(9), v.rearrange("p (u t) -> p u t", t=P),
                                        bc(mask(f"level{2 << lv}"), 1, [P, 4, P]), ALU.mult), "Y_evac")
                    ve.wait_ge(*V("Y_evac", 4 * lv + q4 + 1))
                    ve.sem_inc(free[place[name][0]], 1)
                    ve.sem_inc(S("Y_ready"), 1)
                for q4 in range(4):
                    sl = slice(q4 * BANK, (q4 + 1) * BANK)
                    if lv < 4:
                        v = await_full(ve, f"Z{lv}_{q4}")
                    w = await_full(ve, f"ZT{lv}_{q4}")
                    do(ve.tensor_tensor(page(4)[:, sl], page(4)[:, sl], w, ALU.subtract), f"ZT{lv}_{q4}")
                    if lv < 4:
                        do(ve.tensor_tensor(page(5)[:, sl], page(5)[:, sl], v, ALU.subtract), f"Z{lv}_{q4}")
                        settle()
                        ve.sem_inc(S("X_ready"), 1)
            settle()
            ve.sem_inc(S("XT_final"), 4)
            for q4 in range(4):
                v = await_full(ve, f"uc{q4}")
                do(ve.tensor_copy(page(11)[:, q4 * BANK:(q4 + 1) * BANK], v), f"uc{q4}")
            settle()
            ve.sem_inc(S("vnew_ready"), 2)
            state = page(5)[:, 0:HEADS * P]
            vn = page(11).rearrange("p (h b d) -> p h b d", b=NB, d=P)
            for c in range(T // CHUNK):
                b, r = c // 2, CHUNK * (c % 2)
                if c > 0:
                    split_low(31)
                    for hh in range(2):
                        v = await_full(ve, f"ws{c}_{hh}")
                        dst = vn[r:r + CHUNK, 4 * hh:4 * hh + 4, b, :]
                        do(ve.tensor_tensor(dst, dst, v[r:r + CHUNK, :].rearrange("p (h d) -> p h d", h=4), ALU.subtract),
                           "vnew_evac")
                        ve.wait_ge(*V("vnew_evac", 2 * (c - 1) + hh + 1))
                        ve.sem_inc(free[place[f"ws{c}_{hh}"][0]], 1)
                        ve.sem_inc(S("vnew_ready"), 1)
                if c == 1:
                    split_low(32)
                if c < T // CHUNK - 1:
                    if c > 0:
                        b_, n_ = place[f"o{c}"]
                        ve.wait_ge(full[b_], n_)
                    for hh in range(2):
                        v = await_full(ve, f"ds{c}_{hh}")
                        if c == 0:
                            do(ve.tensor_copy(state[:, hh * 512:(hh + 1) * 512], v), f"ds{c}_{hh}")
                        else:
                            for j in range(4):
                                hd = 4 * hh + j
                                sl = slice(hd * P, (hd + 1) * P)
                                x = hd * 4 + c
                                do(ve.scalar_tensor_tensor(state[:, sl], state[:, sl], cd[:, x:x + 1],
                                                           v[:, j * P:(j + 1) * P], ALU.mult, ALU.add),
                                   f"ds{c}_{hh}" if j == 3 else None)
                    settle()
                    ve.sem_inc(S("state_ready"), 1)
            split_low(34)
            b_, n_ = place["o3"]
            ve.wait_ge(free[b_], n_)
            ve.wait_ge(*V("z_ready", 1))
            for q4 in range(4):
                ve.wait_ge(*V("o_inv", q4 + 1))
                sl = slice(q4 * BANK, (q4 + 1) * BANK)
                do(ve.scalar_tensor_tensor(page(4)[:, sl], page(4)[:, sl], col("dn_norm"), page(7)[:, sl], ALU.mult,
                                           ALU.mult))
                settle()
                do(ve.tensor_tensor(page(4)[:, sl], page(4)[:, sl], page(6)[:, sl], ALU.mult))
                settle()
                ve.sem_inc(S("yb_ready"), 2)
            input_low(1, page_part[4], fm(4), page_part[2])
            for n in range(4):
                v = await_full(ve, f"w_pb{n}")
                sl = slice(n * BANK, (n + 1) * BANK)
                do(ve.tensor_tensor(page(9)[:, sl], v, page(9)[:, sl], ALU.mult), f"w_pb{n}")
                settle()
                do(ve.tensor_tensor(page(1)[:, sl], page(1)[:, sl], page(9)[:, sl], ALU.add), "merged")
                if n < 3:
                    split_low(35 + n)
            input_low(2, page_part[1], fm(1), page_part[3])
            split_low(38)

            def residual(part, alpha, done, names, first_pair=None):
                for n, name in enumerate(names):
                    if first_pair is not None and n < 2:
                        split_low(first_pair + n + 1)
                    v = await_full(ve, name)
                    sl = slice(n * BANK, (n + 1) * BANK)
                    if alpha is None:
                        do(ve.tensor_tensor(page(0)[:, sl], page(0)[:, sl], v, ALU.add), name)
                    else:
                        do(ve.scalar_tensor_tensor(page(0)[:, sl], page(0)[:, sl], alpha, v, ALU.mult, ALU.add), name)
                    settle()
                    ve.sem_inc(S(done), 1)

            residual("w_o", ALPHA, "res1", [f"w_o{n}" for n in range(4)], 38)
            layer_norm("ln1", fm(0), fm(0), page(12)[:, 0:256], page(12)[:, 256:512], "ln1_g")
            if phases < 2:
                return

            r11 = page(11)
            logits = r11[:, 0:72].rearrange("p (b c) -> p b c", b=NB)
            v = await_full(ve, "router")
            ve.wait_ge(*V("ln1_out", KD))
            ve.wait_ge(*V("router_landed", 32))
            do(ve.tensor_tensor(logits, v[:, 0:72].rearrange("p (b c) -> p b c", b=NB), bc(row("b_router", 36), 1, [P, NB, 36]),
                                ALU.add), "router")
            ge = r11[:, 80:96].rearrange("p (b g) -> p b g", b=NB)
            do(ve.memset(r11[:, 80:96], -1.0))
            settle()
            two = lambda n: r11[:, 96 + 2 * n:98 + 2 * n]
            col2 = lambda ap, b: ap[:, b:b + 1]
            do(ve.tensor_reduce(two(0), logits[:, :, 0:GROUPS], AX.X, ALU.max))
            settle()
            do(ve.tensor_tensor(ge[:, :, 0:GROUPS], logits[:, :, 0:GROUPS], bc(two(0), 2, [P, NB, GROUPS]), ALU.subtract),
               "group_centered")
            ve.wait_ge(*V("group_exp", 1))
            do(ve.tensor_reduce(two(1), ge[:, :, 0:GROUPS], AX.X, ALU.add))
            settle()
            do(ve.reciprocal(two(2), two(1)))
            iota = page(10)[:, KD * 36:KD * 36 + ASSIGN]
            expert_row = page(10)[:, KD * 36 + ASSIGN:KD * 36 + ASSIGN + 32]
            group_row = page(10)[:, KD * 36 + ASSIGN + 32:KD * 36 + ASSIGN + 64]
            idx = r11[:, 128:192].bitcast(U32)
            masked = r11[:, 256:320].rearrange("p (b e) -> p b e", b=NB)
            top = lambda b: r11[:, 192 + 24 * b:200 + 24 * b]
            for b in range(NB):
                do(ve.max(top(b), ge[:, b, :]))
            settle()
            for b in range(NB):
                do(ve.max_index(idx[:, 24 * b:24 * b + 8], top(b), ge[:, b, :]))
            settle()
            for b in range(NB):
                do(ve.tensor_copy(r11[:, 112 + b:113 + b], idx[:, 24 * b:24 * b + 1]))
            settle()
            for b in range(NB):
                do(ve.tensor_scalar(masked[:, b, :], group_row, r11[:, 112 + b:113 + b], None, ALU.is_equal))
            settle()
            do(ve.tensor_scalar(r11[:, 256:320], r11[:, 256:320], 1.0, 1e30, ALU.subtract, ALU.mult))
            settle()
            do(ve.tensor_tensor(masked, masked, logits[:, :, GROUPS:36], ALU.add))
            settle()
            for b in range(NB):
                do(ve.max(r11[:, 200 + 8 * b:208 + 8 * b], masked[:, b, :]))
            settle()
            for b in range(NB):
                do(ve.max_index(idx[:, 8 + 8 * b:16 + 8 * b], r11[:, 200 + 8 * b:208 + 8 * b], masked[:, b, :]))
            settle()
            for b in range(NB):
                do(ve.tensor_copy(r11[:, 120 + 2 * b:122 + 2 * b], idx[:, 8 + 8 * b:10 + 8 * b]))
            best = r11[:, 200:216].rearrange("p (b x) -> p b x", b=NB)
            settle()
            do(ve.tensor_tensor(r11[:, 240:242], best[:, :, 1], best[:, :, 0], ALU.subtract), "top_diff")
            eh = lambda s: r11[:, 320 + 64 * s:384 + 64 * s].rearrange("p (b e) -> p b e", b=NB)
            pick = r11[:, 512:576]
            for b in range(NB):
                for s in range(2):
                    do(ve.tensor_scalar(eh(s)[:, b, :], expert_row, r11[:, 120 + 2 * b + s:121 + 2 * b + s], None, ALU.is_equal))
            settle()
            do(ve.tensor_tensor(pick, r11[:, 320:384], r11[:, 384:448], ALU.add), "picked")
            def tokens_low(b):
                for half in range(2):
                    v = await_full(ve, f"h_t{b}{half}")
                    ve.wait_ge(*V("htm_high", 2 * b + half + 1))
                    sl = slice(b * D + half * 512, b * D + (half + 1) * 512)
                    do(ve.tensor_tensor(htm_part["lo"][:, sl], v, htm_part["hi"][:, sl], ALU.subtract), f"h_t{b}{half}")

            tokens_low(0)
            v = await_full(ve, "rank")
            do(ve.tensor_copy(r11[0:EXPERTS, 640:640 + P], v[0:EXPERTS, 96:97].broadcast_to([EXPERTS, P])), "counts_spread")
            tokens_low(1)
            do(ve.tensor_reduce(r11[0:1, 252:253], v[0:1, 64:96], AX.X, ALU.max))
            settle()
            do(ve.tensor_copy(starts[0:1, EXPERTS:EXPERTS + 1], r11[0:1, 252:253]))
            do(ve.tensor_copy(r11[:, 576:640], v[:, 0:64]), "rank")
            v = await_full(ve, "start")
            do(ve.tensor_copy(starts[0:1, 0:EXPERTS], v[0:1, 0:EXPERTS]))
            settle()
            ve.sem_inc(S("starts_ready"), 1)
            where = r11[:, 576:640].rearrange("p (b e) -> p b e", b=NB)
            do(ve.tensor_tensor(where, where, bc(v[:, 0:EXPERTS], 1, [P, NB, EXPERTS]), ALU.add), "start")
            settle()
            for s in range(2):
                do(ve.tensor_tensor(eh(s), eh(s), where, ALU.mult))
            settle()
            for s in range(2):
                do(ve.tensor_reduce(r11[:, 224 + 2 * s:226 + 2 * s], eh(s), AX.X, ALU.add))
            settle()
            gated = page(8)[:, NB * ASSIGN:2 * NB * ASSIGN].rearrange("p (b s) -> p b s", b=NB)
            pos = lambda s, b: r11[:, 224 + 2 * s + b:225 + 2 * s + b]
            gate = lambda s, b: r11[:, 246 + 2 * s + b:247 + 2 * s + b]
            for b in range(NB):
                do(ve.tensor_scalar(onehot[:, b, :], iota, pos(0, b), None, ALU.is_equal))
            settle()
            for b in range(NB):
                do(ve.scalar_tensor_tensor(onehot[:, b, :], iota, pos(1, b), onehot[:, b, :], ALU.is_equal, ALU.add),
                   "onehot_ready")
            ve.wait_ge(*V("top_exp", 1))
            do(ve.tensor_scalar(r11[:, 242:244], r11[:, 240:242], 1.0, None, ALU.add))
            settle()
            do(ve.reciprocal(r11[:, 244:246], r11[:, 242:244]))
            settle()
            do(ve.tensor_tensor(r11[:, 246:248], r11[:, 244:246], two(2), ALU.mult))
            settle()
            do(ve.tensor_tensor(r11[:, 248:250], r11[:, 246:248], r11[:, 240:242], ALU.mult))
            settle()
            spare = r11[:, 1024:1536]
            for b in range(NB):
                do(ve.tensor_scalar(gated[:, b, :], iota, pos(0, b), gate(0, b), ALU.is_equal, ALU.mult))
                do(ve.tensor_scalar(spare, iota, pos(1, b), gate(1, b), ALU.is_equal, ALU.mult))
                settle()
                do(ve.tensor_tensor(gated[:, b, :], gated[:, b, :], spare, ALU.add), "gated_ready")
                settle()
            for k in range(1, KD, 2):
                v = await_full(ve, f"xs{k}")
                do(ve.tensor_copy(page(2, 3).rearrange("p (k s) -> p k s", k=KD)[:, k, 0:ASSIGN], v), f"xs{k}")
            settle()
            ve.sem_inc(S("xs_odd"), 4)
            silu = page(10)[:, 1024:1536].rearrange("p (r s) -> p r s", r=2)
            acts = page(10)[:, 1536:2048].rearrange("p (r s) -> p r s", r=2)
            ys = page(5, 3).rearrange("p (k s) -> p k s", k=KD)
            base = place["moe_base"]
            def place_output(r, start):
                return ve.tensor_copy(ys.rearrange("p (g c) s -> p g c s", g=2)[:, :, :, bass.ds(start, CAP)],
                                      psum[:, 6 + r, :].rearrange("p (c g s) -> p g c s", c=4, g=2))

            with ve.Fori(0, EXPERTS // 2) as it:
                for r in range(2):
                    ve.wait_ge(*V("silu_ready", it * 2 + r + 1))
                    ve.wait_ge(full[2 + r], it + base[2 + r])
                    ve.tensor_tensor(acts[:, r, :], silu[:, r, :], psum[:, r, T:2 * T], ALU.mult).then_inc(free[r], 1)
                for r in range(2):
                    start = ve.value_load(starts[0:1, bass.ds(it * 2 + r, 1)], min_val=0, max_val=ASSIGN)
                    ve.wait_ge(full[6 + r], it + base[6 + r] + 1)
                    if r:
                        ve.wait_ge(free[6], it + base[6] + 1)
                    else:
                        ve.wait_ge(free[7], it + base[7])
                    place_output(r, start).then_inc(free[6 + r], 1)
            st.last = (free[7], base[7] + EXPERTS // 2)
            settle()
            most = ve.value_load(starts[0:1, EXPERTS:EXPERTS + 1], min_val=0, max_val=T)
            with ve.If(most > CAP):
                ve.sem_inc(S("more_out"), 1)
                with ve.Fori(0, EXPERTS) as e:
                    start = ve.value_load(starts[0:1, bass.ds(e, 1)], min_val=0, max_val=ASSIGN)
                    for c in range(MAX_PASSES):
                        n = e * MAX_PASSES + c + 1
                        ve.wait_ge(*V("more_silu", n))
                        ve.tensor_tensor(acts[:, 0, :], silu[:, 0, :], psum[:, 0, T:2 * T], ALU.mult).then_inc(S("more_act"), 1)
                        ve.wait_ge(*V("more_z", n))
                        ve.wait_ge(*V("more_out", n))
                        place_output(0, start + c * CAP).then_inc(S("more_out"), 1)
                ve.wait_ge(*V("more_out", EXPERTS * MAX_PASSES + 1))
            do(ve.memset(ab[:, 0:1], 0.0), "experts_done")
            for s in range(4):
                v = await_full(ve, f"y_t{s}1")
                do(ve.tensor_copy(page(11, 2)[:, s * D + 512:(s + 1) * D], v), f"y_t{s}1")
            settle()
            ve.sem_inc(S("ytm_odd"), 4)
            residual("moe", ALPHA, "res2", [f"moe{m}" for m in range(4)])
            layer_norm("ln2", fm(0), fm(0), page(12)[:, 0:256], page(12)[:, 256:512], "ln2_g")
            if phases < 3:
                return

            attn = lambda n: page(10)[:, n * SPAN:(n + 1) * SPAN]
            dil_t, mult_t, swa_t, causal_t = (attn(n) for n in range(4))
            cos = page(10)[:, 4 * SPAN:4 * SPAN + T]
            sin = page(10)[:, 4 * SPAN + T:4 * SPAN + 2 * T]
            rope = slice(NOPE, NOPE + ROPE)

            def attend(sec, nheads, bias, slope, sink=False, first_pair=None):
                pairs = nheads // 2
                for i in range(pairs + 1):
                    if first_pair is not None and i in (2, 3):
                        split_low(first_pair + i - 1)
                    if i < pairs:
                        e = probs[:, i % 3, :, :]
                        neg_max = stats[:, i % 3, NEG_MAX, :, :]
                        for h2 in range(2):
                            g = 2 * i + h2
                            v = await_full(ve, f"{sec}s{g}")
                            if i >= 3:
                                await_full(ve, f"{sec}t{i - 3}_{h2}")
                            do(ve.scalar_tensor_tensor(e[:, h2, :], bias, slope(g), v[:, 0:SPAN], ALU.mult, ALU.add),
                               f"{sec}s{g}")
                        settle()
                        do(ve.tensor_reduce(neg_max[:, :, 0], e[:, :, 0:P], AX.X, ALU.max, negate=True))
                        do(ve.tensor_reduce(neg_max[:, :, 1], e[:, :, P:SPAN], AX.X, ALU.max, negate=True),
                           None if sink else f"{sec}_max")
                        if sink:
                            settle()
                            first = ROWS["sinks"] + i
                            sinks = rows[:, first:first + HEADS + 1:HEADS].unsqueeze(2).broadcast_to([P, 2, NB])
                            do(ve.scalar_tensor_tensor(neg_max, sinks, -1.0, neg_max, ALU.mult, ALU.min), f"{sec}_max")
                    if i >= 3:
                        output(sec, i - 3)
                    if i >= 1:
                        n = i - 1
                        e = probs[:, n % 3, :, :]
                        z = stats[:, n % 3, TOTAL, :, :]
                        ve.wait_ge(*V(f"{sec}_exp", n + 1))
                        if sec == "dil":
                            for h2 in range(2):
                                for b, sl in enumerate((slice(0, P), slice(P, SPAN))):
                                    do(ve.tensor_tensor_reduce(e[:, h2, sl], e[:, h2, sl], mult_t[:, sl], 1.0, 0.0,
                                                               ALU.mult, ALU.add, z[:, h2, b:b + 1]))
                            settle()
                        if sink:
                            do(ve.tensor_tensor(z, z, stats[:, n % 3, SINK_EXP, :, :], ALU.add))
                            settle()
                        do(ve.reciprocal(z, z))
                        settle()
                        for b, sl in enumerate((slice(0, P), slice(P, SPAN))):
                            size = sl.stop - sl.start
                            do(ve.tensor_tensor(e[:, :, sl], e[:, :, sl], z[:, :, b].unsqueeze(2).broadcast_to([P, 2, size]),
                                                ALU.mult), f"{sec}_probs" if b else None)
                for n in range(pairs - 2, pairs):
                    output(sec, n)

            def output(sec, n):
                name = f"{sec}o{n}"
                v = await_full(ve, name)
                first = {"mla": 0, "dil": 4, "swa": 0}[sec]
                do(ve.tensor_copy(fm(8)[:, first + n, :], v[:, 0:T]), name)
                settle()
                ve.sem_inc(S(f"{sec}_o_ready"), 1)

            def gate_up_low(nm, j, steps):
                steps.step(ve, "gu_high", j)
                ve.tensor_tensor(gu_part["lo"][j % 2], slot(item_no[(nm, 0)] + j)[:, 0:gu_size],
                                 gu_part["hi"][j % 2], ALU.subtract).then_inc(S("gu_split"), 1)

            def ffn(nm, layer, done, next_pairs=None):
                base = place[nm]
                silu_buf = page(2)[:, 1280:2048].rearrange("p (r t) -> p r t", t=T)
                for i in range(4):
                    ve.wait_ge(S("x_high"), 4 * layer + i + 1)
                    sl = slice(2 * i, 2 * i + 2)
                    ve.tensor_tensor(x_part["lo"][:, sl, :], fm(1)[:, sl, :], x_part["hi"][:, sl, :], ALU.subtract)\
                        .then_inc(S("x_split"), 1)

                def one(j, steps):
                    if j + 1 < FF_BLOCKS:
                        gate_up_low(nm, j + 1, steps)
                    steps.step(ve, "down_high", j)
                    ve.tensor_tensor(down_part["lo"][j % 2], slot(item_no[(nm, 0)] + j)[:, gu_size:gu_size + down_size],
                                     down_part["hi"][j % 2], ALU.subtract).then_inc(S("down_split"), 1)
                    j3 = j % 3
                    ve.wait_ge(S(f"{nm}_silu"), steps.at(j + 1, 6))
                    ve.tensor_tensor(hidden[:, j3, :], silu_buf[:, j3, :], psum[:, j3, T:2 * T], ALU.mult).then_inc(free[j3], 1)
                    steps.bank(ve, free, base, j, 1)
                    if j >= 3:
                        ve.wait_ge(S(f"{nm}_down"), steps.at(j - 2, 6))
                    ve.tensor_copy(hidden_part["hi"][:, j3, :], hidden[:, j3, :]).then_inc(S("hidden_high"), 1)
                    steps.step(ve, "hidden_high", j)
                    ve.tensor_tensor(hidden_part["lo"][:, j3, :], hidden[:, j3, :], hidden_part["hi"][:, j3, :],
                                     ALU.subtract).then_inc(S("hidden_split"), 1)

                for j in range(3):
                    one(j, LayerSteps(layer))
                with ve.Fori(0, 3) as it:
                    for j in range(3, 9):
                        one(j, LayerSteps(layer, it))
                if next_pairs:
                    split_low(next_pairs - 1)
                one(21, LayerSteps(layer))
                if next_pairs:
                    split_low(next_pairs)
                for n in range(4):
                    b = 4 + n
                    ve.wait_ge(full[b], base[b] + 1)
                    sl = slice(n * BANK, (n + 1) * BANK)
                    do(ve.tensor_tensor(page(0)[:, sl], page(0)[:, sl], psum[:, b, :], ALU.add), "ffn_sum")
                    settle()
                    ve.sem_inc(free[b], 1)
                    ve.sem_inc(S(done), 1)

            ve.wait_ge(*V("ln2_out", KD))
            split_low(MIXER_PAIRS + 1)
            scale_rows("att0", fm(0), fm(1), page(12)[:, 256:512], "att0", KD, "att0_scaled")
            input_low(3, page_part[8], fm(1), page_part[6])
            split_low(MIXER_PAIRS + 2)
            ve.wait_ge(*V("attn_tables", 16))
            v = await_full(ve, "kr")
            t1, t2 = page(7)[rope, 1536:1792], page(7)[rope, 1792:2048]
            do(ve.tensor_tensor(t1, v[rope, 0:T], cos[rope, :], ALU.mult))
            do(ve.tensor_tensor(t2, v[rope, T:2 * T], sin[rope, :], ALU.mult), "kr")
            settle()
            do(ve.tensor_tensor(t1, t1, t2, ALU.add))
            split_low(MIXER_PAIRS + 4)
            scale_rows("cqn", page(9)[:, 0:512].rearrange("p (k t) -> p k t", t=T),
                       page(9)[:, 768:1280].rearrange("p (k t) -> p k t", t=T), page(12)[:, 512:768], "q_norm", 2, "cqn_scaled")
            scale_rows("ckvn", page(9)[:, 512:768].rearrange("p (k t) -> p k t", t=T),
                       page(9)[:, 1280:1536].rearrange("p (k t) -> p k t", t=T), page(12)[:, 768:1024], "kv_norm", 1, "ckvn_scaled")
            settle()
            do(ve.tensor_copy(fm(3)[rope, :, :], bc(t1, 1, [ROPE, HEADS, T])))
            settle()
            ve.sem_inc(S("kA_ready"), 1)
            for hd in range(HEADS):
                v = await_full(ve, f"qA{hd}")
                ve.wait_ge(*V("qA_nope", hd + 1))
                do(ve.scalar_tensor_tensor(t1, v[rope, 0:T], MLA_SCALE, cos[rope, :], ALU.mult, ALU.mult))
                do(ve.scalar_tensor_tensor(t2, v[rope, T:2 * T], MLA_SCALE, sin[rope, :], ALU.mult, ALU.mult), f"qA{hd}")
                settle()
                do(ve.tensor_tensor(fm(2)[rope, hd, :], t1, t2, ALU.add), "qA_ready")
                settle()
            attend("mla", HEADS, causal_t, lambda g: 1.0)
            attend("dil", HEADS, dil_t, lambda g: 2.0 ** -(g + 1), first_pair=MIXER_PAIRS + 4)
            input_low(4, page_part[8], fm(8), page_part[9])
            residual("e_out", None, "res3", [f"e_out{n}" for n in range(4)], MIXER_PAIRS + 6)
            do(ve.memset(page(2)[:, 768:1280], 0.0), "zeros_ready")
            gate_up_low("ffn0", 0, LayerSteps(0))
            scale_rows("ffn0n", fm(0), fm(1), page(12)[:, 256:512], "ffn0", KD, "ffn0n_scaled")
            ffn("ffn0", 0, "res4", MIXER_PAIRS + 10)
            scale_rows("att1", fm(0), fm(1), page(12)[:, 256:512], "att1", KD, "att1_scaled")
            input_low(5, page_part[9], fm(1), page_part[8])
            split_low(MIXER_PAIRS + 12)
            attend("swa", SWA_HEADS, swa_t, lambda g: 2.0 ** (-0.5 * (g // 2 + HEADS * (g % 2) + 1)), sink=True, first_pair=MIXER_PAIRS + 12)
            input_low(6, page_part[8], fm(8), page_part[9])
            residual("o_out", None, "res5", [f"o_out{n}" for n in range(4)], MIXER_PAIRS + 14)
            do(ve.memset(page(2)[:, 768:1280], 0.0), "zeros_ready")
            gate_up_low("ffn1", 0, LayerSteps(1))
            scale_rows("ffn1n", fm(0), fm(1), page(12)[:, 256:512], "ffn1", KD, "ffn1n_scaled")
            ffn("ffn1", 1, "res6")
            scale_rows("final", fm(0), fm(1), page(12)[:, 256:512], "final", KD, "final_scaled")

        @block.gpsimd
        def _(pool):
            st = Steps(pool, "pool_step")
            pool.wait_ge(*V("mixer_landed", 16 * 5))
            pool.wait_ge(*V("decay_ready", 1))
            beta = ab[:, 16:32].rearrange("p (b h) -> p h b", b=NB)
            v3 = lambda pg: units(pg)
            bcu = lambda ap: ap.unsqueeze(1).broadcast_to([P, UNITS, P])
            st.do(pool.tensor_tensor(v3(11), v3(11), bcu(mask("strict_low")), ALU.mult))
            st.do(pool.tensor_tensor(v3(10), v3(10), bcu(mask("incl_up")), ALU.mult), "decay_masked")
            st.settle()

            def per_token(dst, src, what, name):
                for b in range(NB):
                    d = dst.rearrange("p (h b) t -> p h b t", b=NB)[:, :, b, :]
                    s = src.rearrange("p (h b) t -> p h b t", b=NB)[:, :, b, :]
                    w = what[:, b * HEADS:(b + 1) * HEADS].unsqueeze(2).broadcast_to([P, HEADS, P])
                    st.do(pool.tensor_tensor(d, s, w, ALU.mult), name if b else None)

            per_token(v3(11), v3(11), ab[:, 16:32], "decay_masked")
            pool.wait_ge(*V("tm_ready", 1))
            per_token(v3(8), v3(8), ab[:, 16:32], "vb_ready")
            pool.wait_ge(*V("expG_col", 1))
            st.do(pool.tensor_tensor(ab[:, 96:112], ab[:, 96:112], ab[:, 16:32], ALU.mult))
            st.settle()
            for q4 in range(4):
                b_, n_ = place[f"qk{q4}"]
                pool.wait_ge(full[b_], n_)
            per_token(v3(3), v3(7), ab[:, 96:112], "kbg_ready")
            st.settle()
            per_token(v3(7), v3(7), ab[:, 112:128], "kdec_ready")
            if phases >= 2:
                pool.wait_ge(*V("ln1_out", KD))
                st.do(pool.memset(page(2, 3).rearrange("p (k s) -> p k s", k=KD)[:, :, ASSIGN:SORTED], 0.0), "xs_tail")
                xs = page(2, 3).rearrange("p (k s) -> p k s", k=KD)
                xe = page(9)[:, 1024:2048].rearrange("p (r k s) -> p r k s", r=2, k=KD)
                pool.wait_ge(*V("xs_tail", 1))
                pool.wait_ge(*V("xs_ready", KD))
                pool.wait_ge(*V("starts_ready", 1))
                base = place["moe_base"]
                with pool.Fori(0, EXPERTS // 2) as it:
                    for r in range(2):
                        start = pool.value_load(starts[0:1, bass.ds(it * 2 + r, 1)], min_val=0, max_val=ASSIGN)
                        pool.wait_ge(full[r], it + base[r])
                        pool.tensor_copy(xe[:, r, :, :], xs[:, :, bass.ds(start, CAP)]).then_inc(S("xe_ready"), 1)
                most = pool.value_load(starts[0:1, EXPERTS:EXPERTS + 1], min_val=0, max_val=T)
                pool.wait_ge(full[0], base[0] + EXPERTS // 2)
                with pool.If(most > CAP):
                    pool.sem_inc(S("more_h"), 1)
                    with pool.Fori(0, EXPERTS) as e:
                        start = pool.value_load(starts[0:1, bass.ds(e, 1)], min_val=0, max_val=ASSIGN)
                        for c in range(MAX_PASSES):
                            pool.wait_ge(*V("more_h", e * MAX_PASSES + c + 1))
                            pool.tensor_copy(xe[:, 0, :, :], xs[:, :, bass.ds(start + c * CAP, CAP)])\
                                .then_inc(S("more_xe"), 1)

        @block.sync
        def _(sp):
            sp.dma_start(fm(1), io["xT"].rearrange("(k p) t -> p k t", p=P)).then_inc(S("x_landed"), 16)
            sp.dma_start(tables[:], io["c_tables"]).then_inc(S("x_landed"), 16)
            sp.dma_start(cols[:], io["cols"]).then_inc(S("x_landed"), 16)
            sp.wait_ge(*V("x_landed", 16 * 3))

            def columns(name, c0, width):
                return io[name].rearrange("(k p) c -> p k c", p=P)[:, :, c0:c0 + width]

            first_column = {"gm_u": 0, "gm_v": 1024, "dn_q": 2048, "dn_k": 3072, "dn_v": 4096, "dn_z": 5120,
                            "gate_a": 6160, "gate_b": 7184}

            def source(name, i):
                if name in first_column:
                    return columns("w_in", first_column[name] + 512 * i, 512)
                if name in ("w_pa", "w_pb", "w_o", "e_out", "o_out"):
                    return columns(name, 512 * i, 512)
                if name == "e_in":
                    return columns("e_in", 0, 448) if i == 0 else columns("e_in", 448 + 512 * (i - 1), 512)
                if name == "mla_up":
                    return io["mla_up"]
                if name == "o_in":
                    return columns("o_in", 512 * i, 512)
                if name == "o_kv":
                    return columns("o_in", 1024, 256)
                return io[name][i]

            def await_slot(n):
                if n < moe_first:
                    if n >= MIXER_SLOTS:
                        sp.wait_ge(*released[n - MIXER_SLOTS])
                elif n >= moe_first + SLOTS:
                    sp.wait_ge(*released[n - SLOTS])
                elif slot_no(n) < MIXER_SLOTS:
                    sp.wait_ge(*released[max(m for m in range(moe_first) if slot_no(m) == slot_no(n))])
                else:
                    b, nth = place["w_o3" if slot_no(n) == MIXER_SLOTS else "gate_b_1"]
                    sp.wait_ge(full[b], nth)

            def load(n, name, i):
                await_slot(n)
                src = source(name, i)
                floats = int(np.prod(src.shape[1:]))
                dst = slot(n, floats)
                if len(src.shape) == 3:
                    dst = dst.rearrange("p (k c) -> p k c", k=src.shape[1])
                sp.dma_start(dst, src).then_inc(landed[slot_no(n)], 16)

            expert_src = lambda name, e: io[name][bass.ds(e, 1)].rearrange("e (k p) c -> p (e k) c", p=P)

            def load_expert(n, name, e):
                src = expert_src(name, e)
                sp.dma_start(slot(n).rearrange("p (k c) -> p k c", k=src.shape[1]), src)\
                    .then_inc(landed[slot_no(n)], 16)

            for n, (name, i) in enumerate(items[:moe_first]):
                load(n, name, i)
            if phases >= 2:
                for r in range(2):
                    for x, name in enumerate(("w1", "w3", "w2")):
                        n = moe_first + 3 * r + x
                        await_slot(n)
                        src = io[name][r].rearrange("(k p) c -> p k c", p=P)
                        sp.dma_start(slot(n).rearrange("p (k c) -> p k c", k=src.shape[1]), src)\
                            .then_inc(landed[slot_no(n)], 16)
                base = place["moe_base"]
                with sp.Fori(1, EXPERTS // 2) as it:
                    for r in range(2):
                        n = moe_first + 3 * r
                        sp.wait_ge(*V("w1_read", it * 2 + r - 1))
                        src = expert_src("w1", it * 2 + r)
                        sp.dma_start(slot(n).rearrange("p (k c) -> p k c", k=KD), src).then_inc(landed[slot_no(n)], 16)
                        sp.wait_ge(full[r], it + base[r])
                        src = expert_src("w3", it * 2 + r)
                        sp.dma_start(slot(n + 1).rearrange("p (k c) -> p k c", k=KD), src).then_inc(landed[slot_no(n + 1)], 16)
                        sp.wait_ge(full[4 + r], it + base[4 + r])
                        src = expert_src("w2", it * 2 + r)
                        sp.dma_start(slot(n + 2).rearrange("p (k c) -> p k c", k=FE // P), src).then_inc(landed[slot_no(n + 2)], 16)
                sp.wait_ge(*V("starts_ready", 1))
                most = sp.value_load(starts[0:1, EXPERTS:EXPERTS + 1], min_val=0, max_val=T)
                with sp.If(most > CAP):
                    for n in range(moe_first + 3 * EXPERTS - SLOTS, moe_first + 3 * EXPERTS):
                        sp.wait_ge(*released[n])
                    with sp.Fori(0, EXPERTS) as e:
                        sp.wait_ge(*V("more_y", e * MAX_PASSES + 1))
                        for s, name in enumerate(("w1", "w3", "w2")):
                            src = expert_src(name, e)
                            sp.dma_start(slot(s).rearrange("p (k c) -> p k c", k=src.shape[1]), src)\
                                .then_inc(S("more_landed"), 16)
                    sp.wait_ge(*V("more_y", EXPERTS * MAX_PASSES + 1))
            if phases >= 3:
                for n in range(moe_first + 3 * EXPERTS, len(items)):
                    load(n, *items[n])
            if phases == 3:
                sp.wait_ge(*V("final_scaled", KD))
                result = fm(1)
            else:
                sp.wait_ge(*V("ln1_out" if phases == 1 else "ln2_out", KD))
                result = fm(0)
            sp.dma_start(out.rearrange("(k p) t -> p k t", p=P), result).then_inc(S("stored"), 16)
            sp.wait_ge(*V("stored", 16))


MLA_SCALE = 1.0 / float(np.sqrt(NOPE + ROPE))
DIL_SCALE = 0.125


def silu_block(act_e, act, S, fm, blk):
    act_e.wait_ge(S("conv_done"), blk + 1)
    dst = fm(2 + blk // 8)[:, blk % 8, :]
    act(dst, dst, ACT.Silu, "v_ready" if blk >= 16 else "qk_silu")


def ab_stage(ve, st, S, ab, row, await_full, bc):
    v = await_full(ve, "ab")
    v3 = v[:, 0:32].rearrange("p (b c) -> p b c", b=NB)
    view = lambda c: ab[:, c:c + 16].rearrange("p (b h) -> p b h", b=NB)
    st.do(ve.tensor_tensor(view(144), v3[:, :, 0:8], bc(row("b_a", 8), 1, [P, NB, 8]), ALU.add))
    st.do(ve.tensor_tensor(view(32), v3[:, :, 8:16], bc(row("b_b", 8), 1, [P, NB, 8]), ALU.add), "ab")
    st.settle()
    st.do(ve.tensor_tensor(view(144), view(144), bc(row("dt_bias", 8), 1, [P, NB, 8]), ALU.add))
    st.settle()
    st.do(ve.tensor_scalar(ab[:, 128:144], ab[:, 144:160], -1.0, None, ALU.mult))
    st.settle()
    st.do(ve.tensor_tensor(ab[:, 48:64], ab[:, 128:144], ab[:, 144:160], ALU.max), "ab_ready")


def ab_finish(ve, st, S, ab):
    st.do(ve.tensor_scalar(ab[:, 32:48], ab[:, 32:48], 1.0, None, ALU.add))
    st.do(ve.scalar_tensor_tensor(ab[:, 144:160], ab[:, 144:160], 0.0, ab[:, 48:64], ALU.max, ALU.add))
    st.settle()
    st.do(ve.reciprocal(ab[:, 16:32], ab[:, 32:48]))
    view = lambda c: ab[:, c:c + 16].rearrange("p (b h) -> p b h", b=NB)
    st.do(ve.scalar_tensor_tensor(view(0), view(144), -1.0, ab[:, 64:72].unsqueeze(1).broadcast_to([P, NB, HEADS]),
                                  ALU.mult, ALU.mult), "g_ready")


def lay_out(inputs):
    f = {k: np.asarray(v) for k, v in inputs.items()}
    blocks = lambda v: np.ascontiguousarray(v).reshape(-1, P).T
    b_in = f["b_in"][0]
    ab0 = 6 * D
    main = np.concatenate([b_in[:ab0], b_in[ab0 + 16:]])
    cols = np.concatenate([
        blocks(f["ln_in_g"]), blocks(f["ln_in_b"]), blocks(f["gm_ln_g"]), blocks(f["gm_ln_b"]),
        blocks(f["ln1_g"]), blocks(f["ln1_b"]), blocks(f["ln2_g"]), blocks(f["ln2_b"]),
        blocks(f["attn_norm_2"][0]), blocks(f["attn_norm_2"][1]), blocks(f["ffn_norm_2"][0]),
        blocks(f["ffn_norm_2"][1]), blocks(f["final_norm_2"]), blocks(main), blocks(f["dn_conv_w"][0]),
        blocks(f["dn_norm_w"]), blocks(f["e_q_norm_2"]), blocks(f["e_kv_norm_2"]),
        np.full((P, 1), 1e-5, np.float32), np.full((P, 1), 1e-6, np.float32),
        np.full((P, 1), -0.5 * np.log(float(P)), np.float32)], axis=1)
    rows = np.concatenate([f["dn_a_log"][0], f["dn_dt_bias"][0], b_in[ab0:ab0 + 16], f["b_rg"][0], f["b_re"][0],
                           f["o_sinks_2"][0]])[None, :]
    e_in = f["e_w_in_2"][0]
    swap = lambda w: np.concatenate([w[..., ROPE // 2:], w[..., :ROPE // 2]], axis=-1)
    kr = e_in[:, 384:416]
    e_in = np.concatenate([e_in[:, 0:416], swap(kr), e_in[:, 416:]], axis=1)
    uq = f["e_w_uq_2"][0]
    uq_rope = swap(uq.reshape(MLA_Q, HEADS, 96)[:, :, NOPE:]).reshape(MLA_Q, HEADS * ROPE)
    uq = np.concatenate([uq, uq_rope], axis=1).reshape(2, P, D).transpose(1, 0, 2).reshape(P, 2 * D)
    ukv = f["e_w_ukv_2"][0].reshape(MLA_KV, HEADS, 2, NOPE).transpose(0, 2, 1, 3).reshape(MLA_KV, D)
    pairs = lambda w: w.reshape(2, HEADS, 64, -1).transpose(1, 0, 2, 3).reshape(w.shape)
    o_in = f["o_w_qkv_2"][0]
    o_in = np.concatenate([pairs(np.ascontiguousarray(o_in[:, :D].T)).T, o_in[:, D:]], axis=1)

    def ffn(layer):
        gu = f["f_w_gate_up_2"][layer].reshape(KD, P, 2, FF_BLOCKS, P).transpose(3, 1, 0, 2, 4)
        down = f["f_w_down_2"][layer].reshape(FF_BLOCKS, P, D)
        return np.concatenate([gu.reshape(FF_BLOCKS, P, 2 * KD * P), down], axis=2)

    return {
        "xT": f["x"][0].T, "cols": cols, "rows": rows,
        "w_in": f["w_in"][0], "w_ab": f["w_in"][0][:, ab0:ab0 + 16],
        "w_s": f["gm_w_s"][0].transpose(0, 2, 1), "b_s": f["gm_b_s"][0].reshape(1, -1),
        "w_pa": f["w_pa"][0], "w_pb": f["w_pb"][0], "w_o": f["w_o"][0],
        "w_router": np.concatenate([f["w_rg"][0], f["w_re"][0]], axis=1),
        "w1": f["w1"][0], "w3": f["w3"][0], "w2": f["w2"][0],
        "e_in": e_in, "mla_up": np.concatenate([uq, ukv], axis=1), "e_out": f["e_w_out_2"][0],
        "o_in": o_in, "o_out": pairs(f["o_w_out_2"][0]), "ffn0": ffn(0), "ffn1": ffn(1),
    }


def kernel(phases=3, **inputs):
    import concourse.bacc as bacc
    from concourse.bass_utils import run_bass_kernel_spmd

    nc = bacc.Bacc("TRN2", target_bir_lowering=False, num_devices=1)
    arrays, io = {}, {}
    for name, a in {**lay_out(inputs), **shape_tables()}.items():
        arrays[f"in_{name}"] = np.ascontiguousarray(a)
        io[name] = nc.dram_tensor(f"in_{name}", a.shape, mybir.dt.from_np(a.dtype), kind="ExternalInput").ap()
    out = nc.dram_tensor("out", (D, T), F32, kind="ExternalOutput").ap()
    build(nc, io, out, phases)
    got = run_bass_kernel_spmd(nc, [arrays], core_ids=[0]).results[0]["out"]
    return np.ascontiguousarray(got.T)[None]
```
